# Optimizing a Trainium2 kernel written in Bass

```python
import jax, jax.numpy as jnp
from jax import lax
import numpy as np

D_MODEL = 1024
BATCH = 1
SEQ = 1024
DEPTH = 1

N_MIXERS = 2
N_HGRN_LAYERS = (DEPTH + N_MIXERS - 1) // N_MIXERS
N_ATTN_LAYERS = (DEPTH - 1 + N_MIXERS - 1) // N_MIXERS

HGRN_HEAD_DIM = 128
HGRN_HEADS = D_MODEL // HGRN_HEAD_DIM
HGRN_CHUNK = 64

ATTN_HEADS = 16
ATTN_HEAD_DIM = D_MODEL // ATTN_HEADS
DILATED_GROUPS = ((128, 1), (512, 4), (2048, 16))
N_GROUPS = len(DILATED_GROUPS)
ATTN_BLOCK = 128

MLP_HIDDEN = 4 * D_MODEL
NORM_EPS = 1e-6


def _rmsnorm(x, gain):
    xf = x.astype(jnp.float32)
    y = xf * lax.rsqrt(jnp.mean(xf * xf, axis=-1, keepdims=True) + NORM_EPS)
    return (y * gain.astype(jnp.float32)).astype(x.dtype)

def _hgrn2_chunk_scan(q, k, v, log_f):
    b, s, h, dk = q.shape
    dv = v.shape[-1]
    nc = s // HGRN_CHUNK

    def to_chunks(t):
        return t.reshape(b, nc, HGRN_CHUNK, h, t.shape[-1]).transpose(1, 0, 3, 2, 4)

    causal = jnp.tril(jnp.ones((HGRN_CHUNK, HGRN_CHUNK), dtype=bool))

    def step(state, inp):
        qi, ki, vi, gi = inp
        cum = jnp.cumsum(gi, axis=2)
        o_inter = jnp.einsum('bhtk,bhkv->bhtv', qi * jnp.exp(cum), state)
        diff = cum[:, :, :, None, :] - cum[:, :, None, :, :]
        decay = jnp.exp(jnp.where(causal[:, :, None], diff, -jnp.inf))
        scores = jnp.einsum('bhtk,bhtsk,bhsk->bhts', qi, decay, ki)
        o_intra = jnp.einsum('bhts,bhsv->bhtv', scores, vi)
        last = cum[:, :, -1:, :]
        k_dec = ki * jnp.exp(last - cum)
        new_state = (jnp.exp(last[:, :, 0, :])[..., None] * state
                     + jnp.einsum('bhsk,bhsv->bhkv', k_dec, vi))
        return new_state, o_inter + o_intra

    init = jnp.zeros((b, h, dk, dv), jnp.float32)
    _, o = lax.scan(step, init, (to_chunks(q), to_chunks(k), to_chunks(v), to_chunks(log_f)))
    return o.transpose(1, 0, 3, 2, 4).reshape(b, s, h, dv)

def _hgrn2_mixer(h, w_in, lower_bound, out_norm, w_out):
    b, s, _ = h.shape
    proj = h @ w_in
    q, f, i, g = jnp.split(proj, 4, axis=-1)
    ff = f.astype(jnp.float32)
    lb = lower_bound.astype(jnp.float32)
    log_f = jnp.logaddexp(jnp.log(lb), jnp.log1p(-lb) + jax.nn.log_sigmoid(ff))
    k = (1.0 - lb) * jax.nn.sigmoid(-ff)
    qf = jax.nn.silu(q.astype(jnp.float32)) * (HGRN_HEAD_DIM ** -0.5)
    heads = lambda t: t.reshape(b, s, HGRN_HEADS, HGRN_HEAD_DIM)
    o = _hgrn2_chunk_scan(heads(qf), heads(k), heads(i.astype(jnp.float32)), heads(log_f))
    o = o * lax.rsqrt(jnp.mean(o * o, axis=-1, keepdims=True) + NORM_EPS)
    o = o.reshape(b, s, D_MODEL) * out_norm.astype(jnp.float32) * jax.nn.silu(g.astype(jnp.float32))
    return o.astype(h.dtype) @ w_out

def _banded_causal_attention(q, k, v, reach):
    n, l, h, dh = q.shape
    blk = ATTN_BLOCK
    nb = -(-l // blk)
    lp = nb * blk
    qb = jnp.pad(q, ((0, 0), (0, lp - l), (0, 0), (0, 0))).reshape(n, nb, blk, h, dh)
    pad_kv = ((0, 0), (blk, lp - l), (0, 0), (0, 0))
    kp = jnp.pad(k, pad_kv).reshape(n, nb + 1, blk, h, dh)
    vp = jnp.pad(v, pad_kv).reshape(n, nb + 1, blk, h, dh)
    kb = jnp.concatenate([kp[:, :-1], kp[:, 1:]], axis=2)
    vb = jnp.concatenate([vp[:, :-1], vp[:, 1:]], axis=2)
    bidx = jnp.arange(nb)[:, None, None]
    qpos = bidx * blk + jnp.arange(blk)[None, :, None]
    kpos = (bidx - 1) * blk + jnp.arange(2 * blk)[None, None, :]
    dist = qpos - kpos
    mask = (kpos >= 0) & (dist >= 0) & (dist <= reach)
    s = jnp.einsum('nbqhd,nbkhd->nbhqk', qb, kb).astype(jnp.float32) * (dh ** -0.5)
    s = jnp.where(mask[None, :, None], s, -jnp.inf)
    lse = jax.nn.logsumexp(s, axis=-1)
    p = jnp.exp(s - lse[..., None])
    o = jnp.einsum('nbhqk,nbkhd->nbqhd', p.astype(v.dtype), vb).astype(jnp.float32)
    o = o.reshape(n, lp, h, dh)[:, :l]
    lse = lse.transpose(0, 1, 3, 2).reshape(n, lp, h)[:, :l]
    return o, lse

def _dilated_group(q, k, v, dilation, reach):
    b, s, h, dh = q.shape
    l = s // dilation

    def split(t):
        return t.reshape(b, l, dilation, h, dh).transpose(0, 2, 1, 3, 4).reshape(b * dilation, l, h, dh)

    o, lse = _banded_causal_attention(split(q), split(k), split(v), reach)
    o = o.reshape(b, dilation, l, h, dh).transpose(0, 2, 1, 3, 4).reshape(b, s, h, dh)
    lse = lse.reshape(b, dilation, l, h).transpose(0, 2, 1, 3).reshape(b, s, h)
    return o, lse

def _dilated_attention_mixer(h, w_qkv, w_out):
    b, s, _ = h.shape
    proj = (h @ w_qkv).reshape(b, s, N_GROUPS, 3, ATTN_HEADS, ATTN_HEAD_DIM)
    outs, lses = [], []
    for g, (window, dilation) in enumerate(DILATED_GROUPS):
        o, lse = _dilated_group(proj[:, :, g, 0], proj[:, :, g, 1], proj[:, :, g, 2],
                                dilation, window // dilation)
        outs.append(o)
        lses.append(lse)
    weights = jax.nn.softmax(jnp.stack(lses, axis=0), axis=0)
    o = jnp.sum(weights[..., None] * jnp.stack(outs, axis=0), axis=0)
    return o.reshape(b, s, D_MODEL).astype(h.dtype) @ w_out

def _squared_relu_mlp(h, w1, w2):
    a = jax.nn.relu(h @ w1)
    return (a * a) @ w2

def first_inputs(seed: int = 0) -> dict:
    key = jax.random.key(seed)
    ks = jax.random.split(key, 13)
    nrm = lambda k, shape: jax.random.normal(k, shape, jnp.float32)
    d = D_MODEL
    return {
        "x": nrm(ks[0], (BATCH, SEQ, d)),
        "norm_mix": 1.0 + 0.02 * nrm(ks[1], (DEPTH, d)),
        "norm_mlp": 1.0 + 0.02 * nrm(ks[2], (DEPTH, d)),
        "norm_final": 1.0 + 0.02 * nrm(ks[3], (d,)),
        "hgrn_w_in": nrm(ks[4], (N_HGRN_LAYERS, d, 4 * d)) * d ** -0.5,
        "hgrn_lower_bound": 0.5 * nrm(ks[5], (N_HGRN_LAYERS, d)),
        "hgrn_out_norm": 1.0 + 0.02 * nrm(ks[6], (N_HGRN_LAYERS, d)),
        "hgrn_w_out": nrm(ks[7], (N_HGRN_LAYERS, d, d)) * d ** -0.5,
        "attn_w_qkv": nrm(ks[8], (N_ATTN_LAYERS, d, N_GROUPS * 3 * d)) * d ** -0.5,
        "attn_w_out": nrm(ks[9], (N_ATTN_LAYERS, d, d)) * d ** -0.5,
        "mlp_w1": nrm(ks[10], (DEPTH, d, MLP_HIDDEN)) * d ** -0.5,
        "mlp_w2": nrm(ks[11], (DEPTH, MLP_HIDDEN, d)) * MLP_HIDDEN ** -0.5,
    }

def first_block(x, norm_mix, norm_mlp, norm_final, hgrn_w_in, hgrn_lower_bound, hgrn_out_norm,
              hgrn_w_out, attn_w_qkv, attn_w_out, mlp_w1, mlp_w2):
    lb_all = jnp.cumsum(jax.nn.softmax(hgrn_lower_bound.astype(jnp.float32), axis=0), axis=0)
    lb_all = lb_all - lb_all[0]
    for layer in range(DEPTH):
        j = layer // N_MIXERS
        h = _rmsnorm(x, norm_mix[layer])
        if layer % N_MIXERS == 0:
            mix = _hgrn2_mixer(h, hgrn_w_in[j], lb_all[j], hgrn_out_norm[j], hgrn_w_out[j])
        else:
            mix = _dilated_attention_mixer(h, attn_w_qkv[j], attn_w_out[j])
        x = x + mix
        x = x + _squared_relu_mlp(_rmsnorm(x, norm_mlp[layer]), mlp_w1[layer], mlp_w2[layer])
    return _rmsnorm(x, norm_final)


GRID_W = 64
CTX_LEN = 256
N_FOURIER_GROUPS = 4
FOURIER_GROUP_DIM = 128
FOURIER_WIDTH = N_FOURIER_GROUPS * FOURIER_GROUP_DIM
NA_HEADS = 8
HEAD_DIM = 64
NA_WIDTH = NA_HEADS * HEAD_DIM
IN_WIDTH = FOURIER_WIDTH + 3 * NA_WIDTH
WIN_ROWS = 8
WIN_COLS = 16
N_BRANCHES = 2
D_FF = 4 * D_MODEL
ROPE_THETA = 10000.0
N_MOD = 6


def rms_norm(x, g):
    xf = x.astype(jnp.float32)
    y = xf * lax.rsqrt(jnp.mean(xf * xf, axis=-1, keepdims=True) + NORM_EPS)
    return (y * g.astype(jnp.float32)).astype(x.dtype)

def modulate(h, shift, scale):
    return h * (1 + scale) + shift

def ada_mod(cond, w, b):
    m = jax.nn.silu(cond) @ w + b
    return jnp.split(m, N_MOD, axis=-1)

def split_heads(a):
    return a.reshape(a.shape[0], a.shape[1], NA_HEADS, HEAD_DIM)

def split_projection(p):
    f = p[..., :FOURIER_WIDTH]
    q = p[..., FOURIER_WIDTH:FOURIER_WIDTH + NA_WIDTH]
    k = p[..., FOURIER_WIDTH + NA_WIDTH:FOURIER_WIDTH + 2 * NA_WIDTH]
    v = p[..., FOURIER_WIDTH + 2 * NA_WIDTH:]
    return f, split_heads(q), split_heads(k), split_heads(v)

def rope_1d(x, cos, sin):
    m = x.shape[-1] // 2
    x1, x2 = x[..., :m], x[..., m:]
    cos = cos[None, :, None, :]
    sin = sin[None, :, None, :]
    return jnp.concatenate([x1 * cos - x2 * sin, x1 * sin + x2 * cos], axis=-1)

def axial_rope(x):
    n_tok = x.shape[1]
    t = jnp.arange(n_tok)
    row = (t // GRID_W).astype(jnp.float32)
    col = (t % GRID_W).astype(jnp.float32)
    axis_dim = HEAD_DIM // 2
    inv_freq = ROPE_THETA ** (-jnp.arange(0, axis_dim, 2, dtype=jnp.float32) / axis_dim)
    ang_r = row[:, None] * inv_freq
    ang_c = col[:, None] * inv_freq
    xf = x.astype(jnp.float32)
    xr = rope_1d(xf[..., :axis_dim], jnp.cos(ang_r), jnp.sin(ang_r))
    xc = rope_1d(xf[..., axis_dim:], jnp.cos(ang_c), jnp.sin(ang_c))
    return jnp.concatenate([xr, xc], axis=-1).astype(x.dtype)

def fourier_mix(u):
    b, n, _ = u.shape
    ug = u.astype(jnp.float32).reshape(b, n, N_FOURIER_GROUPS, FOURIER_GROUP_DIM)
    y = jnp.fft.fft2(ug, axes=(1, 3), norm="ortho").real
    return y.reshape(b, n, FOURIER_WIDTH).astype(u.dtype)

def neighbourhood_attention(q, k, v, k_ctx, v_ctx, rpb):
    b, s, h, dh = q.shape
    rows = s // GRID_W
    kr = min(WIN_ROWS, rows)
    kc = WIN_COLS
    n_loc = kr * kc
    scale = dh ** -0.5
    qg = q.reshape(b, rows, GRID_W, h, dh)
    kg = k.reshape(b, rows, GRID_W, h, dh)
    vg = v.reshape(b, rows, GRID_W, h, dh)
    r = jnp.arange(rows)
    cc = jnp.arange(GRID_W)
    row_start = jnp.clip(r - kr // 2, 0, rows - kr)
    col_start = jnp.clip(cc - kc // 2, 0, GRID_W - kc)
    col_idx = col_start[:, None] + jnp.arange(kc)
    dc_idx = col_idx - cc[:, None] + (WIN_COLS - 1)
    dr_idx = row_start[:, None] + jnp.arange(kr) - r[:, None] + (WIN_ROWS - 1)

    def one_row(args):
        q_row, rs, dr = args
        k_rows = lax.dynamic_slice_in_dim(kg, rs, kr, axis=1)
        v_rows = lax.dynamic_slice_in_dim(vg, rs, kr, axis=1)
        k_win = k_rows[:, :, col_idx]
        v_win = v_rows[:, :, col_idx]
        bias = rpb[:, dr][:, :, dc_idx].transpose(0, 2, 1, 3)
        s_loc = (jnp.einsum('bqhd,brqchd->bhqrc', q_row, k_win).astype(jnp.float32) * scale
                 + bias[None].astype(jnp.float32))
        s_ctx = jnp.einsum('bqhd,bkhd->bhqk', q_row, k_ctx).astype(jnp.float32) * scale
        sc = jnp.concatenate([s_loc.reshape(b, h, GRID_W, n_loc), s_ctx], axis=-1)
        p = jax.nn.softmax(sc, axis=-1).astype(v.dtype)
        p_loc = p[..., :n_loc].reshape(b, h, GRID_W, kr, kc)
        p_ctx = p[..., n_loc:]
        return (jnp.einsum('bhqrc,brqchd->bqhd', p_loc, v_win)
                + jnp.einsum('bhqk,bkhd->bqhd', p_ctx, v_ctx))

    out = lax.map(one_row, (qg.transpose(1, 0, 2, 3, 4), row_start, dr_idx))
    return out.transpose(1, 0, 2, 3, 4).reshape(b, s, h * dh)

def context_attention(q, k, v):
    b, n, h, dh = q.shape
    s = jnp.einsum('bqhd,bkhd->bhqk', q, k).astype(jnp.float32) * dh ** -0.5
    p = jax.nn.softmax(s, axis=-1).astype(v.dtype)
    return jnp.einsum('bhqk,bkhd->bqhd', p, v).reshape(b, n, h * dh)

def gated_merge(h, y_four, y_attn, w_gate, w_fo, w_ao, w_o):
    gates = jax.nn.sigmoid(h @ w_gate)
    g_f, g_a = jnp.split(gates, N_BRANCHES, axis=-1)
    merged = g_f * (y_four @ w_fo) + g_a * (y_attn @ w_ao)
    return merged @ w_o

def sqrelu_mlp(h, w1, w2):
    a = jax.nn.relu(h @ w1)
    return (a * a) @ w2

def second_inputs(seed: int = 0) -> dict:
    key = jax.random.key(seed)
    ks = jax.random.split(key, 20)
    nrm = lambda k, shape, s: jax.random.normal(k, shape, jnp.float32) * s
    return {
        "x": nrm(ks[0], (BATCH, SEQ, D_MODEL), 1.0),
        "c": nrm(ks[1], (BATCH, D_MODEL), 1.0),
        "ctx": nrm(ks[2], (BATCH, CTX_LEN, D_MODEL), 1.0),
        "c_ctx": nrm(ks[3], (D_MODEL,), 1.0),
        "w_ada": nrm(ks[4], (DEPTH, D_MODEL, N_MOD * D_MODEL), D_MODEL ** -0.5),
        "b_ada": nrm(ks[5], (DEPTH, N_MOD * D_MODEL), 0.02),
        "norm1_g": 1.0 + nrm(ks[6], (DEPTH, D_MODEL), 0.02),
        "norm2_g": 1.0 + nrm(ks[7], (DEPTH, D_MODEL), 0.02),
        "w_in": nrm(ks[8], (DEPTH, D_MODEL, IN_WIDTH), D_MODEL ** -0.5),
        "q_norm_g": 1.0 + nrm(ks[9], (DEPTH, HEAD_DIM), 0.02),
        "k_norm_g": 1.0 + nrm(ks[10], (DEPTH, HEAD_DIM), 0.02),
        "rpb": nrm(ks[11], (DEPTH, NA_HEADS, 2 * WIN_ROWS - 1, 2 * WIN_COLS - 1), 0.1),
        "w_branch_gate": nrm(ks[12], (DEPTH, D_MODEL, N_BRANCHES * D_MODEL), D_MODEL ** -0.5),
        "w_fourier_out": nrm(ks[13], (DEPTH, FOURIER_WIDTH, D_MODEL), FOURIER_WIDTH ** -0.5),
        "w_attn_out": nrm(ks[14], (DEPTH, NA_WIDTH, D_MODEL), NA_WIDTH ** -0.5),
        "w_out": nrm(ks[15], (DEPTH, D_MODEL, D_MODEL), D_MODEL ** -0.5),
        "w_mlp1": nrm(ks[16], (DEPTH, D_MODEL, D_FF), D_MODEL ** -0.5),
        "w_mlp2": nrm(ks[17], (DEPTH, D_FF, D_MODEL), D_FF ** -0.5),
    }

def second_block(x, c, ctx, c_ctx, w_ada, b_ada, norm1_g, norm2_g, w_in, q_norm_g, k_norm_g,
              rpb, w_branch_gate, w_fourier_out, w_attn_out, w_out, w_mlp1, w_mlp2):
    h_ctx = ctx
    for l in range(DEPTH):
        last = l == DEPTH - 1
        sh1, sc1, g1, sh2, sc2, g2 = [m[:, None, :] for m in ada_mod(c, w_ada[l], b_ada[l])]
        csh1, csc1, cg1, csh2, csc2, cg2 = ada_mod(c_ctx, w_ada[l], b_ada[l])

        hc = modulate(rms_norm(h_ctx, norm1_g[l]), csh1, csc1)
        fc, qc, kc, vc = split_projection(hc @ w_in[l])
        kc = rms_norm(kc, k_norm_g[l])

        hx = modulate(rms_norm(x, norm1_g[l]), sh1, sc1)
        fx, qx, kx, vx = split_projection(hx @ w_in[l])
        qx = axial_rope(rms_norm(qx, q_norm_g[l]))
        kx = axial_rope(rms_norm(kx, k_norm_g[l]))
        y_four = fourier_mix(fx)
        y_attn = neighbourhood_attention(qx, kx, vx, kc, vc, rpb[l])
        mixed = gated_merge(hx, y_four, y_attn, w_branch_gate[l], w_fourier_out[l],
                            w_attn_out[l], w_out[l])
        x = x + g1 * mixed
        hx2 = modulate(rms_norm(x, norm2_g[l]), sh2, sc2)
        x = x + g2 * sqrelu_mlp(hx2, w_mlp1[l], w_mlp2[l])

        if not last:
            qc = rms_norm(qc, q_norm_g[l])
            yc_four = fourier_mix(fc)
            yc_attn = context_attention(qc, kc, vc)
            mixed_c = gated_merge(hc, yc_four, yc_attn, w_branch_gate[l], w_fourier_out[l],
                                  w_attn_out[l], w_out[l])
            h_ctx = h_ctx + cg1 * mixed_c
            hc2 = modulate(rms_norm(h_ctx, norm2_g[l]), csh2, csc2)
            h_ctx = h_ctx + cg2 * sqrelu_mlp(hc2, w_mlp1[l], w_mlp2[l])
    return x


def setup_inputs(seed=0):
    out = dict(first_inputs(seed))
    for name, value in second_inputs(seed + 1).items():
        if name != "x":
            out[name + "_2"] = value
    return out


def reference(
    x, norm_mix, norm_mlp, norm_final, hgrn_w_in, hgrn_lower_bound, hgrn_out_norm, hgrn_w_out,
    attn_w_qkv, attn_w_out, mlp_w1, mlp_w2, c_2, ctx_2, c_ctx_2, w_ada_2, b_ada_2, norm1_g_2,
    norm2_g_2, w_in_2, q_norm_g_2, k_norm_g_2, rpb_2, w_branch_gate_2, w_fourier_out_2,
    w_attn_out_2, w_out_2, w_mlp1_2, w_mlp2_2,
):
    x = first_block(
        x, norm_mix, norm_mlp, norm_final, hgrn_w_in, hgrn_lower_bound, hgrn_out_norm,
        hgrn_w_out, attn_w_qkv, attn_w_out, mlp_w1, mlp_w2,
    )
    return second_block(
        x, c_2, ctx_2, c_ctx_2, w_ada_2, b_ada_2, norm1_g_2, norm2_g_2, w_in_2, q_norm_g_2,
        k_norm_g_2, rpb_2, w_branch_gate_2, w_fourier_out_2, w_attn_out_2, w_out_2, w_mlp1_2,
        w_mlp2_2,
    )


_drawn_inputs = setup_inputs


def setup_inputs(seed=0):
    import zlib

    import numpy as np

    out = dict(_drawn_inputs(seed))
    spreads = {}
    factors = {'norm_mix': 3.234,
     'norm_mlp': 3.302,
     'norm_final': 3.012,
     'hgrn_out_norm': 4.915,
     'norm1_g_2': 8.0,
     'norm2_g_2': 10.05,
     'q_norm_g_2': 8.0,
     'k_norm_g_2': 8.0,
     'rpb_2': 8.0}
    for name, (base, spread) in spreads.items():
        noise = np.random.default_rng([zlib.crc32(name.encode()), seed]).standard_normal(out[name].shape)
        drawn = base * np.exp(spread * noise) if base else spread * noise
        out[name] = __import__('jax').numpy.asarray(drawn.astype(out[name].dtype))
    for name, factor in factors.items():
        out[name] = (out[name] * factor).astype(out[name].dtype)
    return out
```

```python
from contextlib import ExitStack

import numpy as np
import concourse.bass as bass
from concourse import mybir

F = mybir.dt.float32
R = mybir.dt.float32r
U8 = mybir.dt.uint8
ALU = mybir.AluOpType
ACT = mybir.ActivationFunctionType
AX = mybir.AxisListType.X

P = 128
T = 1024
EPS = 1e-6
NEG = -1.0e30
ENGINES = ("tensor", "vector", "scalar", "gpsimd", "sync")

V_MIX, V_MLP, V_FINAL, V_LB, V_ON, V_N1, V_N2, V_C, V_CC, V_BADA = range(0, 80, 8)
V_END = V_BADA + 48


class Queues:

    def __init__(self, nc, ctx):
        self.nc, self.ctx = nc, ctx
        self.q = {e: [] for e in ENGINES}
        self.sems = {}
        self.n = {}

    def sem(self, name):
        if name not in self.sems:
            self.sems[name] = self.ctx.enter_context(self.nc.semaphore("s_" + name))
            self.n[name] = 0
        return self.sems[name]

    def op(self, engine, fn, *waits, sig=True):
        if sig:
            self.sem(engine)
            self.n[engine] += 1
        self.q[engine].append((fn, waits, engine if sig else None, 1))
        return (engine, self.n[engine]) if sig else None

    def dma(self, out, in_, lane, *waits):
        self.sem(lane)
        self.n[lane] += 16
        self.q["sync"].append((lambda e: e.dma_start(out, in_), waits, lane, 16))
        return (lane, self.n[lane])

    def emit(self, engine, e):
        seen = {}

        def wait(w):
            if w is None:
                return
            if isinstance(w, list):
                for x in w:
                    wait(x)
                return
            name, value = w
            if seen.get(name, 0) < value:
                seen[name] = value
                e.wait_ge(self.sems[name], value)

        for fn, waits, name, inc in self.q[engine]:
            wait(list(waits))
            ins = fn(e)
            if name:
                ins.then_inc(self.sems[name], inc)


class Ring:

    def __init__(self, items):
        self.items = items
        self.free = [[] for _ in items]
        self.i = -1

    def get(self):
        self.i = (self.i + 1) % len(self.items)
        return self.items[self.i], self.free[self.i], self.i

    def release(self, i, *tokens):
        self.free[i] = list(tokens)


def run_both(a, b, every=1):
    n = 0
    for _ in a:
        n += 1
        if n % every == 0 and b is not None:
            next(b, None)
    if b is not None:
        for _ in b:
            pass


def build(nc, xT, vecs, w_in, w_out, m_w1, m_w2, ctxT, w_ada, w_in2, gains, biasE, biasM, w_gate, w_fo, w_ao,
          w_o2, m2_w1, m2_w2, ident_d, masks_d, rope_d, dft_d, cd_d, out, stage=9):
    with ExitStack() as ctx:
        Q = Queues(nc, ctx)
        op, dma = Q.op, Q.dma
        base = 16512
        R1A = base
        HA = R1A + 32768
        WRA = HA + 65536
        WSA = WRA + 8192
        SA = WSA + 32768
        CA = SA + 65536

        def at(name, shape, dt, off):
            return nc.alloc_sbuf_tensor_at(name, shape, dt, offset=off)

        R1 = at("R1", [P, 8, T], F, R1A)
        Hh = at("Hh", [P, 8, T], R, HA)
        Hl = at("Hl", [P, 8, T], R, HA + 32768)
        Wraw = [at(f"Wraw{i}", [P, 1024], F, WRA + 4096 * i) for i in range(2)]
        Whi = [at(f"Whi{i}", [P, 1024], R, WSA + 8192 * i) for i in range(4)]
        Wlo = [at(f"Wlo{i}", [P, 1024], R, WSA + 8192 * i + 4096) for i in range(4)]

        def sa(name, i, dt=F, shape=(P, 1024)):
            return at(name, list(shape), dt, SA + 4096 * i)

        coff = [CA]

        def const(name, shape, dt=F, size=4):
            n = int(np.prod(shape[1:])) * size
            t = at(name, shape, dt, coff[0])
            coff[0] += (n + 31) // 32 * 32
            assert coff[0] <= 229344
            return t

        ident = const("ident", [P, P])
        ones = const("ones", [P, P])
        vec = const("vec", [P, V_END])
        masks = const("masks", [P, 8, P], U8, 1)
        eps = const("eps", [P, 1])
        lb = const("lb", [P, 8])
        oml = const("oml", [P, 8])
        lt = const("lt", [P, 3, 8])
        tot = const("tot", [P, 8])
        csil = const("csil", [P, 8, 2])
        mods = const("mods", [P, 48, 2])
        modA = const("modA", [P, 3, 8])
        small = const("small", [P, 96])

        psum = [ctx.enter_context(nc.psum_tensor(f"ps{i}", [P, 1024], F)) for i in range(4)]
        xs_d = nc.dram_tensor("xs_scratch", [8, P, T], F, kind="Internal").ap()
        mf_d = nc.dram_tensor("mf_scratch", [8, P, T], F, kind="Internal").ap()

        class Weights:
            def __init__(self):
                self.plan = []
                self.loaded = 0
                self.taken = 0
                self.raw_free = [[], []]
                self.free = [[], [], [], []]
                self.released = [True] * 4
                self.tok = {}
                self.lo_engine = "vector"

            def pump(self):
                while self.loaded < len(self.plan) and self.loaded < self.taken + 4 and self.released[self.loaded % 4]:
                    n = self.loaded
                    src, a = self.plan[n]
                    r, s = n % 2, n % 4
                    raw, hi, lo = Wraw[r], Whi[s], Wlo[s]
                    d = dma(raw[:].rearrange("p (a b) -> p a b", a=a), src, f"w{r}", self.raw_free[r])
                    th = op("scalar", lambda e, raw=raw, hi=hi: e.activation(hi[:], raw[:], ACT.Copy), d, self.free[s])
                    tl = op(self.lo_engine, lambda e, raw=raw, hi=hi, lo=lo: e.tensor_tensor(
                        lo[:], raw[:], hi[:].bitcast(F), ALU.subtract), th, self.free[s])
                    self.raw_free[r] = [th, tl]
                    self.tok[n] = (th, tl)
                    self.released[s] = False
                    self.loaded += 1

            def get(self, a):
                n = self.taken
                self.taken += 1
                self.pump()
                assert self.loaded > n and self.plan[n][1] == a
                s = n % 4
                v = lambda t: t[:].rearrange("p (a b) -> p a b", a=a)
                return v(Whi[s]), v(Wlo[s]), self.tok[n][0], self.tok[n][1], s

            def release(self, s, tok):
                self.free[s] = [tok]
                self.released[s] = True
                self.pump()

        W = Weights()

        def cols128(w, c0, rows=1024, r0=0):
            return (w[r0:r0 + rows, c0:c0 + 128].rearrange("(k p) c -> p k c", p=P), rows // P)

        def cols256(w, c0, r0):
            return (w[r0:r0 + 512, c0:c0 + 256].rearrange("(k p) c -> p k c", p=P), 4)

        for h in range(8):
            W.plan += [cols128(w_in, 1024 + 128 * h), cols128(w_in, 128 * h), cols128(w_in, 3072 + 128 * h)]
            if h % 2 == 0:
                W.plan += [cols256(w_in, 2048 + 128 * h, 0), cols256(w_in, 2048 + 128 * h, 512)]
        W.plan += [cols128(w_out, 128 * m) for m in range(8)]

        def mlp_plan(w1, w2):
            s1 = lambda t: [cols128(w1, 128 * t)]
            s2 = lambda c: [cols256(w2, 256 * j, 512 * c) for j in range(4)]
            order = []
            for t in range(4):
                order += s1(t)
            for c in range(8):
                if c < 7:
                    order += s1(4 * c + 4)
                order += s2(c)
                if c < 7:
                    for t in range(4 * c + 5, 4 * c + 8):
                        order += s1(t)
            return order

        W.plan += mlp_plan(m_w1, m_w2)
        if stage > 3:
            for c0 in (0, 256):
                W.plan += [cols256(w_in2, c0, 0), cols256(w_in2, c0, 512)]
            for par in range(2):
                for j in range(2):
                    for cs in range(2):
                        W.plan.append((dft_d[par, cs].rearrange("(k p) c -> p k c", p=P)[:, :, 256 * j:256 * j + 256], 4))
            for m in range(0, 8, 2):
                W.plan += [cols128(w_gate, 128 * m), cols128(w_gate, 128 * m + 128), cols256(w_fo, 128 * m, 0)]
            for c0 in (1024, 1280, 1536, 1792):
                W.plan += [cols256(w_in2, c0, 0), cols256(w_in2, c0, 512)]
            for half in range(2):
                for c0 in (512, 1024, 1536):
                    W.plan += [cols256(w_in2, c0 + 256 * half, 0), cols256(w_in2, c0 + 256 * half, 512)]
            for m in range(0, 8, 2):
                W.plan += [cols128(w_gate, 1024 + 128 * m), cols128(w_gate, 1152 + 128 * m), cols256(w_ao, 128 * m, 0)]
            W.plan += [cols128(w_o2, 128 * m) for m in range(8)]
            W.plan += mlp_plan(m2_w1, m2_w2)

        def mm(out_, l, r, *waits, start=False, stop=False, sig=False):
            return op("tensor", lambda e: e.matmul(out_, l, r, start=start, stop=stop), *waits, sig=sig)

        def fm_steps(ps, psw, w, kt, Ah, Al, tokh, tokl, m0=0, nw=128):
            wh, wl, th, tl, _ = w
            last = None
            for k in range(kt):
                for hf in range(2):
                    c = slice(512 * hf, 512 * hf + 512)
                    mm(ps[:, c], wh[:, k, m0:m0 + nw], Ah[:, k, c], psw, th, tokh[k], start=(k == 0))
                for hf in range(2):
                    c = slice(512 * hf, 512 * hf + 512)
                    mm(ps[:, c], wl[:, k, m0:m0 + nw], Ah[:, k, c], tl)
                if k % 2:
                    yield None
            for k in range(kt):
                for hf in range(2):
                    c = slice(512 * hf, 512 * hf + 512)
                    end = k == kt - 1
                    last = mm(ps[:, c], wh[:, k, m0:m0 + nw], Al[:, k, c], tokl[k], stop=end, sig=end and hf == 1)
                if k % 2:
                    yield None
            return last

        def fm_tile(ring, kt, Ah, Al, tokh, tokl, post, w=None, m0=0, release=True):
            if w is None:
                w = W.get(kt)
            ps, psw, i = ring.get()
            last = yield from fm_steps(ps, psw, w, kt, Ah, Al, tokh, tokl, m0)
            if release:
                W.release(w[4], last)
            post(ps, last, ring, i)

        def tm_pair(ring, tiles, Ah, Al, tokh, tokl, post):
            ws = [W.get(4), W.get(4)]
            last = None
            for s in range((tiles + 3) // 4):
                ps, psw, i = ring.get()
                nt = min(4, tiles - 4 * s)
                for t in range(nt):
                    o = ps[:, 256 * t:256 * t + 256]
                    c = slice(128 * (4 * s + t), 128 * (4 * s + t) + 128)
                    for k in range(8):
                        wh, wl, th, tl, _ = ws[k // 4]
                        mm(o, Ah[:, k, c], wh[:, k % 4, :], psw, th, tokh[k], start=(k == 0))
                        mm(o, Ah[:, k, c], wl[:, k % 4, :], tl)
                        end = k == 7
                        last = mm(o, Al[:, k, c], wh[:, k % 4, :], tokl[k], stop=end, sig=end and t == nt - 1)
                        if k % 2:
                            yield None
                if s == (tiles + 3) // 4 - 1:
                    for w in ws:
                        W.release(w[4], last)
                post(s, ps, last, ring, i)

        def drain(g):
            for _ in g:
                pass

        allps = Ring(psum)

        t_id = dma(ident[:], ident_d, "c0")
        t_vec = dma(vec[:], vecs, "c1")
        t_x = [dma(R1[:, k, :], xT[k], f"x{k}") for k in range(8)]
        t_ones = op("vector", lambda e: e.memset(ones[:], 1.0))
        t_eps = op("vector", lambda e: e.memset(eps[:], EPS))

        lbr = vec[:, V_LB:V_LB + 8]
        a = op("vector", lambda e: e.tensor_tensor(lt[:, 0, :], lbr, lbr, ALU.subtract), t_vec)
        a = op("scalar", lambda e: e.activation(lt[:, 1, :], lt[:, 0, :], ACT.Exp), a)
        a = op("vector", lambda e: e.reciprocal(lt[:, 2, :], lt[:, 1, :]), a)
        a = op("vector", lambda e: e.tensor_tensor(lt[:, 0, :], lt[:, 1, :], lt[:, 2, :], ALU.mult), a)
        a = op("vector", lambda e: e.tensor_tensor(lb[:], lt[:, 0, :], lt[:, 0, :], ALU.subtract), a)
        t_lb = op("vector", lambda e: e.tensor_scalar(oml[:], lb[:], -1.0, 1.0, ALU.mult, ALU.add), a)
        cc = vec[:, V_C:V_C + 16].rearrange("p (two k) -> p k two", two=2)
        a = op("scalar", lambda e: e.activation(csil[:], cc, ACT.Sigmoid), t_vec)
        t_csil = op("vector", lambda e: e.tensor_tensor(csil[:], csil[:], cc, ALU.mult), a)

        class Stats:

            def __init__(self, acc, sq, waits, n=T):
                self.acc, self.sq = acc, sq
                self.sqfree = [list(waits) for _ in sq]
                self.i, self.n = 0, n
                self.tok = list(waits)

            def add(self, x, tok):
                n = self.n
                if self.i == 0:
                    self.tok = [op("scalar", lambda e: e.activation(self.acc[:, :n], x, ACT.Square), tok, self.tok)]
                else:
                    s = self.i % len(self.sq)
                    sq = self.sq[s]
                    a = op("scalar", lambda e: e.activation(sq[:, :n], x, ACT.Square), tok, self.sqfree[s])
                    b = op("vector", lambda e: e.tensor_tensor(self.acc[:, :n], self.acc[:, :n], sq[:, :n], ALU.add),
                           a, self.tok)
                    self.tok = [b]
                    self.sqfree[s] = [b]
                self.i += 1

            def finish(self, ring, rstd, waits, inv=1.0 / 1024):
                ps, psw, i = ring.get()
                n = self.n
                w = min(512, n)
                toks = []
                for c0 in range(0, n, w):
                    c = slice(c0, c0 + w)
                    a = mm(ps[:, c], ones[:], self.acc[:, c], psw, self.tok, t_ones, start=True, stop=True, sig=True)
                    b = op("scalar", lambda e, c=c: e.activation(rstd[:, c], ps[:, c], ACT.Ln, bias=eps[:, 0:1],
                                                                 scale=inv), a, t_eps, waits)
                    d = op("scalar", lambda e, c=c: e.activation(rstd[:, c], rstd[:, c], ACT.Exp, scale=-0.5), b)
                    toks.append(d)
                ring.release(i, toks[-1])
                return toks[-1]

        def split(src, hi, lo, tok, waits, lo_engine="vector"):
            th = op("scalar", lambda e: e.activation(hi, src, ACT.Copy), tok, waits)
            tl = op(lo_engine, lambda e: e.tensor_tensor(lo, src, hi.bitcast(F), ALU.subtract), th, waits)
            return th, tl

        def apply_norm(xk, tok, gain, rstd, rt, tmps, Hh_, Hl_, waits, shift=None, n=T):
            tokh, tokl = [], []
            free = [[] for _ in tmps]
            for k in range(8):
                s = k % len(tmps)
                t = tmps[s]
                a = op("vector", lambda e, k=k, t=t: e.scalar_tensor_tensor(
                    t[:, :n], xk(k), gain(k), rstd[:, :n], ALU.mult, ALU.mult), tok[k], rt, free[s], waits)
                hi, lo = Hh_[:, k, :n], Hl_[:, k, :n]
                if shift is None:
                    th, tl = split(t[:, :n], hi, lo, a, waits, "gpsimd" if k % 2 else "vector")
                else:
                    th = op("scalar", lambda e, k=k, t=t, hi=hi: e.activation(hi, t[:, :n], ACT.Identity,
                                                                              bias=shift(k)), a, waits)
                    tl = op("vector", lambda e, k=k, t=t, hi=hi, lo=lo: e.scalar_tensor_tensor(
                        lo, t[:, :n], shift(k), hi.bitcast(F), ALU.add, ALU.subtract), th, waits)
                free[s] = [th, tl]
                tokh.append(th)
                tokl.append(tl)
            return tokh, tokl, free

        col = lambda c: (lambda k: vec[:, c + k:c + k + 1])

        V = sa("V", 0, F, (P, 8, 256))
        qt, Pt, Sf, kt_, sg = (sa(n, i) for n, i in (("q", 2), ("Pt", 3), ("Sf", 4), ("kk", 5), ("sg", 6)))
        Mt = [sa(f"M{i}", 7 + i) for i in range(3)]
        acc = sa("acc", 10)
        kST = sa("kST", 11)
        St = sa("St", 12)
        t1, t2, t3 = sa("t1", 13), sa("t2", 14), sa("t3", 15)

        t_mraw = dma(Sf[:].rearrange("p (a b) -> p a b", a=8), masks_d, "c2")
        t_mask = op("gpsimd", lambda e: e.tensor_copy(masks[:], Sf[:].rearrange("p (a b) -> p a b", a=8)), t_mraw)
        st = Stats(t1, [t2, t3], [])
        for k in range(8):
            st.add(R1[:, k, :], t_x[k])
        W.pump()
        rt = st.finish(allps, t2, st.sqfree[0])
        tokh, tokl, fr = apply_norm(lambda k: R1[:, k, :], t_x, col(V_MIX), t2, rt, [t3, kST, St], Hh, Hl, [t_vec])
        h_done = tokl[-1]
        t_memacc = op("gpsimd", lambda e: e.memset(acc[:], 0.0))

        A = Ring(psum[0:2])
        B = Ring(psum[2:4])
        A.free = [list(allps.free[0]), list(allps.free[1])]
        B.free = [list(allps.free[2]), list(allps.free[3])]
        c3 = lambda t: t[:].rearrange("p (c m) -> p c m", m=128)
        mring = Ring(Mt)
        free = {n: [] for n in ("q", "P", "Sf", "k", "sg", "acc", "kST", "St", "tot", "V")}
        free["acc"] = [t_memacc]
        free["Sf"] = [t_mask]
        free["kST"] = fr[1]
        free["St"] = fr[2]
        free["t1"] = [rt]
        free["t2"] = list(tokl[-3:])
        free["t3"] = list(tokl[-3:])
        last_t = {}
        tv = {}
        oT = []

        def v_post(s, ps, last, ring, i):
            a = op("scalar", lambda e: e.activation(V[:, 4 * s:4 * s + 4, :],
                                                    ps[:].rearrange("p (c m) -> p c m", m=256), ACT.Copy),
                   last, free["V"])
            ring.release(i, a)
            tv[s] = a

        def head_f(h):
            def post(ps, last, ring, i):
                a = op("scalar", lambda e: e.activation(Pt[:], ps[:], ACT.Sigmoid), last, free["P"])
                b = op("scalar", lambda e: e.activation(kt_[:], ps[:], ACT.Sigmoid, scale=-1.0), last, free["k"])
                ring.release(i, b)
                last_t["P"] = op("vector", lambda e: e.tensor_scalar(Pt[:], Pt[:], oml[:, h:h + 1], lb[:, h:h + 1],
                                                                     ALU.mult, ALU.add), a, t_lb)
                last_t["k"] = op("vector", lambda e: e.tensor_scalar(kt_[:], kt_[:], oml[:, h:h + 1], None, ALU.mult),
                                 b, t_lb)
                last_t["Sf"] = op("gpsimd", lambda e: e.memset(Sf[:], 1.0), free["Sf"])
            return fm_tile(A, 8, Hh, Hl, tokh, tokl, post)

        def head_q(h):
            def post(ps, last, ring, i):
                a = op("scalar", lambda e: e.activation(qt[:], ps[:], ACT.Sigmoid), last, free["q"])
                b = op("vector", lambda e: e.scalar_tensor_tensor(qt[:], qt[:], float(128 ** -0.5), ps[:], ALU.mult,
                                                                  ALU.mult), a)
                ring.release(i, b)
                last_t["q"] = b
            return fm_tile(A, 8, Hh, Hl, tokh, tokl, post)

        def head_g(h):
            def post(ps, last, ring, i):
                a = op("scalar", lambda e: e.activation(sg[:], ps[:], ACT.Sigmoid), last, free["sg"])
                b = op("vector", lambda e: e.tensor_tensor(sg[:], sg[:], ps[:], ALU.mult), a)
                ring.release(i, b)
                last_t["sg"] = b
                last_t["proj"] = last
            return fm_tile(A, 8, Hh, Hl, tokh, tokl, post)

        def scan_levels(h):
            tq, tk, tp, ts = last_t["q"], last_t["k"], last_t["P"], last_t["Sf"]
            k3, q3, a3 = c3(kt_), c3(qt), c3(acc)

            def masked(ps, i, tok, lev, prev):
                toks = []
                for hf in range(2):
                    c = slice(4 * hf, 4 * hf + 4)
                    toks.append(op("vector", lambda e, c=c: e.copy_predicated(
                        a3[:, c, :], masks[:, lev, :][:, None, :].broadcast_to([P, 4, P]), c3(ps)[:, c, :]),
                        tok, t_mask, prev[hf]))
                B.release(i, toks[1])
                return toks

            ps, psw, i = B.get()
            for c in range(8):
                last = mm(c3(ps)[:, c, :], k3[:, c, :], q3[:, c, :], psw, tq, tk, start=True, stop=True, sig=c == 7)
            prev = masked(ps, i, last, 0, [free["acc"], free["acc"]])
            yield None
            m = 1
            lev = 1
            while m < 128:
                v = lambda t, m=m: t[:].rearrange("p (b two m) -> p b two m", two=2, m=m)
                M, mw, mi = mring.get()
                nb = T // (2 * m)
                a = op("vector", lambda e, v=v, M=M: e.tensor_tensor(v(M)[:, :, 1, :], v(qt)[:, :, 1, :],
                                                                     v(Pt)[:, :, 1, :], ALU.mult), mw, tq, tp)
                b = op("gpsimd", lambda e, v=v, M=M: e.tensor_tensor(v(M)[:, :, 0, :], v(kt_)[:, :, 0, :],
                                                                     v(Sf)[:, :, 0, :], ALU.mult), mw, tk, ts)
                ps, psw, i = B.get()
                M3 = c3(M)
                for c in range(8):
                    last = mm(c3(ps)[:, c, :], M3[:, c, :], M3[:, c, :], psw, a, b, start=True, stop=True, sig=c == 7)
                mring.release(mi, last)
                sh = [P, nb, m]
                ts = op("gpsimd", lambda e, v=v, m=m, sh=sh: e.tensor_tensor(
                    v(Sf)[:, :, 0, :], v(Sf)[:, :, 0, :], v(Pt)[:, :, 1, m - 1:m].broadcast_to(sh), ALU.mult), b, tp, ts)
                tp = op("vector", lambda e, v=v, m=m, sh=sh: e.tensor_tensor(
                    v(Pt)[:, :, 1, :], v(Pt)[:, :, 1, :], v(Pt)[:, :, 0, m - 1:m].broadcast_to(sh), ALU.mult), a, ts)
                prev = masked(ps, i, last, lev, prev)
                yield None
                m *= 2
                lev += 1
            last_t["acc"] = prev
            kS, kw, ki = mring.get()
            tks = op("gpsimd", lambda e: e.tensor_tensor(kS[:], kt_[:], Sf[:], ALU.mult), kw, tk, ts)
            free["k"] = [last, tks]
            free["Sf"] = [tks]
            qP, qw, qi = mring.get()
            tqp = op("vector", lambda e: e.tensor_tensor(qP[:], qt[:], Pt[:], ALU.mult), qw, tq, tp)
            ttot = op("vector", lambda e: e.tensor_copy(tot[:], c3(Pt)[:, :, 127]), tp, free["tot"])
            free["q"] = [last, tqp]
            free["P"] = [tqp, ttot, ts]
            last_t["kS"], last_t["qP"], last_t["tot"] = (kS, tks, ki), (qP, tqp, qi), ttot

        def scan_tail(h):
            kS, tks, ki = last_t["kS"]
            qP, tqp, qi = last_t["qP"]
            acct = last_t["acc"]
            tsg = last_t["sg"]
            vo = 128 * (h % 2)
            a3 = c3(acc)
            ps, psw, i = B.get()
            for c in range(7):
                last = op("tensor", lambda e, c=c, ps=ps: e.transpose(c3(ps)[:, c, :], c3(kS)[:, c, :], ident[:]),
                          psw, tks, t_id, sig=c == 6)
            mring.release(ki, last)
            t = op("scalar", lambda e, ps=ps: e.activation(kST[:, 0:896], ps[:, 0:896], ACT.Copy), last, free["kST"])
            B.release(i, t)
            yield None
            yield None
            ps, psw, i = B.get()
            for c in range(7):
                last = mm(c3(ps)[:, c, :], c3(kST)[:, c, :], V[:, c, vo:vo + 128], psw, t, tv[0], tv[1], start=True,
                          stop=True, sig=c == 6)
            free["kST"] = [last]
            s3 = c3(St)
            t = op("vector", lambda e, ps=ps: e.tensor_copy(s3[:, 1, :], c3(ps)[:, 0, :]), last, free["St"])
            for c in range(1, 7):
                t = op("vector", lambda e, c=c, ps=ps: e.scalar_tensor_tensor(
                    s3[:, c + 1, :], s3[:, c, :], tot[:, c:c + 1], c3(ps)[:, c, :], ALU.mult, ALU.add), t,
                    last_t["tot"])
            B.release(i, t)
            free["tot"] = [t]
            yield None
            yield None
            ps, psw, i = B.get()
            for c in range(8):
                mm(c3(ps)[:, c, :], V[:, c, vo:vo + 128], a3[:, c, :], psw, acct, tv[0], tv[1], start=True,
                   stop=(c == 0))
                if c:
                    last = mm(c3(ps)[:, c, :], s3[:, c, :], c3(qP)[:, c, :], tqp, t, stop=True, sig=c == 7)
            mring.release(qi, last)
            free["acc"] = [last]
            free["St"] = [last]
            free["V"] = [last]
            to = op("scalar", lambda e, ps=ps: e.activation(R1[:, h, :], ps[:], ACT.Copy), last, h_done)
            tq2 = op("scalar", lambda e, ps=ps: e.activation(t1[:], ps[:], ACT.Square), last, free["t1"])
            B.release(i, to, tq2)
            yield None
            yield None
            ps, psw, i = B.get()
            for hf in range(2):
                c = slice(512 * hf, 512 * hf + 512)
                last = mm(ps[:, c], ones[:], t1[:, c], psw, tq2, start=True, stop=True, sig=hf == 1)
            free["t1"] = [last]
            t = op("scalar", lambda e, ps=ps: e.activation(t2[:], ps[:], ACT.Ln, bias=eps[:, 0:1], scale=1.0 / 128),
                   last, free["t2"])
            B.release(i, t)
            t = op("scalar", lambda e: e.activation(t2[:], t2[:], ACT.Exp, scale=-0.5), t)
            t = op("vector", lambda e: e.tensor_tensor(t2[:], t2[:], sg[:], ALU.mult), t, tsg)
            free["sg"] = [t]
            t = op("vector", lambda e: e.scalar_tensor_tensor(R1[:, h, :], R1[:, h, :],
                                                              vec[:, V_ON + h:V_ON + h + 1], t2[:], ALU.mult,
                                                              ALU.mult), t, to)
            free["t2"] = [t]
            oT.append(t)
            yield None

        def chain(*gs):
            for g in gs:
                yield from g

        tail = None
        for h in range(8):
            run_both(head_f(h), tail, 1)
            drain(head_q(h))
            more = [head_g(h)]
            if h % 2 == 0:
                more.append(tm_pair(A, 8, Hh, Hl, tokh, tokl, v_post))
            run_both(chain(*more), scan_levels(h), 1 if h % 2 else 4)
            tail = scan_tail(h)
        drain(tail)
        h_read = last_t["proj"]

        tokh, tokl = [], []
        for k in range(8):
            th, tl = split(R1[:, k, :], Hh[:, k, :], Hl[:, k, :], oT[k], [h_read], "gpsimd" if k % 2 else "vector")
            tokh.append(th)
            tokl.append(tl)
        t_x = [dma(R1[:, k, :], xT[k], f"x{k}", tokh[k], tokl[k]) for k in range(8)]
        allps.free = [A.free[0], A.free[1], B.free[0], B.free[1]]

        def add_tile(m, st, scale=None, tok=None, final=True):
            def post(ps, last, ring, i):
                if scale is None:
                    t = op("vector", lambda e: e.tensor_tensor(R1[:, m, :], ps[:], R1[:, m, :], ALU.add), last, tok[m])
                else:
                    t = op("vector", lambda e: e.scalar_tensor_tensor(R1[:, m, :], ps[:], scale(m), R1[:, m, :],
                                                                      ALU.mult, ALU.add), last, tok[m])
                ring.release(i, t)
                tok[m] = t
                if final and st is not None:
                    st.add(R1[:, m, :], t)
            return post

        tx = list(t_x)
        st = Stats(t1, [kST, t3], [free["t1"], free["kST"], free["t3"], free["t2"]])
        for m in range(8):
            drain(fm_tile(allps, 8, Hh, Hl, tokh, tokl, add_tile(m, st, tok=tx)))
        h_read = allps_last = Q.n["tensor"]
        h_read = ("tensor", h_read)

        def mlp(tx, tokh, tokl, waits, st_of, scale=None, done=None):
            ah = at("ah" + ("2" if scale else ""), [P, 5, T], R, SA)
            al = at("al" + ("2" if scale else ""), [P, 5, T], R, SA + 5 * 4096)
            nm = "m2" if scale else "m1"
            tr = Ring([sa(nm + "r0", 10), sa(nm + "r1", 11)])
            sr = Ring([sa(nm + "s0", 12), sa(nm + "s1", 13)])
            for r in (tr, sr):
                r.free = [list(waits) for _ in r.free]
            afree = [list(waits) for _ in range(5)]
            at_ = {}

            def s1(t):
                sl = t % 5

                def post(ps, last, ring, i):
                    rl, w1, i1 = tr.get()
                    a = op("scalar", lambda e: e.activation(rl[:], ps[:], ACT.Relu), last, w1)
                    ring.release(i, a)
                    sq, w2, i2 = sr.get()
                    b = op("vector", lambda e: e.tensor_tensor(sq[:], rl[:], rl[:], ALU.mult), a, w2)
                    tr.release(i1, b)
                    th, tl = split(sq[:], ah[:, sl, :], al[:, sl, :], b, afree[sl])
                    sr.release(i2, th, tl)
                    at_[t] = (th, tl)
                drain(fm_tile(allps, 8, Hh, Hl, tokh, tokl, post))

            def s2(c):
                for j in range(4):
                    w = W.get(4)
                    for mm_ in range(2):
                        m = 2 * j + mm_
                        ps, psw, i = allps.get()
                        for part in range(2):
                            for k in range(4):
                                sl = (4 * c + k) % 5
                                th, tl = at_[4 * c + k]
                                for hf in range(2):
                                    cs = slice(512 * hf, 512 * hf + 512)
                                    ws = slice(128 * mm_, 128 * mm_ + 128)
                                    if part == 0:
                                        mm(ps[:, cs], w[0][:, k, ws], ah[:, sl, cs], psw, w[2], th, start=(k == 0))
                                        mm(ps[:, cs], w[1][:, k, ws], ah[:, sl, cs], w[3])
                                    else:
                                        last = mm(ps[:, cs], w[0][:, k, ws], al[:, sl, cs], tl, stop=(k == 3),
                                                  sig=(k == 3 and hf == 1))
                        if mm_ == 1:
                            W.release(w[4], last)
                        if m == 7:
                            for k in range(4):
                                afree[(4 * c + k) % 5] = [last]
                        if c == 7 and m == 0:
                            done["st"] = st_of()
                        add_tile(m, done.get("st"), scale, tx, final=(c == 7))(ps, last, allps, i)
                        if c == 7 and done.get("post"):
                            done["post"](m)

            for t in range(4):
                s1(t)
            for c in range(8):
                if c < 7:
                    s1(4 * c + 4)
                s2(c)
                if c < 7:
                    for t in range(4 * c + 5, 4 * c + 8):
                        s1(t)
            done["relu"] = [x for r in (tr, sr) for f in r.free for x in f]

        if stage >= 2:
            rt = st.finish(allps, t2, st.sqfree[0])
            tokh, tokl, fr = apply_norm(lambda k: R1[:, k, :], tx, col(V_MLP), t2, rt, [t3, sa("t4", 9), sa("t5", 8)],
                                        Hh, Hl, [h_read, st.sqfree[1], st.sqfree[0]])
            tn = [tokl[-1], tokl[-2], tokh[-1]]
            done = {}
            n1, n2, n3 = sa("n1", 14), sa("n2", 15), sa("n3", 13)
            mlp(tx, tokh, tokl, tn, lambda: Stats(n1, [n2], tn), done=done)
            h_read = ("tensor", Q.n["tensor"])

        if stage >= 3:
            st = done["st"]
            rs = sa("rs", 12)
            rt = st.finish(allps, rs, done["relu"])
            st2 = Stats(n1, [n2, n3], [rt, done["relu"]])
            for k in range(8):
                tx[k] = op("vector", lambda e, k=k: e.scalar_tensor_tensor(
                    R1[:, k, :], R1[:, k, :], vec[:, V_FINAL + k:V_FINAL + k + 1], rs[:], ALU.mult, ALU.mult),
                    rt, tx[k])
                if stage > 3:
                    st2.add(R1[:, k, :], tx[k])
        if stage > 3:
            pe_now = lambda: ("tensor", Q.n["tensor"])
            araw = [sa(f"araw{i}", i) for i in range(10)]
            af = [[h_read] for _ in araw]
            ps, psw, pi = allps.get()
            for m in range(48):
                r = m % 10
                d = dma(araw[r][:].rearrange("p (k c) -> p k c", k=8),
                        w_ada[:, 128 * m:128 * m + 128].rearrange("(k p) c -> p k c", p=P), f"a{r}", af[r])
                for k in range(8):
                    a = mm(ps[:, 2 * m:2 * m + 2], araw[r][:, 128 * k:128 * k + 128], csil[:, k, :], psw, d, t_csil,
                           start=(k == 0), stop=(k == 7), sig=(k == 7))
                af[r] = [a]
            t_mod = op("vector", lambda e, ps=ps: e.tensor_tensor(
                mods[:], ps[:, 0:96].rearrange("p (m c) -> p m c", c=2),
                vec[:, V_BADA:V_BADA + 48][:, :, None].broadcast_to([P, 48, 2]), ALU.add), a)
            allps.release(pi, t_mod)
            ada_done = a
            for j, (g0, m0, w0) in enumerate(((V_N1, 8, 0), (V_N1, 8, 1), (V_N2, 32, 0))):
                t_A = op("vector", lambda e, j=j, g0=g0, m0=m0, w0=w0: e.scalar_tensor_tensor(
                    modA[:, j, :], mods[:, m0:m0 + 8, w0], 1.0, vec[:, g0:g0 + 8], ALU.add, ALU.mult), t_mod)
            gA = lambda j: (lambda k: modA[:, j, k:k + 1])
            mc = lambda m0, w0=0: (lambda k: mods[:, m0 + k, w0:w0 + 1])

            rt = st2.finish(allps, rs, tx[7])
            t_sp = [dma(xs_d[k], R1[:, k, :], f"sp{k}", tx[k]) for k in range(8)]
            tokh, tokl, fr = apply_norm(lambda k: R1[:, k, :], tx, gA(0), rs, rt, [n1, n2, n3], Hh, Hl,
                                        [h_read, t_A, st2.sqfree, st2.tok], shift=mc(0))
            x_free = [tokh, tokl]

            U = [[at(f"U{a}{b}", [P, 4, 512], R, R1A + 8192 * (2 * a + b)) for b in range(2)] for a in range(2)]
            Yh, Yl = at("Yh", [P, 4, T], R, SA), at("Yl", [P, 4, T], R, SA + 16384)
            Z = [[sa(f"Z{a}{b}", 8 + 2 * a + b, R) for b in range(2)] for a in range(2)]
            f1, f2, f3 = sa("f1", 12), sa("f2", 13), sa("f3", 14)
            CD = [[sa(f"CD{b}", 15, R, (P, 4, 128))[:, 2 * b + a, :] for b in range(2)] for a in range(2)]
            cdr = at("cdr", [P, 2, 128], F, SA + 15 * 4096 + 2048)
            n_done = [tokl[-1], tokl[-2], tokl[-3], tokh[-1]]
            d = dma(cdr[:], cd_d, "c3", n_done, ada_done)
            cdt = []
            for a in range(2):
                cdt += split(cdr[:, a, :], CD[a][0], CD[a][1], d, n_done)
            tU = []
            ufree = {"f1": n_done, "f2": n_done, "f3": n_done}
            sp_done = [t_sp, x_free]

            def u_post(c0):
                held = {}

                def post(s, ps, last, ring, i):
                    if s == 0:
                        held[0] = (ps, last, ring, i)
                        return
                    ps0, l0, _, i0 = held[0]
                    a = op("scalar", lambda e: e.activation(f1[:], ps0[:], ACT.Copy), l0, ufree["f1"])
                    ring.release(i0, a)
                    b = op("vector", lambda e: e.tensor_tensor(f2[:], f1[:], ps[:], ALU.add), a, last, ufree["f2"])
                    c = op("vector", lambda e: e.tensor_tensor(f3[:], f1[:], ps[:], ALU.subtract), a, last,
                           ufree["f3"])
                    ring.release(i, c)
                    ufree["f1"] = [c, b]
                    for par, (f, t, nm) in enumerate(((f2, b, "f2"), (f3, c, "f3"))):
                        f4 = f[:].rearrange("p (t c) -> p t c", c=256)
                        th, tl = split(f4, U[par][0][:, :, c0:c0 + 256], U[par][1][:, :, c0:c0 + 256], t, sp_done)
                        ufree[nm] = [th, tl]
                        tU.extend([th, tl])
                return post

            for c0 in (0, 256):
                drain(tm_pair(allps, 8, Hh, Hl, tokh, tokl, u_post(c0)))

            zfree = [[], []]
            tY = []
            y_wait = [ada_done, af]

            def dft_step(par, j):
                tz = []
                for cs in range(2):
                    w = W.get(4)
                    ps, psw, i = allps.get()
                    for g in range(4):
                        o = ps[:, 256 * g:256 * g + 256]
                        gs = slice(128 * g, 128 * g + 128)
                        for k in range(4):
                            mm(o, U[par][0][:, k, gs], w[0][:, k, :], psw, w[2], tU, start=(k == 0))
                            mm(o, U[par][0][:, k, gs], w[1][:, k, :], w[3])
                            last = mm(o, U[par][1][:, k, gs], w[0][:, k, :], stop=(k == 3),
                                      sig=(k == 3 and g == 3))
                    W.release(w[4], last)
                    th, tl = split(ps[:], Z[cs][0][:], Z[cs][1][:], last, [zfree[cs], y_wait])
                    allps.release(i, th, tl)
                    tz.append((th, tl))
                return tz

            def chan_step(par, j, tz):
                ps, psw, i = allps.get()
                for g in range(4):
                    o = ps[:, 256 * g:256 * g + 256]
                    gs = slice(256 * g, 256 * g + 256)
                    for cs in range(2):
                        mm(o, CD[cs][0], Z[cs][0][:, gs], psw, tz[cs][0], cdt, start=(cs == 0))
                        mm(o, CD[cs][1], Z[cs][0][:, gs])
                        last = mm(o, CD[cs][0], Z[cs][1][:, gs], tz[cs][1], stop=(cs == 1), sig=(cs == 1 and g == 3))
                zfree[0] = [last]
                zfree[1] = [last]
                v = lambda t: t[:].rearrange("p g (n two) -> p g n two", two=2)[:, :, 256 * j:256 * j + 256, par]
                th, tl = split(ps[:].rearrange("p (g n) -> p g n", g=4), v(Yh), v(Yl), last, [y_wait])
                allps.release(i, th, tl)
                tY.extend([th, tl])

            for par in range(2):
                for j in range(2):
                    chan_step(par, j, dft_step(par, j))
            u_done = pe_now()

            cx = at("cx", [P, 8, 256], F, R1A)
            cacc, csq, crs = (at(n, [P, 256], F, R1A + 8192 + 1024 * i) for i, n in enumerate(("cacc", "csq", "crs")))
            ctmp = [at(f"ctmp{i}", [P, 256], F, R1A + 12288 + 1024 * i) for i in range(3)]
            hch, hcl = at("hch", [P, 8, 256], R, SA + 8 * 4096), at("hcl", [P, 8, 256], R, SA + 10 * 4096)
            gnq = at("gnq", [P, 128], F, R1A + 24576 - 512)
            tcx = dma(cx[:], ctxT.rearrange("k p t -> p k t"), "c3", u_done, tU)
            t_g = dma(gnq[:], gains, "c4", u_done, tU)
            stc = Stats(cacc, [csq], [u_done, tU], n=256)
            for k in range(8):
                stc.add(cx[:, k, :], tcx)
            rtc = stc.finish(allps, crs, [u_done, tU])
            tch, tcl, _ = apply_norm(lambda k: cx[:, k, :], [tcx] * 8, gA(1), crs, rtc, ctmp, hch, hcl,
                                     [u_done, tU], shift=mc(0, 1), n=256)

            mfr = Ring([sa("mf0", 12), sa("mf1", 13)])
            sgr = Ring([sa("sgr0", 14), sa("sgr1", 15)])
            for r in (mfr, sgr):
                r.free = [[u_done, tU, cdt] for _ in r.free]
            mf_st = {}

            def gate(sigs):
                def post(ps, last, ring, i):
                    g, w, gi = sgr.get()
                    a = op("scalar", lambda e: e.activation(g[:], ps[:], ACT.Sigmoid), last, w)
                    ring.release(i, a)
                    sigs.append((g, a, gi))
                return post

            for m in range(0, 8, 2):
                sigs = []
                for x in range(2):
                    drain(fm_tile(allps, 8, Hh, Hl, tokh, tokl, gate(sigs)))
                w = W.get(4)
                for x in range(2):
                    def post(ps, last, ring, i, x=x):
                        g, a, gi = sigs[x]
                        o, ow, oi = mfr.get()
                        b = op("vector", lambda e: e.tensor_tensor(o[:], g[:], ps[:], ALU.mult), a, last, ow)
                        ring.release(i, b)
                        sgr.release(gi, b)
                        mf_st[m + x] = dma(mf_d[m + x], o[:], f"mf{(m + x) % 2}", b)
                        mfr.release(oi, mf_st[m + x])
                    drain(fm_tile(allps, 4, Yh, Yl, [tY] * 4, [tY] * 4, post, w=w, m0=128 * x, release=(x == 1)))
            y_read = pe_now()
            mf_done = [mf_st[6], mf_st[7]]

            qT = at("qT", [P, 2, T], F, R1A)
            kT = at("kT", [P, 2, T], F, R1A + 8192)
            Vx = at("Vx", [P, 8, 256], F, R1A + 16384)
            kcT = at("kcT", [P, 4, 256], F, R1A + 24576)
            vc = at("vc", [P, 2, 512], F, R1A + 28672)
            gq = const("gq", [P, 128])
            rope = at("rope", [P, 2, 8, 64], F, SA)
            a1, a2, a3_ = (sa(n, 1 + i) for i, n in enumerate(("a1", "a2", "a3")))
            ya = at("ya", [P, 4, T], F, SA + 8 * 4096)
            be = [at(f"be{i}", [P, 14, 64], F, SA + (4 + i) * 4096) for i in range(2)]
            bm = [at(f"bm{i}", [P, 9, 64], F, SA + (6 + i) * 4096) for i in range(2)]
            pr = Ring([sa("pr0", 12), sa("pr1", 13)])
            ptr = Ring([sa("pt0", 14), sa("pt1", 15)])
            for r, src in ((pr, mfr), (ptr, sgr)):
                r.free = [list(f) for f in src.free]
            ctx_done = [tch, tcl, rtc, stc.tok, stc.sqfree]
            t_gq = op("vector", lambda e: e.tensor_scalar(gq[:, 0:64], gnq[:, 0:64], 0.125, None, ALU.mult), t_g)
            t_gk = op("vector", lambda e: e.tensor_copy(gq[:, 64:128], gnq[:, 64:128]), t_g)
            t_rope = dma(rope[:], rope_d.rearrange("p two t c -> p two t c"), "c5", y_read)
            fre = {n: [y_read] for n in ("a1", "a2", "a3")}

            def heads_post(nt, which, dst, tile0, roped, dfree):
                n = nt * 256

                def post(s, ps, last, ring, i):
                    v3 = lambda t: t[:, 0:n].rearrange("p (x c) -> p x c", c=64)
                    b3 = [P, n // 64, 64]
                    ss = small[:, 0:n // 64]
                    a = op("scalar", lambda e: e.activation(a1[:, 0:n], ps[:, 0:n], ACT.Copy), last, fre["a1"])
                    b = op("scalar", lambda e: e.activation(a2[:, 0:n], ps[:, 0:n], ACT.Square), last, fre["a2"])
                    ring.release(i, b)
                    c = op("vector", lambda e: e.tensor_reduce(ss, v3(a2), AX, ALU.add), b, fre.get("ss"))
                    c = op("scalar", lambda e: e.activation(ss, ss, ACT.Ln, bias=eps[:, 0:1], scale=1.0 / 64), c)
                    c = op("scalar", lambda e: e.activation(ss, ss, ACT.Exp, scale=-0.5), c)
                    c = op("vector", lambda e: e.tensor_tensor(v3(a1), v3(a1), ss[:, :, None].broadcast_to(b3),
                                                               ALU.mult), a, c)
                    fre["ss"] = [c]
                    gcol = gq[:, 64 * which:64 * which + 64][:, None, :].broadcast_to(b3)
                    c = op("vector", lambda e: e.tensor_tensor(v3(a1), v3(a1), gcol, ALU.mult), c, t_gq, t_gk)
                    src = a1
                    if roped:
                        tl0 = 4 * s
                        v4 = lambda t: t[:, 0:n].rearrange("p (t h c) -> p t h c", t=4, c=64)
                        tab = lambda j: rope[:, j, tl0:tl0 + 4, :][:, :, None, :].broadcast_to([P, 4, 4, 64])
                        d = op("vector", lambda e: e.tensor_tensor(v4(a2), v4(a1), tab(0), ALU.mult), c, t_rope)
                        for ax in range(2):
                            for hf in range(2):
                                o = slice(32 * ax + 16 * hf, 32 * ax + 16 * hf + 16)
                                w_ = slice(32 * ax + 16 - 16 * hf, 32 * ax + 32 - 16 * hf)
                                g = op("vector", lambda e, o=o, w_=w_: e.tensor_tensor(
                                    v4(a3_)[:, :, :, o], v4(a1)[:, :, :, w_], tab(1)[:, :, :, o], ALU.mult), c,
                                    t_rope, fre["a3"])
                        c = op("vector", lambda e: e.tensor_tensor(a2[:, 0:n], a2[:, 0:n], a3_[:, 0:n], ALU.add),
                               g, d)
                        fre["a1"] = [g, d]
                        fre["a3"] = [c]
                        src = a2
                    ps2, pw, i2 = ring.get()
                    for cb in range(2):
                        for t in range(nt):
                            l2 = op("tensor", lambda e, cb=cb, t=t: e.transpose(
                                ps2[:, 128 * (cb * nt + t):128 * (cb * nt + t) + 128],
                                src[:, 256 * t + 128 * cb:256 * t + 128 * cb + 128], ident[:]), pw, c,
                                sig=(cb == 1 and t == nt - 1))
                    if roped:
                        fre["a2"] = [l2]
                    else:
                        fre["a1"] = [l2]
                        fre["a2"] = [c]
                    td = op("scalar", lambda e: e.activation(
                        dst[:, tile0:tile0 + 2, 512 * s:512 * s + 128 * nt],
                        ps2[:, 0:256 * nt].rearrange("p (cb t) -> p cb t", cb=2), ACT.Copy), l2, dfree)
                    ring.release(i2, td)
                    att.append(td)
                return post

            att = []
            hist = [tch[7], tcl[7]]
            for j in range(2):
                drain(tm_pair(allps, 2, hch, hcl, tch, tcl, heads_post(2, 1, kcT, 2 * j, False, ctx_done)))
            for j in range(2):
                def vpost(s, ps, last, ring, i, j=j):
                    a = op("vector", lambda e: e.tensor_copy(vc[:, :, 256 * j:256 * j + 256],
                                                             ps[:, 0:512].rearrange("p (t c) -> p t c", t=2)), last,
                           ctx_done)
                    ring.release(i, a)
                    att.append(a)
                drain(tm_pair(allps, 2, hch, hcl, tch, tcl, vpost))
            hc_read = pe_now()
            ctx_att = list(att)

            bias_free = [[y_read], [y_read]]
            bias_t = {}

            def load_bias(h):
                i = h % 2
                bias_t[h] = [dma(be[i][:], biasE[h], f"be{i}", bias_free[i]),
                             dma(bm[i][:], biasM[h], f"bm{i}", bias_free[i])]

            tya = []
            attf = {"qT": [ctx_done, t_gq, t_gk], "O": [y_read]}
            for half in range(2):
                att = []
                drain(tm_pair(allps, 8, Hh, Hl, tokh, tokl, heads_post(4, 0, qT, 0, True, attf["qT"])))
                drain(tm_pair(allps, 8, Hh, Hl, tokh, tokl, heads_post(4, 1, kT, 0, True, attf["qT"])))

                def vpost(s, ps, last, ring, i):
                    a = op("vector", lambda e: e.tensor_copy(Vx[:, 4 * s:4 * s + 4, :],
                                                             ps[:].rearrange("p (t c) -> p t c", c=256)), last,
                           attf["qT"])
                    ring.release(i, a)
                    att.append(a)
                if half == 0:
                    load_bias(0)
                    load_bias(1)
                drain(tm_pair(allps, 8, Hh, Hl, tokh, tokl, vpost))
                att_t = [list(att), ctx_att]
                Ob = [sa(f"Ob{half}0", 1), sa(f"Ob{half}1", 2)]
                of = [[fre["a1"], fre["a2"], fre["a3"], attf["O"]] for _ in Ob]
                SR = Ring(psum[0:2])
                SR.free = [list(allps.free[0]), list(allps.free[1])]
                ptfree = list(allps.free[2])
                OR = Ring([psum[3][:, 0:512], psum[3][:, 512:1024]])
                OR.free = [list(allps.free[3]) for _ in range(2)]
                its = [(hh, j) for hh in range(4) for j in (0, 1, 6, 7, 2, 3, 4, 5)]
                state = {}

                def qk(n):
                    hh, j = its[n]
                    h = 4 * half + hh
                    cb, pb = hh // 2, 64 * (hh % 2)
                    mid_ = 2 <= j <= 5
                    rs_ = 2 * j - 4 if mid_ else (0 if j < 2 else 8)
                    ps, psw, i = SR.get()
                    q = qT[pb:pb + 64, cb, 128 * j:128 * j + 128]
                    mm(ps[:, 0:512], q, kT[pb:pb + 64, cb, 64 * rs_:64 * rs_ + 512], psw, att_t, start=True, stop=True)
                    if mid_:
                        mm(ps[:, 512:576], q, kT[pb:pb + 64, cb, 64 * rs_ + 512:64 * rs_ + 576], start=True, stop=True)
                    last = mm(ps[:, 576:832], q, kcT[pb:pb + 64, 2 * half + cb, :], start=True, stop=True, sig=True)
                    L = 576 if mid_ else 512
                    b = h % 2
                    if mid_:
                        bias = bm[b][:].rearrange("p a b -> p (a b)")
                    else:
                        i0 = rs_ - 2 * j + 6
                        bias = be[b][:, i0:i0 + 8, :].rearrange("p a b -> p (a b)")
                    pt, pw, pi = pr.get()
                    z = 32 + 8 * (n % 4)
                    col_ = lambda c: small[:, z + c:z + c + 1]
                    o4 = state.get(("s", n - 4))
                    a = op("vector", lambda e: e.tensor_reduce(col_(0), ps[:, 576:832], AX, ALU.max), last, o4)
                    a = op("vector", lambda e: e.tensor_tensor_reduce(pt[:, 0:L], ps[:, 0:L], bias, 1.0, col_(0),
                                                                      ALU.add, ALU.max, col_(1)), a, pw, bias_t[h])
                    if j == 5:
                        bias_free[b] = [a]
                        if h + 2 < 8:
                            load_bias(h + 2)
                    a = op("vector", lambda e: e.tensor_scalar(col_(2), col_(1), -1.0, None, ALU.mult), a)
                    x2 = op("scalar", lambda e: e.activation(pt[:, 576:832], ps[:, 576:832], ACT.Exp, bias=col_(2),
                                                             accum_out=col_(4)), a, pw)
                    SR.release(i, x2)
                    x1 = op("scalar", lambda e: e.activation(pt[:, 0:L], pt[:, 0:L], ACT.Exp, bias=col_(2),
                                                             accum_out=col_(3)), a)
                    state[n] = dict(pt=pt, pi=pi, x=[x1, x2], L=L, rs=rs_, z=z)

                def tr(n):
                    s = state[n]
                    hh, j = its[n]
                    ps = psum[2]
                    col_ = lambda c: small[:, s["z"] + c:s["z"] + c + 1]
                    a = op("vector", lambda e: e.tensor_tensor(col_(5), col_(3), col_(4), ALU.add), s["x"])
                    s["r"] = op("vector", lambda e: e.reciprocal(col_(6), col_(5)), a)
                    pt = s["pt"]
                    half9 = s["L"] == 576
                    for b in range(4):
                        last = op("tensor", lambda e, b=b: e.transpose(ps[:, 128 * b:128 * b + 128],
                                                                       pt[:, 128 * b:128 * b + 128], ident[:]),
                                  ptstate["free"], s["x"], sig=(b == 3))
                    first = last
                    for b in range(2):
                        last = op("tensor", lambda e, b=b: e.transpose(ps[:, 512 + 128 * b:640 + 128 * b],
                                                                       pt[:, 576 + 128 * b:704 + 128 * b], ident[:]),
                                  sig=(b == 1 and not half9))
                    if half9:
                        last = op("tensor", lambda e: e.transpose(ps[0:64, 768:896], pt[:, 512:576], ident[:]))
                    pr.release(s["pi"], last)
                    o, ow, oi = ptr.get()
                    c1 = op("vector", lambda e: e.tensor_copy(o[:, 0:512], ps[:, 0:512]), first, ow)
                    c2 = op("scalar", lambda e: e.activation(o[:, 512:768], ps[:, 512:768], ACT.Copy), last, ow)
                    if half9:
                        c2 = op("scalar", lambda e: e.activation(o[0:64, 768:896], ps[0:64, 768:896], ACT.Copy), last)
                    ptstate["free"] = [c1, c2]
                    s["o"], s["oi"], s["c"] = o, oi, [c1, c2]

                def pv(n):
                    s = state.pop(n)
                    hh, j = its[n]
                    h = 4 * half + hh
                    ob_, ow_, oi_ = OR.get()
                    O = ob_[:, 0:64]
                    t0 = s["rs"] // 2
                    o = s["o"]
                    half9 = s["L"] == 576
                    for b in range(4):
                        mm(O, o[:, 128 * b:128 * b + 128], Vx[:, t0 + b, 64 * hh:64 * hh + 64], ow_, s["c"],
                           start=(b == 0))
                    for b in range(2):
                        last = mm(O, o[:, 512 + 128 * b:640 + 128 * b], vc[:, b, 64 * h:64 * h + 64],
                                  stop=(b == 1 and not half9), sig=(b == 1 and not half9))
                    if half9:
                        last = mm(O, o[0:64, 768:896], Vx[0:64, t0 + 4, 64 * hh:64 * hh + 64], stop=True, sig=True)
                    ptr.release(s["oi"], last)
                    ob = Ob[hh // 2]
                    c0 = 128 * j + 64 * (hh % 2)
                    rc = small[:, s["z"] + 6:s["z"] + 7]
                    t = op("vector", lambda e: e.tensor_scalar(ob[:, c0:c0 + 64], O, rc, None, ALU.mult), last,
                           s["r"], of[hh // 2] if hh % 2 == 0 else None)
                    state[("s", n)] = t
                    OR.release(oi_, t)
                    if hh % 2 == 1 and j in (7, 5):
                        tiles = (0, 1, 6, 7) if j == 7 else (2, 3, 4, 5)
                        yb, yw, yi = OR.get()
                        for x, jj in enumerate(tiles):
                            l2 = op("tensor", lambda e, x=x, jj=jj: e.transpose(
                                yb[:, 128 * x:128 * x + 128], ob[:, 128 * jj:128 * jj + 128], ident[:]),
                                t, yw, sig=(x == 3))
                        cbk = 2 * half + hh // 2
                        if j == 7:
                            dst = ya[:, cbk, :].rearrange("p (a b) -> p a b", b=256)[:, 0:4:3, :]
                            srcv = yb.rearrange("p (a b) -> p a b", b=256)
                        else:
                            dst, srcv = ya[:, cbk, 256:768], yb
                        ty = op("scalar", lambda e: e.activation(dst, srcv, ACT.Copy), l2, hc_read)
                        OR.release(yi, ty)
                        attf["O"] = [l2]
                        tya.append(ty)

                ptstate = {"free": ptfree}
                N = len(its)
                for n in range(N + 2):
                    if n < N:
                        qk(n)
                    if 0 <= n - 1 < N:
                        tr(n - 1)
                    if n >= 2:
                        pv(n - 2)
                attf["qT"] = [pe_now()]
                allps.free = [SR.free[0], SR.free[1], ptstate["free"], [OR.free]]

            a_read = pe_now()
            t_mf = [dma(R1[:, m, :], mf_d[m], f"x{m}", a_read, mf_done, att_t) for m in range(8)]
            yah, yal = at("yah", [P, 4, T], R, SA), at("yal", [P, 4, T], R, SA + 16384)
            sgr2 = Ring([sa("sg20", 12), sa("sg21", 13)])
            mr2 = Ring([sa("mr20", 14), sa("mr21", 15)])
            for r, src in ((sgr2, pr), (mr2, ptr)):
                r.free = [list(f) for f in src.free]
            tyh, tyl = [], []
            for k in range(4):
                th, tl = split(ya[:, k, :], yah[:, k, :], yal[:, k, :], tya, [a_read, bias_free, fre["ss"]])
                tyh.append(th)
                tyl.append(tl)
            sgr = sgr2
            tm_ = [None] * 8
            for m in range(0, 8, 2):
                sigs = []
                for x in range(2):
                    def gpost(ps, last, ring, i):
                        g, w, gi = sgr2.get()
                        a = op("scalar", lambda e: e.activation(g[:], ps[:], ACT.Sigmoid), last, w)
                        ring.release(i, a)
                        sigs.append((g, a, gi))
                    drain(fm_tile(allps, 8, Hh, Hl, tokh, tokl, gpost))
                w = W.get(4)
                for x in range(2):
                    def post(ps, last, ring, i, mx=m + x, x=x):
                        g, a, gi = sigs[x]
                        o, ow, oi = mr2.get()
                        b = op("vector", lambda e: e.tensor_tensor(o[:], g[:], ps[:], ALU.mult), a, last, ow)
                        ring.release(i, b)
                        sgr2.release(gi, b)
                        b = op("vector", lambda e: e.tensor_tensor(R1[:, mx, :], R1[:, mx, :], o[:], ALU.add), b,
                               t_mf[mx])
                        mr2.release(oi, b)
                        tm_[mx] = b
                    drain(fm_tile(allps, 4, yah, yal, tyh, tyl, post, w=w, m0=128 * x, release=(x == 1)))
            h_read = pe_now()
            tokh, tokl = [], []
            for k in range(8):
                th, tl = split(R1[:, k, :], Hh[:, k, :], Hl[:, k, :], tm_[k], [h_read],
                               "gpsimd" if k % 2 else "vector")
                tokh.append(th)
                tokl.append(tl)
            tx = [dma(R1[:, k, :], xs_d[k], f"x{k}", tokh[k], tokl[k], t_sp[k]) for k in range(8)]
            b1, b2, b3_, b4 = sa("b1", 12), sa("b2", 13), sa("b3", 14), sa("b4", 15)
            bw = [sgr2.free, mr2.free]
            st = Stats(b1, [b2, b3_], bw)
            for m in range(8):
                drain(fm_tile(allps, 8, Hh, Hl, tokh, tokl, add_tile(m, st, mc(16), tok=tx)))
            h_read = pe_now()
            rt = st.finish(allps, b4, bw)
            tokh, tokl, fr = apply_norm(lambda k: R1[:, k, :], tx, gA(2), b4, rt, [sa("b5", 10), sa("b6", 11), b2],
                                        Hh, Hl, [h_read, t_A, st.sqfree], shift=mc(24))
            tn = [tokl[-1], tokl[-2], tokh[-1], tokh[-2], rt, st.tok, h_read]
            done = {"post": lambda m: outs.append(dma(out[m], R1[:, m, :], f"x{m}", tx[m]))}
            outs = []
            mlp(tx, tokh, tokl, tn, lambda: None, scale=mc(40), done=done)
        if stage <= 3:
            for k in range(8):
                dma(out[k], R1[:, k, :], f"x{k}", tx[k])
        fin = [(f"x{k}", Q.n[f"x{k}"]) for k in range(8)]
        Q.q["sync"].append((lambda e: None, (fin,), None, 0))

        block = ctx.enter_context(nc.Block())
        for name in ENGINES:
            on = {"tensor": block.tensor, "vector": block.vector, "scalar": block.scalar, "gpsimd": block.gpsimd,
                  "sync": block.sync}[name]
            on(lambda e, name=name: Q.emit(name, e))


def layout(inputs):
    c = np.ascontiguousarray
    f = np.float32
    i = inputs

    def fm(a):
        return c(np.asarray(a).T.reshape(8, 128, -1))

    def pk(a):
        return np.asarray(a).reshape(-1, 128).T

    vecs = c(np.concatenate([pk(i[n]) for n in (
        "norm_mix", "norm_mlp", "norm_final", "hgrn_lower_bound", "hgrn_out_norm", "norm1_g_2", "norm2_g_2", "c_2",
        "c_ctx_2", "b_ada_2")], axis=1))
    gains = c(np.broadcast_to(np.concatenate([i["q_norm_g_2"][0], i["k_norm_g_2"][0]]), (128, 128)))

    rpb = np.asarray(i["rpb_2"])[0]
    cq, ck = np.arange(64)[:, None], np.arange(64)[None, :]
    start = np.clip(cq - 8, 0, 48)
    inside = (ck >= start) & (ck < start + 16)
    idx = np.clip(ck - cq + 15, 0, 30)
    toe = np.where(inside[None, None], rpb[:, :, idx], f(NEG)).transpose(0, 2, 1, 3)
    edge = np.full((8, 128, 14, 64), NEG, f)
    edge[:, :64] = toe[:, :, 1:15]
    edge[:, 64:] = toe[:, :, 0:14]
    mid = np.full((8, 128, 9, 64), NEG, f)
    mid[:, :64, 0:8] = toe[:, :, 3:11]
    mid[:, 64:, 1:9] = toe[:, :, 3:11]

    s, t = np.arange(128)[:, None], np.arange(128)[None, :]
    masks = [s == t]
    for lev in range(7):
        m = 1 << lev
        masks.append((s // (2 * m) == t // (2 * m)) & (s // m % 2 == 0) & (t // m % 2 == 1))
    masks = c(np.stack(masks, 1).astype(f))

    tok = np.arange(1024)
    inv = f(10000.0) ** (-np.arange(0, 32, 2, dtype=f) / f(32))
    ang = np.stack([(tok // 64).astype(f)[:, None] * inv, (tok % 64).astype(f)[:, None] * inv], 1)
    cos, sin = np.cos(ang).astype(f), np.sin(ang).astype(f)
    rope = np.stack([np.stack([cos, cos], 2), np.stack([-sin, sin], 2)], 0)
    rope = c(rope.reshape(2, 8, 128, 64).transpose(2, 0, 1, 3))

    n = np.arange(512)
    dft = np.empty((2, 2, 512, 512))
    for par in range(2):
        a = 2 * np.pi * (n[:, None] * (2 * n[None, :] + par) % 1024) / 1024
        dft[par] = np.cos(a), np.sin(a)
    d = np.arange(128)
    a = 2 * np.pi * (d[:, None] * d[None, :] % 128) / 128
    g = 1.0 / np.sqrt(1024 * 128)
    cd = np.stack([np.cos(a) * g, -np.sin(a) * g], 1)

    return {
        "xT": fm(i["x"][0]), "vecs": vecs, "w_in": c(i["hgrn_w_in"][0]), "w_out": c(i["hgrn_w_out"][0]),
        "m_w1": c(i["mlp_w1"][0]), "m_w2": c(i["mlp_w2"][0]), "ctxT": fm(i["ctx_2"][0]), "w_ada": c(i["w_ada_2"][0]),
        "w_in2": c(i["w_in_2"][0]), "gains": gains, "biasE": c(edge), "biasM": c(mid),
        "w_gate": c(i["w_branch_gate_2"][0]), "w_fo": c(i["w_fourier_out_2"][0]), "w_ao": c(i["w_attn_out_2"][0]),
        "w_o2": c(i["w_out_2"][0]), "m2_w1": c(i["w_mlp1_2"][0]), "m2_w2": c(i["w_mlp2_2"][0]),
        "ident_d": np.eye(128, dtype=f), "masks_d": masks, "rope_d": rope, "dft_d": dft.astype(f),
        "cd_d": c(cd.astype(f)),
    }


def kernel(**inputs):
    from concourse import bacc
    from concourse.bass_utils import run_bass_kernel_spmd

    arrays = layout({k: np.asarray(v) for k, v in inputs.items()})
    nc = bacc.Bacc("TRN2", target_bir_lowering=False, num_devices=1)
    args = [nc.dram_tensor("in_" + n, a.shape, mybir.dt.from_np(a.dtype), kind="ExternalInput").ap()
            for n, a in arrays.items()]
    args.append(nc.dram_tensor("out_0", (8, 128, 1024), F, kind="ExternalOutput").ap())
    build(nc, *args)
    r = run_bass_kernel_spmd(nc, [{"in_" + n: a for n, a in arrays.items()}], core_ids=[0])
    got = np.asarray(r.results[0]["out_0"])
    return np.ascontiguousarray(got.reshape(1024, 1024).T).reshape(1, 1024, 1024)
```

```python
from contextlib import ExitStack

import numpy as np
import concourse.bass as bass
from concourse import mybir

F = mybir.dt.float32
R = mybir.dt.float32r
U8 = mybir.dt.uint8
ALU = mybir.AluOpType
ACT = mybir.ActivationFunctionType
AX = mybir.AxisListType.X

P = 128
T = 1024
EPS = 1e-6
NEG = -1.0e30
ENGINES = ("tensor", "vector", "scalar", "gpsimd", "sync")

V_MIX, V_MLP, V_FINAL, V_LB, V_ON, V_N1, V_N2, V_C, V_CC, V_BADA = range(0, 80, 8)
V_END = V_BADA + 48


class Queues:

    def __init__(self, nc, ctx):
        self.nc, self.ctx = nc, ctx
        self.q = {e: [] for e in ENGINES}
        self.sems = {}
        self.n = {}
        self.marks = []

    def mark(self, name):
        self.marks.append((name, len(self.q["tensor"])))

    def sem(self, name):
        if name not in self.sems:
            self.sems[name] = self.ctx.enter_context(self.nc.semaphore("s_" + name))
            self.n[name] = 0
        return self.sems[name]

    def op(self, engine, fn, *waits, sig=True):
        if sig:
            self.sem(engine)
            self.n[engine] += 1
        self.q[engine].append((fn, waits, engine if sig else None, 1))
        return (engine, self.n[engine]) if sig else None

    def dma(self, out, in_, lane, *waits):
        self.sem(lane)
        self.n[lane] += 16
        self.q["sync"].append((lambda e: e.dma_start(out, in_), waits, lane, 16))
        return (lane, self.n[lane])

    def emit(self, engine, e):
        seen = {}

        def wait(w):
            if w is None:
                return
            if isinstance(w, list):
                for x in w:
                    wait(x)
                return
            if isinstance(w, dict):
                wait(list(w.values()))
                return
            name, value = w
            if seen.get(name, 0) < value:
                seen[name] = value
                e.wait_ge(self.sems[name], value)

        for fn, waits, name, inc in self.q[engine]:
            wait(list(waits))
            ins = fn(e)
            if name:
                ins.then_inc(self.sems[name], inc)


class Ring:

    def __init__(self, items):
        self.items = items
        self.free = [[] for _ in items]
        self.i = -1

    def get(self):
        self.i = (self.i + 1) % len(self.items)
        return self.items[self.i], self.free[self.i], self.i

    def release(self, i, *tokens):
        self.free[i] = list(tokens)


def run_both(a, b, every=1):
    n = 0
    for _ in a:
        n += 1
        if n % every == 0 and b is not None:
            next(b, None)
    if b is not None:
        for _ in b:
            pass


def build(nc, xT, vecs, w_in, w_out, m_w1, m_w2, ctxT, w_ada, w_in2, gains, biasE, biasM, w_gate, w_fo, w_ao,
          w_o2, m2_w1, m2_w2, ident_d, masks_d, rope_d, dft_d, cd_d, out, stage=9):
    with ExitStack() as ctx:
        Q = Queues(nc, ctx)
        op, dma = Q.op, Q.dma
        base = 16512
        R1A = base
        HA = R1A + 32768
        WRA = HA + 65536
        WSA = WRA + 8192
        SA = WSA + 32768
        CA = SA + 65536

        def at(name, shape, dt, off):
            return nc.alloc_sbuf_tensor_at(name, shape, dt, offset=off)

        R1 = at("R1", [P, 8, T], F, R1A)
        Hh = at("Hh", [P, 8, T], R, HA)
        Hl = at("Hl", [P, 8, T], R, HA + 32768)
        HT = at("HT", [P, 8, T], F, HA + 32768)
        Wraw = [at(f"Wraw{i}", [P, 1024], F, WRA + 4096 * i) for i in range(2)]
        Whi = [at(f"Whi{i}", [P, 1024], R, WSA + 8192 * i) for i in range(4)]
        Wlo = [at(f"Wlo{i}", [P, 1024], R, WSA + 8192 * i + 4096) for i in range(4)]

        def sa(name, i, dt=F, shape=(P, 1024)):
            return at(name, list(shape), dt, SA + 4096 * i)

        coff = [CA]

        def const(name, shape, dt=F, size=4):
            n = int(np.prod(shape[1:])) * size
            t = at(name, shape, dt, coff[0])
            coff[0] += (n + 31) // 32 * 32
            assert coff[0] <= 229344
            return t

        ident = const("ident", [P, P])
        ones = const("ones", [P, P])
        vec = const("vec", [P, V_END])
        masks = const("masks", [P, 8, P], U8, 1)
        eps = const("eps", [P, 1])
        lb = const("lb", [P, 8])
        oml = const("oml", [P, 8])
        lt = const("lt", [P, 3, 8])
        tot = const("tot", [P, 8])
        csil = const("csil", [P, 8, 2])
        mods = const("mods", [P, 48, 2])
        modA = const("modA", [P, 3, 8])
        small = const("small", [P, 96])
        gq = const("gq", [P, 128])
        spare = coff[0]
        assert spare + 3328 <= 229344

        psum = [ctx.enter_context(nc.psum_tensor(f"ps{i}", [P, 1024], F)) for i in range(4)]
        xs_d = nc.dram_tensor("xs_scratch", [8, P, T], F, kind="Internal").ap()
        mf_d = nc.dram_tensor("mf_scratch", [8, P, T], F, kind="Internal").ap()

        class Weights:
            def __init__(self):
                self.plan = []
                self.loaded = 0
                self.taken = 0
                self.raw_free = [[], []]
                self.free = [[], [], [], []]
                self.released = [True] * 4
                self.tok = {}
                self.lo_engine = "vector"

            def pump(self):
                while self.loaded < len(self.plan) and self.loaded < self.taken + 4 and self.released[self.loaded % 4]:
                    n = self.loaded
                    src, a = self.plan[n]
                    r, s = n % 2, n % 4
                    raw, hi, lo = Wraw[r], Whi[s], Wlo[s]
                    d = dma(raw[:].rearrange("p (a b) -> p a b", a=a), src, f"w{r}", self.raw_free[r])
                    th = op("scalar", lambda e, raw=raw, hi=hi: e.activation(hi[:], raw[:], ACT.Copy), d, self.free[s])
                    tl = op(self.lo_engine, lambda e, raw=raw, hi=hi, lo=lo: e.tensor_tensor(
                        lo[:], raw[:], hi[:].bitcast(F), ALU.subtract), th, self.free[s])
                    self.raw_free[r] = [th, tl]
                    self.tok[n] = (th, tl)
                    self.released[s] = False
                    self.loaded += 1

            def get(self, a):
                n = self.taken
                self.taken += 1
                self.pump()
                assert self.loaded > n and self.plan[n][1] == a
                s = n % 4
                v = lambda t: t[:].rearrange("p (a b) -> p a b", a=a)
                return v(Whi[s]), v(Wlo[s]), self.tok[n][0], self.tok[n][1], s

            def release(self, s, tok):
                self.free[s] = [tok]
                self.released[s] = True
                self.pump()

        W = Weights()

        def cols128(w, c0, rows=1024, r0=0):
            return (w[r0:r0 + rows, c0:c0 + 128].rearrange("(k p) c -> p k c", p=P), rows // P)

        def cols256(w, c0, r0):
            return (w[r0:r0 + 512, c0:c0 + 256].rearrange("(k p) c -> p k c", p=P), 4)

        W.plan += [cols128(w_in, 1024)]
        for h in range(8):
            W.plan += [cols128(w_in, 128 * h), cols128(w_in, 3072 + 128 * h)]
            if h % 2 == 0:
                W.plan += [cols256(w_in, 2048 + 128 * h, 0), cols256(w_in, 2048 + 128 * h, 512)]
            if h < 7:
                W.plan += [cols128(w_in, 1152 + 128 * h)]
        W.plan += [cols128(w_out, 128 * m) for m in range(8)]

        def mlp_plan(w1, w2):
            s1 = lambda t: [cols128(w1, 128 * t)]
            s2 = lambda c: [cols256(w2, 256 * j, 512 * c) for j in range(4)]
            order = []
            for t in range(4):
                order += s1(t)
            for c in range(8):
                if c < 7:
                    order += s1(4 * c + 4)
                order += s2(c)
                if c < 7:
                    for t in range(4 * c + 5, 4 * c + 8):
                        order += s1(t)
            return order

        W.plan += mlp_plan(m_w1, m_w2)
        if stage > 3:
            for c0 in (0, 256):
                W.plan += [cols256(w_in2, c0, 0), cols256(w_in2, c0, 512)]
            for par in range(2):
                for j in range(2):
                    for cs in range(2):
                        W.plan.append((dft_d[par, cs].rearrange("(k p) c -> p k c", p=P)[:, :, 256 * j:256 * j + 256], 4))
            for m in range(0, 8, 2):
                W.plan += [cols128(w_gate, 128 * m), cols128(w_gate, 128 * m + 128), cols256(w_fo, 128 * m, 0)]
            for c0 in (1024, 1280, 1536, 1792):
                W.plan += [cols256(w_in2, c0, 0), cols256(w_in2, c0, 512)]
            for half in range(2):
                for c0 in (512, 1024, 1536):
                    W.plan += [cols256(w_in2, c0 + 256 * half, 0), cols256(w_in2, c0 + 256 * half, 512)]
            for m in range(0, 8, 2):
                W.plan += [cols128(w_gate, 1024 + 128 * m), cols128(w_gate, 1152 + 128 * m), cols256(w_ao, 128 * m, 0)]
            W.plan += [cols128(w_o2, 128 * m) for m in range(8)]
            W.plan += mlp_plan(m2_w1, m2_w2)

        def mm(out_, l, r, *waits, start=False, stop=False, sig=False):
            return op("tensor", lambda e: e.matmul(out_, l, r, start=start, stop=stop), *waits, sig=sig)

        def fm_steps(ps, psw, w, kt, Ah, Al, tokh, tokl, m0=0, nw=128):
            wh, wl, th, tl, _ = w
            last = None
            for k in range(kt):
                for hf in range(2):
                    c = slice(512 * hf, 512 * hf + 512)
                    mm(ps[:, c], wh[:, k, m0:m0 + nw], Ah[:, k, c], psw, th, tokh[k], start=(k == 0))
                for hf in range(2):
                    c = slice(512 * hf, 512 * hf + 512)
                    mm(ps[:, c], wl[:, k, m0:m0 + nw], Ah[:, k, c], tl)
                if k % 2:
                    yield None
            for k in range(kt):
                for hf in range(2):
                    c = slice(512 * hf, 512 * hf + 512)
                    end = k == kt - 1
                    last = mm(ps[:, c], wh[:, k, m0:m0 + nw], Al[:, k, c], tokl[k], stop=end, sig=end and hf == 1)
                if k % 2:
                    yield None
            return last

        def fm_tile(ring, kt, Ah, Al, tokh, tokl, post, w=None, m0=0, release=True, before=None):
            if w is None:
                w = W.get(kt)
            ps, psw, i = ring.get()
            last = yield from fm_steps(ps, psw, w, kt, Ah, Al, tokh, tokl, m0)
            if release:
                W.release(w[4], last)
            if before is not None:
                for _ in before:
                    pass
            post(ps, last, ring, i)

        def tm_pair(ring, tiles, Ah, Al, tokh, tokl, post):
            ws = [W.get(4), W.get(4)]
            last = None
            for s in range((tiles + 3) // 4):
                ps, psw, i = ring.get()
                nt = min(4, tiles - 4 * s)
                for t in range(nt):
                    o = ps[:, 256 * t:256 * t + 256]
                    c = slice(128 * (4 * s + t), 128 * (4 * s + t) + 128)
                    for k in range(8):
                        wh, wl, th, tl, _ = ws[k // 4]
                        mm(o, Ah[:, k, c], wh[:, k % 4, :], psw, th, tokh[k], start=(k == 0))
                        mm(o, Ah[:, k, c], wl[:, k % 4, :], tl)
                        end = k == 7
                        last = mm(o, Al[:, k, c], wh[:, k % 4, :], tokl[k], stop=end, sig=end and t == nt - 1)
                        if k % 2:
                            yield None
                if s == (tiles + 3) // 4 - 1:
                    for w in ws:
                        W.release(w[4], last)
                flush()
                post(s, ps, last, ring, i)

        def drain(g):
            for _ in g:
                pass

        allps = Ring(psum)
        pending = []

        def flush():
            while pending:
                pending.pop(0)()

        t_x = [dma(R1[:, k, :], xT[k], f"x{k}") for k in range(8)]
        t_vec = dma(vec[:], vecs, "c1")
        t_id = dma(ident[:], ident_d, "c0")
        t_ones = op("vector", lambda e: e.memset(ones[:], 1.0))
        t_eps = op("vector", lambda e: e.memset(eps[:], EPS))

        lbr = vec[:, V_LB:V_LB + 8]
        a = op("vector", lambda e: e.tensor_tensor(lt[:, 0, :], lbr, lbr, ALU.subtract), t_vec)
        a = op("scalar", lambda e: e.activation(lt[:, 1, :], lt[:, 0, :], ACT.Exp), a)
        a = op("vector", lambda e: e.reciprocal(lt[:, 2, :], lt[:, 1, :]), a)
        a = op("vector", lambda e: e.tensor_tensor(lt[:, 0, :], lt[:, 1, :], lt[:, 2, :], ALU.mult), a)
        a = op("vector", lambda e: e.tensor_tensor(lb[:], lt[:, 0, :], lt[:, 0, :], ALU.subtract), a)
        t_lb = op("vector", lambda e: e.tensor_scalar(oml[:], lb[:], -1.0, 1.0, ALU.mult, ALU.add), a)
        cc = vec[:, V_C:V_C + 16].rearrange("p (two k) -> p k two", two=2)
        a = op("scalar", lambda e: e.activation(csil[:], cc, ACT.Sigmoid), t_vec)
        t_csil = op("vector", lambda e: e.tensor_tensor(csil[:], csil[:], cc, ALU.mult), a)

        class Stats:

            def __init__(self, acc, sq, waits, n=T, acc2=None, gain=None):
                self.acc, self.sq, self.acc2, self.gain = acc, sq, acc2, gain
                self.tok2 = list(waits)
                self.sqfree = [list(waits) for _ in sq]
                self.i, self.n = 0, n
                self.tok = list(waits)

            def add(self, x, tok):
                n = self.n
                if self.i == 0:
                    self.tok = [op("scalar", lambda e: e.activation(self.acc[:, :n], x, ACT.Square), tok, self.tok)]
                else:
                    s = self.i % len(self.sq)
                    sq = self.sq[s]
                    a = op("scalar", lambda e: e.activation(sq[:, :n], x, ACT.Square), tok, self.sqfree[s])
                    b = op("vector", lambda e: e.tensor_tensor(self.acc[:, :n], self.acc[:, :n], sq[:, :n], ALU.add),
                           a, self.tok)
                    self.tok = [b]
                    self.sqfree[s] = [b]
                if self.acc2 is not None:
                    g = self.gain(self.i)
                    if self.i == 0:
                        self.tok2 = [op("scalar", lambda e: e.activation(self.acc2[:, :n], x, ACT.Square, scale=g),
                                        tok, self.tok2)]
                    else:
                        a = op("scalar", lambda e: e.activation(self.sq[0][:, :n], x, ACT.Square, scale=g), tok,
                               self.sqfree[0])
                        self.tok2 = [op("vector", lambda e: e.tensor_tensor(
                            self.acc2[:, :n], self.acc2[:, :n], self.sq[0][:, :n], ALU.add), a, self.tok2)]
                        self.sqfree[0] = self.tok2
                self.i += 1

            def second(self, ring, rs, rt, rs2, waits):
                ps, psw, i = ring.get()
                for c0 in range(0, T, 512):
                    c = slice(c0, c0 + 512)
                    a = mm(ps[:, c], ones[:], self.acc2[:, c], psw, self.tok2, start=True, stop=True, sig=True)
                    b = op("scalar", lambda e, c=c: e.activation(rs2[:, c], rs[:, c], ACT.Square), rt, waits)
                    b = op("vector", lambda e, c=c: e.tensor_tensor(rs2[:, c], rs2[:, c], ps[:, c], ALU.mult), a, b)
                    d = op("scalar", lambda e, c=c: e.activation(rs2[:, c], rs2[:, c], ACT.Ln, bias=eps[:, 0:1],
                                                                 scale=1.0 / 1024), b)
                    d = op("scalar", lambda e, c=c: e.activation(rs2[:, c], rs2[:, c], ACT.Exp, scale=-0.5), d)
                ring.release(i, b)
                return d

            def finish(self, ring, rstd, waits, inv=1.0 / 1024):
                ps, psw, i = ring.get()
                n = self.n
                w = min(512, n)
                toks = []
                for c0 in range(0, n, w):
                    c = slice(c0, c0 + w)
                    a = mm(ps[:, c], ones[:], self.acc[:, c], psw, self.tok, t_ones, start=True, stop=True, sig=True)
                    b = op("scalar", lambda e, c=c: e.activation(rstd[:, c], ps[:, c], ACT.Ln, bias=eps[:, 0:1],
                                                                 scale=inv), a, t_eps, waits)
                    d = op("scalar", lambda e, c=c: e.activation(rstd[:, c], rstd[:, c], ACT.Exp, scale=-0.5), b)
                    toks.append(d)
                ring.release(i, toks[-1])
                return toks[-1]

        def split(src, hi, lo, tok, waits, lo_engine="vector"):
            th = op("scalar", lambda e: e.activation(hi, src, ACT.Copy), tok, waits)
            tl = op(lo_engine, lambda e: e.tensor_tensor(lo, src, hi.bitcast(F), ALU.subtract), th, waits)
            return th, tl

        def apply_norm(xk, tok, gain, rstd, rt, Tk, Hh_, Hl_, waits, shift=None, n=T):
            ta = []
            for k in range(8):
                ta.append(op("vector", lambda e, k=k: e.scalar_tensor_tensor(
                    Tk[:, k, :n], xk(k), gain(k), rstd[:, :n], ALU.mult, ALU.mult), tok[k], rt, waits))
            tokh, tokl = [], []
            for k in range(8):
                t, hi, lo = Tk[:, k, :n], Hh_[:, k, :n], Hl_[:, k, :n]
                if shift is not None and k % 2 == 0:
                    a = op("scalar", lambda e, k=k, t=t: e.activation(t, t, ACT.Identity, bias=shift(k)), ta[k])
                    th = op("scalar", lambda e, t=t, hi=hi: e.activation(hi, t, ACT.Copy), a)
                elif shift is not None:
                    th = op("scalar", lambda e, k=k, t=t, hi=hi: e.activation(hi, t, ACT.Identity, bias=shift(k)),
                            ta[k])
                else:
                    th = op("scalar", lambda e, t=t, hi=hi: e.activation(hi, t, ACT.Copy), ta[k])
                if shift is not None and k % 2:
                    tl = op("vector", lambda e, k=k, t=t, hi=hi, lo=lo: e.scalar_tensor_tensor(
                        lo, t, shift(k), hi.bitcast(F), ALU.add, ALU.subtract), th)
                else:
                    tl = op("vector" if k % 2 else "gpsimd", lambda e, t=t, hi=hi, lo=lo: e.tensor_tensor(
                        lo, t, hi.bitcast(F), ALU.subtract), th)
                tokh.append(th)
                tokl.append(tl)
            return tokh, tokl

        col = lambda c: (lambda k: vec[:, c + k:c + k + 1])

        V = sa("V", 0, F, (P, 8, 256))
        qt, Pt, Sf, kt_, sg = (sa(n, i) for n, i in (("q", 2), ("Pt", 3), ("Sf", 4), ("kk", 5), ("sg", 6)))
        Mt = [sa(f"M{i}", 7 + i) for i in range(3)]
        acc = sa("acc", 10)
        kST = sa("kST", 11)
        St = sa("St", 12)
        t1, t2, t3 = sa("t1", 13), sa("t2", 14), sa("t3", 15)

        t_mraw = dma(Sf[:].rearrange("p (a b) -> p a b", a=8), masks_d, "c2")
        t_mask = op("gpsimd", lambda e: e.tensor_copy(masks[:], Sf[:].rearrange("p (a b) -> p a b", a=8)), t_mraw)
        Q.mark("norm1")
        st = Stats(t1, [t2, t3], [])
        for k in range(8):
            st.add(R1[:, k, :], t_x[k])
        W.pump()
        rt = st.finish(allps, t2, st.sqfree[0])
        tokh, tokl = apply_norm(lambda k: R1[:, k, :], t_x, col(V_MIX), t2, rt, HT, Hh, Hl, [t_vec])
        h_done = list(tokl)
        t_memacc = op("gpsimd", lambda e: e.memset(acc[:], 0.0))

        A = Ring(psum[0:2])
        B = Ring(psum[2:4])
        A.free = [list(allps.free[0]), list(allps.free[1])]
        B.free = [list(allps.free[2]), list(allps.free[3])]
        c3 = lambda t: t[:].rearrange("p (c m) -> p c m", m=128)
        mring = Ring(Mt)
        free = {n: [] for n in ("q", "P", "Sf", "k", "sg", "acc", "kST", "St", "tot", "V")}
        free["acc"] = [t_memacc]
        free["Sf"] = [t_mask]
        free["t1"] = [rt]
        free["t2"] = list(tokh)
        free["t3"] = list(tokh)
        last_t = {}
        tv = {}
        oT = []

        def v_post(s, ps, last, ring, i):
            a = op("scalar", lambda e: e.activation(V[:, 4 * s:4 * s + 4, :],
                                                    ps[:].rearrange("p (c m) -> p c m", m=256), ACT.Copy),
                   last, free["V"])
            ring.release(i, a)
            tv[s] = a

        def head_f(h, before=None):
            def post(ps, last, ring, i):
                a = op("scalar", lambda e: e.activation(Pt[:], ps[:], ACT.Sigmoid), last, free["P"])
                b = op("scalar", lambda e: e.activation(kt_[:], ps[:], ACT.Sigmoid, scale=-1.0), last, free["k"])
                ring.release(i, b)
                last_t["P"] = op("vector", lambda e: e.tensor_scalar(Pt[:], Pt[:], oml[:, h:h + 1], lb[:, h:h + 1],
                                                                     ALU.mult, ALU.add), a, t_lb)
                last_t["k"] = op("vector", lambda e: e.tensor_scalar(kt_[:], kt_[:], oml[:, h:h + 1], None, ALU.mult),
                                 b, t_lb)
                last_t["Sf"] = op("gpsimd", lambda e: e.memset(Sf[:], 1.0), free["Sf"])
            return fm_tile(A, 8, Hh, Hl, tokh, tokl, post, before=before)

        def head_q(h):
            def post(ps, last, ring, i):
                a = op("scalar", lambda e: e.activation(qt[:], ps[:], ACT.Sigmoid), last, free["q"])
                b = op("vector", lambda e: e.scalar_tensor_tensor(qt[:], qt[:], float(128 ** -0.5), ps[:], ALU.mult,
                                                                  ALU.mult), a)
                ring.release(i, b)
                last_t["q"] = b
            return fm_tile(A, 8, Hh, Hl, tokh, tokl, post)

        def head_g(h):
            def post(ps, last, ring, i):
                a = op("scalar", lambda e: e.activation(sg[:], ps[:], ACT.Sigmoid), last, free["sg"])
                b = op("vector", lambda e: e.tensor_tensor(sg[:], sg[:], ps[:], ALU.mult), a)
                ring.release(i, b)
                last_t["sg"] = b
                last_t["proj"] = last
            return fm_tile(A, 8, Hh, Hl, tokh, tokl, post)

        def scan_levels(h):
            tq, tk, tp, ts = last_t["q"], last_t["k"], last_t["P"], last_t["Sf"]
            k3, q3, a3 = c3(kt_), c3(qt), c3(acc)

            def masked(ps, i, tok, lev, prev):
                toks = []
                for hf in range(2):
                    c = slice(4 * hf, 4 * hf + 4)
                    toks.append(op("vector", lambda e, c=c: e.copy_predicated(
                        a3[:, c, :], masks[:, lev, :][:, None, :].broadcast_to([P, 4, P]), c3(ps)[:, c, :]),
                        tok, t_mask, prev[hf]))
                B.release(i, toks[1])
                return toks

            ps, psw, i = B.get()
            for c in range(8):
                last = mm(c3(ps)[:, c, :], k3[:, c, :], q3[:, c, :], psw, tq, tk, start=True, stop=True, sig=c == 7)
            prev = masked(ps, i, last, 0, [free["acc"], free["acc"]])
            yield None
            m = 1
            lev = 1
            while m < 128:
                v = lambda t, m=m: t[:].rearrange("p (b two m) -> p b two m", two=2, m=m)
                M, mw, mi = mring.get()
                nb = T // (2 * m)
                a = op("vector", lambda e, v=v, M=M: e.tensor_tensor(v(M)[:, :, 1, :], v(qt)[:, :, 1, :],
                                                                     v(Pt)[:, :, 1, :], ALU.mult), mw, tq, tp)
                b = op("gpsimd", lambda e, v=v, M=M: e.tensor_tensor(v(M)[:, :, 0, :], v(kt_)[:, :, 0, :],
                                                                     v(Sf)[:, :, 0, :], ALU.mult), mw, tk, ts)
                ps, psw, i = B.get()
                M3 = c3(M)
                for c in range(8):
                    last = mm(c3(ps)[:, c, :], M3[:, c, :], M3[:, c, :], psw, a, b, start=True, stop=True, sig=c == 7)
                mring.release(mi, last)
                sh = [P, nb, m]
                ts = op("gpsimd", lambda e, v=v, m=m, sh=sh: e.tensor_tensor(
                    v(Sf)[:, :, 0, :], v(Sf)[:, :, 0, :], v(Pt)[:, :, 1, m - 1:m].broadcast_to(sh), ALU.mult), b, tp, ts)
                tp = op("vector", lambda e, v=v, m=m, sh=sh: e.tensor_tensor(
                    v(Pt)[:, :, 1, :], v(Pt)[:, :, 1, :], v(Pt)[:, :, 0, m - 1:m].broadcast_to(sh), ALU.mult), a, ts)
                prev = masked(ps, i, last, lev, prev)
                yield None
                m *= 2
                lev += 1
            last_t["acc"] = prev
            kS, kw, ki = mring.get()
            tks = op("gpsimd", lambda e: e.tensor_tensor(kS[:], kt_[:], Sf[:], ALU.mult), kw, tk, ts)
            free["k"] = [last, tks]
            free["Sf"] = [tks]
            qP, qw, qi = mring.get()
            tqp = op("vector", lambda e: e.tensor_tensor(qP[:], qt[:], Pt[:], ALU.mult), qw, tq, tp)
            ttot = op("vector", lambda e: e.tensor_copy(tot[:], c3(Pt)[:, :, 127]), tp, free["tot"])
            free["q"] = [last, tqp]
            free["P"] = [tqp, ttot, ts]
            last_t["kS"], last_t["qP"], last_t["tot"] = (kS, tks, ki), (qP, tqp, qi), ttot

        def scan_tail(h):
            kS, tks, ki = last_t["kS"]
            qP, tqp, qi = last_t["qP"]
            acct = last_t["acc"]
            tsg = last_t["sg"]
            vo = 128 * (h % 2)
            a3 = c3(acc)
            ps, psw, i = B.get()
            for c in range(7):
                last = op("tensor", lambda e, c=c, ps=ps: e.transpose(c3(ps)[:, c, :], c3(kS)[:, c, :], ident[:]),
                          psw, tks, t_id, sig=c == 6)
            mring.release(ki, last)
            t = op("scalar", lambda e, ps=ps: e.activation(kST[:, 0:896], ps[:, 0:896], ACT.Copy), last, free["kST"])
            B.release(i, t)
            yield None
            yield None
            ps, psw, i = B.get()
            for c in range(7):
                last = mm(c3(ps)[:, c, :], c3(kST)[:, c, :], V[:, c, vo:vo + 128], psw, t, tv[0], tv[1], start=True,
                          stop=True, sig=c == 6)
            free["kST"] = [last]
            s3 = c3(St)
            t = op("vector", lambda e, ps=ps: e.tensor_copy(s3[:, 1, :], c3(ps)[:, 0, :]), last, free["St"])
            for c in range(1, 7):
                t = op("vector", lambda e, c=c, ps=ps: e.scalar_tensor_tensor(
                    s3[:, c + 1, :], s3[:, c, :], tot[:, c:c + 1], c3(ps)[:, c, :], ALU.mult, ALU.add), t,
                    last_t["tot"])
            B.release(i, t)
            free["tot"] = [t]
            yield None
            yield None
            ps, psw, i = B.get()
            for c in range(8):
                mm(c3(ps)[:, c, :], V[:, c, vo:vo + 128], a3[:, c, :], psw, acct, tv[0], tv[1], start=True,
                   stop=(c == 0))
                if c:
                    last = mm(c3(ps)[:, c, :], s3[:, c, :], c3(qP)[:, c, :], tqp, t, stop=True, sig=c == 7)
            mring.release(qi, last)
            free["acc"] = [last]
            free["St"] = [last]
            free["V"] = [last]
            to = op("scalar", lambda e, ps=ps: e.activation(R1[:, h, :], ps[:], ACT.Copy), last, h_done)
            tq2 = op("scalar", lambda e, ps=ps: e.activation(t1[:], ps[:], ACT.Square), last, free["t1"])
            B.release(i, to, tq2)
            yield None
            yield None
            ps, psw, i = B.get()
            for hf in range(2):
                c = slice(512 * hf, 512 * hf + 512)
                last = mm(ps[:, c], ones[:], t1[:, c], psw, tq2, start=True, stop=True, sig=hf == 1)
            free["t1"] = [last]
            t = op("scalar", lambda e, ps=ps: e.activation(t2[:], ps[:], ACT.Ln, bias=eps[:, 0:1], scale=1.0 / 128),
                   last, free["t2"])
            B.release(i, t)
            t = op("scalar", lambda e: e.activation(t2[:], t2[:], ACT.Exp, scale=-0.5), t)
            t = op("vector", lambda e: e.tensor_tensor(t2[:], t2[:], sg[:], ALU.mult), t, tsg)
            free["sg"] = [t]
            t = op("vector", lambda e: e.scalar_tensor_tensor(R1[:, h, :], R1[:, h, :],
                                                              vec[:, V_ON + h:V_ON + h + 1], t2[:], ALU.mult,
                                                              ALU.mult), t, to)
            free["t2"] = [t]
            oT.append(t)
            yield None

        def chain(*gs):
            for g in gs:
                yield from g

        drain(head_f(0))
        tail = None
        for h in range(8):
            Q.mark("head")
            run_both(head_q(h), tail, 1)
            levels = scan_levels(h)
            more = [head_g(h)]
            if h % 2 == 0:
                more.append(tm_pair(A, 8, Hh, Hl, tokh, tokl, v_post))
            if h < 7:
                more.append(head_f(h + 1, levels))
            run_both(chain(*more), levels, 2 if h % 2 else 4)
            tail = scan_tail(h)
        drain(tail)
        h_read = last_t["proj"]

        Q.mark("wout")
        tokh, tokl = [], []
        for k in range(8):
            th, tl = split(R1[:, k, :], Hh[:, k, :], Hl[:, k, :], oT[k], [h_read], "gpsimd" if k % 2 else "vector")
            tokh.append(th)
            tokl.append(tl)
        t_x = [dma(R1[:, k, :], xT[k], f"x{k}", tokh[k], tokl[k]) for k in range(8)]
        allps.free = [A.free[0], A.free[1], B.free[0], B.free[1]]

        def add_tile(m, st, scale=None, tok=None, final=True):
            def post(ps, last, ring, i):
                if scale is None:
                    t = op("vector", lambda e: e.tensor_tensor(R1[:, m, :], ps[:], R1[:, m, :], ALU.add), last, tok[m])
                else:
                    t = op("vector", lambda e: e.scalar_tensor_tensor(R1[:, m, :], ps[:], scale(m), R1[:, m, :],
                                                                      ALU.mult, ALU.add), last, tok[m])
                ring.release(i, t)
                tok[m] = t
                if final and st is not None:
                    st.add(R1[:, m, :], t)
            return post

        tx = list(t_x)
        st = Stats(t1, [kST, t3], [free["t1"], free["kST"], free["t3"], free["t2"]])
        for m in range(8):
            drain(fm_tile(allps, 8, Hh, Hl, tokh, tokl, add_tile(m, st, tok=tx)))
        h_read = allps_last = Q.n["tensor"]
        h_read = ("tensor", h_read)

        def mlp(tx, tokh, tokl, waits, st_of, scale=None, done=None):
            ah = at("ah" + ("2" if scale else ""), [P, 5, T], R, SA)
            al = at("al" + ("2" if scale else ""), [P, 5, T], R, SA + 5 * 4096)
            nm = "m2" if scale else "m1"
            tr = Ring([sa(nm + f"r{i}", 10 + i) for i in range(3)])
            tr.free = [list(waits) for _ in tr.free]

            def hook():
                if done.get("hook"):
                    next(done["hook"], None)
            afree = [list(waits) for _ in range(5)]
            at_ = {}

            def s1(t):
                sl = t % 5

                def post(ps, last, ring, i):
                    rl, w1, i1 = tr.get()
                    a = op("scalar", lambda e: e.activation(rl[:], ps[:], ACT.Relu), last, w1)
                    ring.release(i, a)
                    b = op("vector", lambda e: e.tensor_tensor(rl[:], rl[:], rl[:], ALU.mult), a)
                    th, tl = split(rl[:], ah[:, sl, :], al[:, sl, :], b, afree[sl])
                    tr.release(i1, th, tl)
                    at_[t] = (th, tl)
                    hook()
                drain(fm_tile(allps, 8, Hh, Hl, tokh, tokl, post))

            def s2(c):
                for j in range(4):
                    w = W.get(4)
                    for mm_ in range(2):
                        m = 2 * j + mm_
                        ps, psw, i = allps.get()
                        for part in range(2):
                            for k in range(4):
                                sl = (4 * c + k) % 5
                                th, tl = at_[4 * c + k]
                                for hf in range(2):
                                    cs = slice(512 * hf, 512 * hf + 512)
                                    ws = slice(128 * mm_, 128 * mm_ + 128)
                                    if part == 0:
                                        mm(ps[:, cs], w[0][:, k, ws], ah[:, sl, cs], psw, w[2], th, start=(k == 0))
                                        mm(ps[:, cs], w[1][:, k, ws], ah[:, sl, cs], w[3])
                                    else:
                                        last = mm(ps[:, cs], w[0][:, k, ws], al[:, sl, cs], tl, stop=(k == 3),
                                                  sig=(k == 3 and hf == 1))
                        if mm_ == 1:
                            W.release(w[4], last)
                        if m == 7:
                            for k in range(4):
                                afree[(4 * c + k) % 5] = [last]
                        if c == 7 and m == 0:
                            if done.get("hook"):
                                drain(done["hook"])
                            done["st"] = st_of()
                        add_tile(m, done.get("st"), scale, tx, final=(c == 7))(ps, last, allps, i)
                        if c < 7:
                            hook()
                        if c == 7 and done.get("post"):
                            done["post"](m)

            Q.mark("mlp")
            for t in range(4):
                s1(t)
            for c in range(8):
                if c < 7:
                    s1(4 * c + 4)
                s2(c)
                if c < 7:
                    for t in range(4 * c + 5, 4 * c + 8):
                        s1(t)
            done["relu"] = [tr.free]

        if stage >= 2:
            Q.mark("norm2")
            rt = st.finish(allps, t2, st.sqfree[0])
            tokh, tokl = apply_norm(lambda k: R1[:, k, :], tx, col(V_MLP), t2, rt, HT, Hh, Hl, [h_read])
            tn = [tokl, tokh, st.sqfree]
            done = {}
            n1, n2, n3 = sa("n1", 14), sa("n2", 15), sa("n3", 13)
            mod_t = []

            def modulations():
                raws = Ring([n3, n1])
                raws.free = [[tn, h_read]] * 2
                afree = [tn, h_read]
                b3 = vec[:, V_BADA:V_BADA + 48]
                for part in range(8):
                    w, c0 = (0, part) if part < 6 else (1, part - 6)
                    t = afree
                    for k in range(8):
                        raw, rw, ri = raws.get()
                        d = dma(raw[:], w_ada[128 * k:128 * k + 128, 1024 * c0:1024 * c0 + 1024], f"a{ri}", rw)
                        s_ = csil[:, k, w:w + 1]
                        if k == 0:
                            t = op("vector", lambda e, raw=raw, s_=s_: e.tensor_scalar(n2[:], raw[:], s_, None,
                                                                                      ALU.mult), d, t, t_csil)
                        else:
                            t = op("vector", lambda e, raw=raw, s_=s_: e.scalar_tensor_tensor(
                                n2[:], raw[:], s_, n2[:], ALU.mult, ALU.add), d, t)
                        raws.release(ri, t)
                        yield None
                    yield None
                    ps, psw, i = allps.get()
                    for j in range(8):
                        last = mm(ps[:, j:j + 1], n2[:, 128 * j:128 * j + 128], ones[:, 0:1], psw, t, start=True,
                                  stop=True, sig=(j == 7))
                    afree = [last]
                    m = op("vector", lambda e, ps=ps, c0=c0, w=w: e.tensor_tensor(
                        mods[:, 8 * c0:8 * c0 + 8, w], ps[:, 0:8], b3[:, 8 * c0:8 * c0 + 8], ALU.add), last)
                    allps.release(i, m)
                    mod_t.append(m)
                done["ada"] = [afree, raws.free]
                yield None

            done["hook"] = modulations()
            mlp(tx, tokh, tokl, tn, lambda: Stats(n1, [n2], [tn, done["ada"]], acc2=n3, gain=col(V_FINAL)), done=done)
            h_read = ("tensor", Q.n["tensor"])

        if stage >= 3:
            Q.mark("final")
            st = done["st"]
            rs, rs2 = sa("rs", 12), sa("rs2", 11)
            rt = st.finish(allps, rs, done["relu"])
            rt2 = st.second(allps, rs, rt, rs2, done["relu"])
            for k in range(8):
                tx[k] = op("vector", lambda e, k=k: e.scalar_tensor_tensor(
                    R1[:, k, :], R1[:, k, :], vec[:, V_FINAL + k:V_FINAL + k + 1], rs[:], ALU.mult, ALU.mult),
                    rt, tx[k])
        if stage > 3:
            pe_now = lambda: ("tensor", Q.n["tensor"])
            t_mod = mod_t
            ada_done = mod_t
            af = []
            for j, (g0, m0, w0) in enumerate(((V_N1, 8, 0), (V_N1, 8, 1), (V_N2, 32, 0))):
                t_A = op("vector", lambda e, j=j, g0=g0, m0=m0, w0=w0: e.scalar_tensor_tensor(
                    modA[:, j, :], mods[:, m0:m0 + 8, w0], 1.0, vec[:, g0:g0 + 8], ALU.add, ALU.mult), t_mod)
            gA = lambda j: (lambda k: modA[:, j, k:k + 1])
            mc = lambda m0, w0=0: (lambda k: mods[:, m0 + k, w0:w0 + 1])

            Q.mark("n2norm")
            t_sp = [dma(xs_d[k], R1[:, k, :], f"sp{k}", tx[k]) for k in range(8)]
            tokh, tokl = apply_norm(lambda k: R1[:, k, :], tx, gA(0), rs2, rt2, HT, Hh, Hl, [h_read, t_A],
                                    shift=mc(0))
            x_free = [tokh, tokl]

            U = [[at(f"U{a}{b}", [P, 4, 512], R, R1A + 8192 * (2 * a + b)) for b in range(2)] for a in range(2)]
            Yh, Yl = at("Yh", [P, 4, T], R, SA), at("Yl", [P, 4, T], R, SA + 16384)
            Z = [[[sa(f"Z{z}{a}{b}", (8, 12)[z] + 2 * a + b, R) for b in range(2)] for a in range(2)]
                 for z in range(2)]
            f1, f2, f3 = sa("f1", 12), sa("f2", 13), sa("f3", 14)
            CD = [[at(f"CD{a}{b}", [P, 128], R, spare + 512 * (2 * a + b))[:] for b in range(2)] for a in range(2)]
            cdr = at("cdr", [P, 2, 128], F, SA + 8 * 4096)
            n_done = [tokl, tokh, rt2, st.sqfree]
            d = dma(cdr[:], cd_d, "c3", n_done, ada_done)
            cdt = []
            for a in range(2):
                cdt += split(cdr[:, a, :], CD[a][0], CD[a][1], d, n_done)
            tU = []
            ufree = {"f1": n_done, "f2": n_done, "f3": n_done}
            sp_done = [t_sp, x_free]

            def u_post(c0):
                held = {}

                def post(s, ps, last, ring, i):
                    if s == 0:
                        held[0] = (ps, last, ring, i)
                        return
                    ps0, l0, _, i0 = held[0]
                    a = op("scalar", lambda e: e.activation(f1[:], ps0[:], ACT.Copy), l0, ufree["f1"])
                    ring.release(i0, a)
                    b = op("vector", lambda e: e.tensor_tensor(f2[:], f1[:], ps[:], ALU.add), a, last, ufree["f2"])
                    c = op("vector", lambda e: e.tensor_tensor(f3[:], f1[:], ps[:], ALU.subtract), a, last,
                           ufree["f3"])
                    ring.release(i, c)
                    ufree["f1"] = [c, b]
                    for par, (f, t, nm) in enumerate(((f2, b, "f2"), (f3, c, "f3"))):
                        f4 = f[:].rearrange("p (t c) -> p t c", c=256)
                        th, tl = split(f4, U[par][0][:, :, c0:c0 + 256], U[par][1][:, :, c0:c0 + 256], t, sp_done)
                        ufree[nm] = [th, tl]
                        tU.extend([th, tl])
                return post

            Q.mark("U")
            for c0 in (0, 256):
                drain(tm_pair(allps, 8, Hh, Hl, tokh, tokl, u_post(c0)))

            zs = Ring([0, 1])
            tY = []
            y_wait = [ada_done, af, cdt]
            zs.free[1] = [ufree]
            zs.free[0] = [n_done]

            def dft_step(par, j):
                tz = []
                zi, zw, _ = zs.get()
                for cs in range(2):
                    w = W.get(4)
                    ps, psw, i = allps.get()
                    for g in range(4):
                        o = ps[:, 256 * g:256 * g + 256]
                        gs = slice(128 * g, 128 * g + 128)
                        for k in range(4):
                            mm(o, U[par][0][:, k, gs], w[0][:, k, :], psw, w[2], tU, start=(k == 0))
                            mm(o, U[par][0][:, k, gs], w[1][:, k, :], w[3])
                            last = mm(o, U[par][1][:, k, gs], w[0][:, k, :], stop=(k == 3),
                                      sig=(k == 3 and g == 3))
                    W.release(w[4], last)
                    th, tl = split(ps[:], Z[zi][cs][0][:], Z[zi][cs][1][:], last, [zw, y_wait])
                    allps.release(i, th, tl)
                    tz.append((th, tl))
                return zi, tz

            def chan_step(par, j, ztz):
                zi, tz = ztz
                Zz = Z[zi]
                ps, psw, i = allps.get()
                for g in range(4):
                    o = ps[:, 256 * g:256 * g + 256]
                    gs = slice(256 * g, 256 * g + 256)
                    for cs in range(2):
                        mm(o, CD[cs][0], Zz[cs][0][:, gs], psw, tz[cs][0], cdt, start=(cs == 0))
                        mm(o, CD[cs][1], Zz[cs][0][:, gs])
                        last = mm(o, CD[cs][0], Zz[cs][1][:, gs], tz[cs][1], stop=(cs == 1), sig=(cs == 1 and g == 3))
                zs.release(zi, last)
                v = lambda t: t[:].rearrange("p g (n two) -> p g n two", two=2)[:, :, 256 * j:256 * j + 256, par]
                th, tl = split(ps[:].rearrange("p (g n) -> p g n", g=4), v(Yh), v(Yl), last, [y_wait])
                allps.release(i, th, tl)
                tY.extend([th, tl])

            Q.mark("dft")
            for par in range(2):
                for j in range(2):
                    tz = dft_step(par, j)
                    flush()
                    pending.append(lambda par=par, j=j, tz=tz: chan_step(par, j, tz))
            flush()
            u_done = pe_now()

            cx = at("cx", [P, 8, 256], F, R1A)
            cacc, csq, crs = (at(n, [P, 256], F, R1A + 8192 + 1024 * i) for i, n in enumerate(("cacc", "csq", "crs")))
            hcT = at("hcT", [P, 8, 256], F, SA + 10 * 4096)
            hch, hcl = at("hch", [P, 8, 256], R, SA + 8 * 4096), at("hcl", [P, 8, 256], R, SA + 10 * 4096)
            gnq = at("gnq", [P, 128], F, R1A + 24576 - 512)
            tcx = dma(cx[:], ctxT.rearrange("k p t -> p k t"), "c3", u_done, tU)
            t_g = dma(gnq[:], gains, "c4", u_done, tU)
            stc = Stats(cacc, [csq], [u_done, tU], n=256)
            for k in range(8):
                stc.add(cx[:, k, :], tcx)
            mfr = Ring([sa("mf0", 12), sa("mf1", 13)])
            sgr = Ring([sa("sgr0", 14), sa("sgr1", 15)])
            for r in (mfr, sgr):
                r.free = [[u_done, tU, cdt] for _ in r.free]
            Q.mark("gate1")
            mf_st = {}

            def gate(sigs):
                def post(ps, last, ring, i):
                    g, w, gi = sgr.get()
                    a = op("scalar", lambda e: e.activation(g[:], ps[:], ACT.Sigmoid), last, w)
                    ring.release(i, a)
                    sigs.append((g, a, gi))
                return post

            for m in range(0, 8, 2):
                sigs = []
                for x in range(2):
                    drain(fm_tile(allps, 8, Hh, Hl, tokh, tokl, gate(sigs)))
                w = W.get(4)
                for x in range(2):
                    def post(ps, last, ring, i, x=x):
                        g, a, gi = sigs[x]
                        o, ow, oi = mfr.get()
                        b = op("vector", lambda e: e.tensor_tensor(o[:], g[:], ps[:], ALU.mult), a, last, ow)
                        ring.release(i, b)
                        sgr.release(gi, b)
                        mf_st[m + x] = dma(mf_d[m + x], o[:], f"mf{(m + x) % 2}", b)
                        mfr.release(oi, mf_st[m + x])
                    drain(fm_tile(allps, 4, Yh, Yl, [tY] * 4, [tY] * 4, post, w=w, m0=128 * x, release=(x == 1)))
                if m == 0:
                    rtc = stc.finish(allps, crs, [u_done, tU])
                    tch, tcl = apply_norm(lambda k: cx[:, k, :], [tcx] * 8, gA(1), crs, rtc, hcT, hch, hcl,
                                             [u_done, tU], shift=mc(0, 1), n=256)
            y_read = pe_now()
            mf_done = [mf_st[6], mf_st[7]]

            qT = at("qT", [P, 4, T], F, R1A)
            kT = at("kT", [P, 2, T], F, SA + 12 * 4096)
            Vx = at("Vx", [P, 8, 256], F, R1A + 16384)
            kcT = at("kcT", [P, 4, 256], F, R1A + 24576)
            vc = at("vc", [P, 2, 512], F, R1A + 28672)
            rope = at("rope", [P, 2, 8, 64], F, SA)
            a1, a2, a3_ = (sa(n, 1 + i) for i, n in enumerate(("a1", "a2", "a3")))
            ya = at("ya", [P, 4, T], F, SA + 8 * 4096)
            aA = SA + 4 * 4096
            be = [at(f"be{i}", [P, 14, 64], F, aA + 3584 * i) for i in range(2)]
            bm = [at(f"bm{i}", [P, 9, 64], F, aA + 7168 + 2304 * i) for i in range(2)]
            pr = Ring([at("pr0", [P, 832], F, spare), at("pr1", [P, 832], F, aA + 11776),
                       at("pr2", [P, 832], F, SA + 3 * 4096)])
            ptr = Ring([at(f"pt{i}", [P, 896], F, SA + 14 * 4096 + 3584 * i) for i in range(2)])
            pr.free = [[u_done, y_read]] * 3
            ptr.free = [[u_done, y_read, mfr.free, sgr.free]] * 2
            ctx_done = [tch, tcl, rtc, stc.tok, stc.sqfree]
            t_gq = op("vector", lambda e: e.tensor_scalar(gq[:, 0:64], gnq[:, 0:64], 0.125, None, ALU.mult), t_g)
            t_gk = op("vector", lambda e: e.tensor_copy(gq[:, 64:128], gnq[:, 64:128]), t_g)
            t_qz = [op("gpsimd", lambda e: e.memset(qT[64:128, 0:4:2, :], 0.0), ctx_done, u_done),
                    op("gpsimd", lambda e: e.memset(qT[0:64, 1:4:2, :], 0.0), ctx_done, u_done)]
            t_rope = dma(rope[:], rope_d.rearrange("p two t c -> p two t c"), "c5", y_read)
            fre = {n: [y_read] for n in ("a1", "a2", "a3")}

            def heads_post(nt, which, dst, tile0, roped, dfree):
                n = nt * 256

                def post(s, ps, last, ring, i):
                    v3 = lambda t: t[:, 0:n].rearrange("p (x c) -> p x c", c=64)
                    b3 = [P, n // 64, 64]
                    ss = small[:, 0:n // 64]
                    a = op("scalar", lambda e: e.activation(a1[:, 0:n], ps[:, 0:n], ACT.Copy), last, fre["a1"])
                    b = op("scalar", lambda e: e.activation(a2[:, 0:n], ps[:, 0:n], ACT.Square), last, fre["a2"])
                    ring.release(i, b)
                    c = op("vector", lambda e: e.tensor_reduce(ss, v3(a2), AX, ALU.add), b, fre.get("ss"))
                    c = op("scalar", lambda e: e.activation(ss, ss, ACT.Ln, bias=eps[:, 0:1], scale=1.0 / 64), c)
                    c = op("scalar", lambda e: e.activation(ss, ss, ACT.Exp, scale=-0.5), c)
                    c = op("vector", lambda e: e.tensor_tensor(v3(a1), v3(a1), ss[:, :, None].broadcast_to(b3),
                                                               ALU.mult), a, c)
                    fre["ss"] = [c]
                    gcol = gq[:, 64 * which:64 * which + 64][:, None, :].broadcast_to(b3)
                    c = op("vector", lambda e: e.tensor_tensor(v3(a1), v3(a1), gcol, ALU.mult), c, t_gq, t_gk)
                    src = a1
                    if roped:
                        tl0 = 4 * s
                        v4 = lambda t: t[:, 0:n].rearrange("p (t h c) -> p t h c", t=4, c=64)
                        tab = lambda j: rope[:, j, tl0:tl0 + 4, :][:, :, None, :].broadcast_to([P, 4, 4, 64])
                        d = op("vector", lambda e: e.tensor_tensor(v4(a2), v4(a1), tab(0), ALU.mult), c, t_rope)
                        for ax in range(2):
                            for hf in range(2):
                                o = slice(32 * ax + 16 * hf, 32 * ax + 16 * hf + 16)
                                w_ = slice(32 * ax + 16 - 16 * hf, 32 * ax + 32 - 16 * hf)
                                g = op("vector", lambda e, o=o, w_=w_: e.tensor_tensor(
                                    v4(a3_)[:, :, :, o], v4(a1)[:, :, :, w_], tab(1)[:, :, :, o], ALU.mult), c,
                                    t_rope, fre["a3"])
                        c = op("vector", lambda e: e.tensor_tensor(a2[:, 0:n], a2[:, 0:n], a3_[:, 0:n], ALU.add),
                               g, d)
                        fre["a1"] = [g, d]
                        fre["a3"] = [c]
                        src = a2
                    def later():
                        ps2, pw, i2 = ring.get()
                        for cb in range(2):
                            for t in range(nt):
                                l2 = op("tensor", lambda e, cb=cb, t=t: e.transpose(
                                    ps2[:, 128 * (cb * nt + t):128 * (cb * nt + t) + 128],
                                    src[:, 256 * t + 128 * cb:256 * t + 128 * cb + 128], ident[:]), pw, c,
                                    sig=(cb == 1 and t == nt - 1))
                        if roped:
                            fre["a2"] = [l2]
                        else:
                            fre["a1"] = [l2]
                            fre["a2"] = [c]
                        tc = slice(512 * s, 512 * s + 128 * nt)
                        p3 = ps2[:, 0:256 * nt].rearrange("p (cb t) -> p cb t", cb=2)
                        if which == 0:
                            td = [op("scalar", lambda e: e.activation(dst[0:64, 0:4:2, tc], p3[0:64], ACT.Copy), l2,
                                     dfree),
                                  op("vector", lambda e: e.tensor_copy(dst[64:128, 1:4:2, tc], p3[64:128]), l2,
                                     dfree)]
                        else:
                            td = [op("scalar", lambda e: e.activation(dst[:, tile0:tile0 + 2, tc], p3, ACT.Copy), l2,
                                     dfree)]
                        ring.release(i2, *td)
                        att.extend(td)
                    pending.append(later)
                return post

            att = []
            Q.mark("ctxproj")
            for j in range(2):
                drain(tm_pair(allps, 2, hch, hcl, tch, tcl, heads_post(2, 1, kcT, 2 * j, False, ctx_done)))
            for j in range(2):
                def vpost(s, ps, last, ring, i, j=j):
                    a = op("vector", lambda e: e.tensor_copy(vc[:, :, 256 * j:256 * j + 256],
                                                             ps[:, 0:512].rearrange("p (t c) -> p t c", t=2)), last,
                           ctx_done)
                    ring.release(i, a)
                    att.append(a)
                drain(tm_pair(allps, 2, hch, hcl, tch, tcl, vpost))
            hc_read = pe_now()
            ctx_att = list(att)

            bias_free = [[y_read], [y_read]]
            bias_t = {}

            def load_bias(h):
                i = h % 2
                bias_t[h] = [dma(be[i][:], biasE[h], f"be{i}", bias_free[i]),
                             dma(bm[i][:], biasM[h], f"bm{i}", bias_free[i])]

            tya = []
            attf = {"qT": [ctx_done, t_gq, t_gk, u_done, y_read, mfr.free, sgr.free], "O": []}
            Q.mark("dummy")
            for half in range(2):
                Q.mark("qkv")
                att = []
                drain(tm_pair(allps, 8, Hh, Hl, tokh, tokl, heads_post(4, 0, qT, 0, True, attf["qT"])))
                drain(tm_pair(allps, 8, Hh, Hl, tokh, tokl, heads_post(4, 1, kT, 0, True, attf["qT"])))

                def vpost(s, ps, last, ring, i):
                    a = op("vector", lambda e: e.tensor_copy(Vx[:, 4 * s:4 * s + 4, :],
                                                             ps[:].rearrange("p (t c) -> p t c", c=256)), last,
                           attf["qT"])
                    ring.release(i, a)
                    att.append(a)
                if half == 0:
                    load_bias(0)
                    load_bias(1)
                drain(tm_pair(allps, 8, Hh, Hl, tokh, tokl, vpost))
                flush()
                att_t = [list(att), ctx_att, t_qz]
                pr.free[2] = [pr.free[2], fre["a3"]]
                SR = Ring(psum[0:2])
                SR.free = [list(allps.free[0]), list(allps.free[1])]
                ptfree = list(allps.free[2])
                OR = Ring([psum[3][:, 0:512], psum[3][:, 512:1024]])
                OR.free = [list(allps.free[3]) for _ in range(2)]
                its = [(hh, j) for hh in range(4) for j in (0, 1, 6, 7, 2, 3, 4, 5)]
                state = {}

                def qk(n):
                    hh, j = its[n]
                    h = 4 * half + hh
                    cb = hh // 2
                    mid_ = 2 <= j <= 5
                    rs_ = 2 * j - 4 if mid_ else (0 if j < 2 else 8)
                    ps, psw, i = SR.get()
                    pt, pw, pi = pr.get()
                    z = 32 + 8 * (n % 4)
                    L = 576 if mid_ else 512
                    s = state[n] = dict(pt=pt, pi=pi, L=L, rs=rs_, z=z)

                    def scores():
                        q = qT[:, hh, 128 * j:128 * j + 128]
                        k0, na = 64 * rs_, 320 if mid_ else 256
                        mm(ps[:, 512 - na:512], q, kT[:, cb, k0:k0 + na], psw, att_t, start=True, stop=True)
                        mm(ps[:, 512:768], q, kT[:, cb, k0 + na:k0 + na + 256], start=True, stop=True)
                        last = mm(ps[:, 768:1024], q, kcT[:, 2 * half + cb, :], start=True, stop=True, sig=True)
                        s["qk"] = last

                    def softmax():
                        last = s["qk"]
                        b = h % 2
                        if mid_:
                            bias = bm[b][:].rearrange("p a b -> p (a b)")
                        else:
                            i0 = rs_ - 2 * j + 6
                            bias = be[b][:, i0:i0 + 8, :].rearrange("p a b -> p (a b)")
                        col_ = lambda c: small[:, z + c:z + c + 1]
                        o4 = state.get(("s", n - 4))
                        a = op("vector", lambda e: e.tensor_reduce(col_(0), ps[:, 768:1024], AX, ALU.max), last, o4)
                        a = op("vector", lambda e: e.tensor_tensor_reduce(pt[:, 0:L], ps[:, 768 - L:768], bias, 1.0, col_(0),
                                                                          ALU.add, ALU.max, col_(1)), a, pw, bias_t[h])
                        if j == 5:
                            bias_free[b] = [a]
                            if h + 2 < 8:
                                load_bias(h + 2)
                        a = op("vector", lambda e: e.tensor_scalar(col_(2), col_(1), -1.0, None, ALU.mult), a)
                        x2 = op("scalar", lambda e: e.activation(pt[:, L:L + 256], ps[:, 768:1024], ACT.Exp, bias=col_(2),
                                                                 accum_out=col_(4)), a, pw)
                        SR.release(i, x2)
                        x1 = op("scalar", lambda e: e.activation(pt[:, 0:L], pt[:, 0:L], ACT.Exp, bias=col_(2),
                                                                 accum_out=col_(3)), a)
                        s["x"] = [x1, x2]

                    return scores, softmax

                def fin(n):
                    s = state[n]
                    pt, L, z = s["pt"], s["L"], s["z"]
                    col_ = lambda c: small[:, z + c:z + c + 1]
                    a = op("vector", lambda e: e.tensor_tensor(col_(5), col_(3), col_(4), ALU.add), s["x"])
                    a = op("vector", lambda e: e.reciprocal(col_(6), col_(5)), a)
                    a = op("vector", lambda e: e.tensor_scalar(pt[:, 0:L + 256], pt[:, 0:L + 256], col_(6), None,
                                                               ALU.mult), a)
                    state[("s", n)] = a
                    s["a"] = a

                def tr(n):
                    s = state[n]
                    hh, j = its[n]
                    ps = psum[2]
                    col_ = lambda c: small[:, s["z"] + c:s["z"] + c + 1]
                    pt, L = s["pt"], s["L"]
                    half9 = L == 576
                    a = s["a"]
                    for b in range(4):
                        last = op("tensor", lambda e, b=b: e.transpose(ps[:, 128 * b:128 * b + 128],
                                                                       pt[:, 128 * b:128 * b + 128], ident[:]),
                                  ptstate["free"], a, sig=(b == 3))
                    first = last
                    for b in range(2):
                        last = op("tensor", lambda e, b=b: e.transpose(ps[:, 512 + 128 * b:640 + 128 * b],
                                                                       pt[:, L + 128 * b:L + 128 * b + 128], ident[:]),
                                  sig=(b == 1 and not half9))
                    if half9:
                        last = op("tensor", lambda e: e.transpose(ps[0:64, 768:896], pt[:, 512:576], ident[:]))
                    pr.release(s["pi"], last)
                    s["tr"] = first, last

                def evac(n):
                    s = state[n]
                    ps = psum[2]
                    half9 = s["L"] == 576
                    first, last = s["tr"]
                    o, ow, oi = ptr.get()
                    c1 = op("vector", lambda e: e.tensor_copy(o[:, 0:512], ps[:, 0:512]), first, ow)
                    c2 = op("scalar", lambda e: e.activation(o[:, 512:768], ps[:, 512:768], ACT.Copy), last, ow)
                    if half9:
                        c2 = op("scalar", lambda e: e.activation(o[0:64, 768:896], ps[0:64, 768:896], ACT.Copy), last)
                    ptstate["free"] = [c1, c2]
                    s["o"], s["oi"], s["c"] = o, oi, [c1, c2]

                def pv(n):
                    s = state.pop(n)
                    hh, j = its[n]
                    h = 4 * half + hh
                    pb = 64 * (hh % 2)
                    ob, ow, oi = OR.get()
                    O = ob[pb:pb + 64, 0:128]
                    t0 = s["rs"] // 2
                    o = s["o"]
                    half9 = s["L"] == 576
                    for b in range(4):
                        mm(O, Vx[:, t0 + b, 64 * hh:64 * hh + 64], o[:, 128 * b:128 * b + 128], ow, s["c"],
                           start=(b == 0))
                    for b in range(2):
                        last = mm(O, vc[:, b, 64 * h:64 * h + 64], o[:, 512 + 128 * b:640 + 128 * b],
                                  stop=(b == 1 and not half9), sig=(b == 1 and not half9))
                    if half9:
                        last = mm(O, Vx[0:64, t0 + 4, 64 * hh:64 * hh + 64], o[0:64, 768:896], stop=True, sig=True)
                    ptr.release(s["oi"], last)
                    dst = ya[pb:pb + 64, 2 * half + hh // 2, 128 * j:128 * j + 128]
                    ty = op("scalar", lambda e: e.activation(dst, O, ACT.Copy), last, hc_read)
                    OR.release(oi, ty)
                    tya.append(ty)

                ptstate = {"free": ptfree}
                Q.mark("attn")
                N = len(its)
                for n in range(N + 3):
                    if 0 <= n - 1 < N:
                        fin(n - 1)
                    if n < N:
                        scores, softmax = qk(n)
                        scores()
                    if 0 <= n - 2 < N:
                        tr(n - 2)
                    if n < N:
                        softmax()
                    if 0 <= n - 2 < N:
                        evac(n - 2)
                    if n >= 3:
                        pv(n - 3)
                fre["a3"] = [fre["a3"], pe_now()]
                attf["qT"] = [pe_now()]
                allps.free = [SR.free[0], SR.free[1], ptstate["free"], [OR.free]]

            a_read = pe_now()
            t_mf = [dma(R1[:, m, :], mf_d[m], f"x{m}", a_read, mf_done, att_t) for m in range(8)]
            Q.mark("gate2")
            yah, yal = at("yah", [P, 4, T], R, SA), at("yal", [P, 4, T], R, SA + 16384)
            sgr2 = Ring([sa("sg20", 12), sa("sg21", 13)])
            mr2 = Ring([sa("mr20", 14), sa("mr21", 15)])
            for r in (sgr2, mr2):
                r.free = [[a_read, ptr.free]] * 2
            tyh, tyl = [], []
            for k in range(4):
                th, tl = split(ya[:, k, :], yah[:, k, :], yal[:, k, :], tya, [a_read, bias_free, fre["ss"], pr.free])
                tyh.append(th)
                tyl.append(tl)
            sgr = sgr2
            tm_ = [None] * 8
            for m in range(0, 8, 2):
                sigs = []
                for x in range(2):
                    def gpost(ps, last, ring, i):
                        g, w, gi = sgr2.get()
                        a = op("scalar", lambda e: e.activation(g[:], ps[:], ACT.Sigmoid), last, w)
                        ring.release(i, a)
                        sigs.append((g, a, gi))
                    drain(fm_tile(allps, 8, Hh, Hl, tokh, tokl, gpost))
                w = W.get(4)
                for x in range(2):
                    def post(ps, last, ring, i, mx=m + x, x=x):
                        g, a, gi = sigs[x]
                        o, ow, oi = mr2.get()
                        b = op("vector", lambda e: e.tensor_tensor(o[:], g[:], ps[:], ALU.mult), a, last, ow)
                        ring.release(i, b)
                        sgr2.release(gi, b)
                        b = op("vector", lambda e: e.tensor_tensor(R1[:, mx, :], R1[:, mx, :], o[:], ALU.add), b,
                               t_mf[mx])
                        mr2.release(oi, b)
                        tm_[mx] = b
                    drain(fm_tile(allps, 4, yah, yal, tyh, tyl, post, w=w, m0=128 * x, release=(x == 1)))
            h_read = pe_now()
            tokh, tokl = [], []
            for k in range(8):
                th, tl = split(R1[:, k, :], Hh[:, k, :], Hl[:, k, :], tm_[k], [h_read],
                               "gpsimd" if k % 2 else "vector")
                tokh.append(th)
                tokl.append(tl)
            tx = [dma(R1[:, k, :], xs_d[k], f"x{k}", tokh[k], tokl[k], t_sp[k]) for k in range(8)]
            b1, b2, b3_, b4 = sa("b1", 12), sa("b2", 13), sa("b3", 14), sa("b4", 15)
            bw = [sgr2.free, mr2.free]
            Q.mark("wo2")
            st = Stats(b1, [b2, b3_], bw)
            for m in range(8):
                drain(fm_tile(allps, 8, Hh, Hl, tokh, tokl, add_tile(m, st, mc(16), tok=tx)))
            h_read = pe_now()
            Q.mark("norm2b")
            rt = st.finish(allps, b4, bw)
            tokh, tokl = apply_norm(lambda k: R1[:, k, :], tx, gA(2), b4, rt, HT, Hh, Hl, [h_read, t_A],
                                    shift=mc(24))
            tn = [tokl, tokh, rt, st.tok, st.sqfree, h_read]
            done = {"post": lambda m: outs.append(dma(out[m], R1[:, m, :], f"x{m}", tx[m]))}
            outs = []
            mlp(tx, tokh, tokl, tn, lambda: None, scale=mc(40), done=done)
        if stage <= 3:
            for k in range(8):
                dma(out[k], R1[:, k, :], f"x{k}", tx[k])
        fin = [(f"x{k}", Q.n[f"x{k}"]) for k in range(8)]
        Q.q["sync"].append((lambda e: None, (fin,), None, 0))

        block = ctx.enter_context(nc.Block())
        for name in ENGINES:
            on = {"tensor": block.tensor, "vector": block.vector, "scalar": block.scalar, "gpsimd": block.gpsimd,
                  "sync": block.sync}[name]
            on(lambda e, name=name: Q.emit(name, e))
        return Q.marks


def layout(inputs):
    c = np.ascontiguousarray
    f = np.float32
    i = inputs

    def fm(a):
        return c(np.asarray(a).T.reshape(8, 128, -1))

    def pk(a):
        return np.asarray(a).reshape(-1, 128).T

    vecs = c(np.concatenate([pk(i[n]) for n in (
        "norm_mix", "norm_mlp", "norm_final", "hgrn_lower_bound", "hgrn_out_norm", "norm1_g_2", "norm2_g_2", "c_2",
        "c_ctx_2", "b_ada_2")], axis=1))
    gains = c(np.broadcast_to(np.concatenate([i["q_norm_g_2"][0], i["k_norm_g_2"][0]]), (128, 128)))

    rpb = np.asarray(i["rpb_2"])[0]
    cq, ck = np.arange(64)[:, None], np.arange(64)[None, :]
    start = np.clip(cq - 8, 0, 48)
    inside = (ck >= start) & (ck < start + 16)
    idx = np.clip(ck - cq + 15, 0, 30)
    toe = np.where(inside[None, None], rpb[:, :, idx], f(NEG)).transpose(0, 2, 1, 3)
    edge = np.full((8, 128, 14, 64), NEG, f)
    edge[:, :64] = toe[:, :, 1:15]
    edge[:, 64:] = toe[:, :, 0:14]
    mid = np.full((8, 128, 9, 64), NEG, f)
    mid[:, :64, 0:8] = toe[:, :, 3:11]
    mid[:, 64:, 1:9] = toe[:, :, 3:11]

    s, t = np.arange(128)[:, None], np.arange(128)[None, :]
    masks = [s == t]
    for lev in range(7):
        m = 1 << lev
        masks.append((s // (2 * m) == t // (2 * m)) & (s // m % 2 == 0) & (t // m % 2 == 1))
    masks = c(np.stack(masks, 1).astype(f))

    tok = np.arange(1024)
    inv = f(10000.0) ** (-np.arange(0, 32, 2, dtype=f) / f(32))
    ang = np.stack([(tok // 64).astype(f)[:, None] * inv, (tok % 64).astype(f)[:, None] * inv], 1)
    cos, sin = np.cos(ang).astype(f), np.sin(ang).astype(f)
    rope = np.stack([np.stack([cos, cos], 2), np.stack([-sin, sin], 2)], 0)
    rope = c(rope.reshape(2, 8, 128, 64).transpose(2, 0, 1, 3))

    n = np.arange(512)
    dft = np.empty((2, 2, 512, 512))
    for par in range(2):
        a = 2 * np.pi * (n[:, None] * (2 * n[None, :] + par) % 1024) / 1024
        dft[par] = np.cos(a), np.sin(a)
    d = np.arange(128)
    a = 2 * np.pi * (d[:, None] * d[None, :] % 128) / 128
    g = 1.0 / np.sqrt(1024 * 128)
    cd = np.stack([np.cos(a) * g, -np.sin(a) * g], 1)

    return {
        "xT": fm(i["x"][0]), "vecs": vecs, "w_in": c(i["hgrn_w_in"][0]), "w_out": c(i["hgrn_w_out"][0]),
        "m_w1": c(i["mlp_w1"][0]), "m_w2": c(i["mlp_w2"][0]), "ctxT": fm(i["ctx_2"][0]), "w_ada": c(i["w_ada_2"][0]),
        "w_in2": c(i["w_in_2"][0]), "gains": gains, "biasE": c(edge), "biasM": c(mid),
        "w_gate": c(i["w_branch_gate_2"][0]), "w_fo": c(i["w_fourier_out_2"][0]), "w_ao": c(i["w_attn_out_2"][0]),
        "w_o2": c(i["w_out_2"][0]), "m2_w1": c(i["w_mlp1_2"][0]), "m2_w2": c(i["w_mlp2_2"][0]),
        "ident_d": np.eye(128, dtype=f), "masks_d": masks, "rope_d": rope, "dft_d": dft.astype(f),
        "cd_d": c(cd.astype(f)),
    }


def kernel(**inputs):
    from concourse import bacc
    from concourse.bass_utils import run_bass_kernel_spmd

    arrays = layout({k: np.asarray(v) for k, v in inputs.items()})
    nc = bacc.Bacc("TRN2", target_bir_lowering=False, num_devices=1)
    args = [nc.dram_tensor("in_" + n, a.shape, mybir.dt.from_np(a.dtype), kind="ExternalInput").ap()
            for n, a in arrays.items()]
    args.append(nc.dram_tensor("out_0", (8, 128, 1024), F, kind="ExternalOutput").ap())
    build(nc, *args)
    r = run_bass_kernel_spmd(nc, [{"in_" + n: a for n, a in arrays.items()}], core_ids=[0])
    got = np.asarray(r.results[0]["out_0"])
    return np.ascontiguousarray(got.reshape(1024, 1024).T).reshape(1, 1024, 1024)
```

```python
from contextlib import ExitStack

import numpy as np
import concourse.bass as bass
from concourse import mybir

F = mybir.dt.float32
R = mybir.dt.float32r
U8 = mybir.dt.uint8
ALU = mybir.AluOpType
ACT = mybir.ActivationFunctionType
AX = mybir.AxisListType.X

P = 128
T = 1024
EPS = 1e-6
NEG = -1.0e30
ENGINES = ("tensor", "vector", "scalar", "gpsimd", "sync")

V_MIX, V_MLP, V_FINAL, V_LB, V_ON, V_N1, V_N2, V_BADA = range(0, 64, 8)
V_END = V_BADA + 48


class Queues:

    def __init__(self, nc, ctx):
        self.nc, self.ctx = nc, ctx
        self.q = {e: [] for e in ENGINES}
        self.sems = {}
        self.n = {}

    def sem(self, name):
        if name not in self.sems:
            self.sems[name] = self.ctx.enter_context(self.nc.semaphore("s_" + name))
            self.n[name] = 0
        return self.sems[name]

    def op(self, engine, fn, *waits, sig=True):
        if sig:
            self.sem(engine)
            self.n[engine] += 1
        self.q[engine].append((fn, waits, engine if sig else None, 1))
        return (engine, self.n[engine]) if sig else None

    def dma(self, out, in_, lane, *waits):
        self.sem(lane)
        self.n[lane] += 16
        self.q["sync"].append((lambda e: e.dma_start(out, in_), waits, lane, 16))
        return (lane, self.n[lane])

    def emit(self, engine, e):
        seen = {}

        def wait(w):
            if w is None:
                return
            if isinstance(w, list):
                for x in w:
                    wait(x)
                return
            if isinstance(w, dict):
                wait(list(w.values()))
                return
            name, value = w
            if seen.get(name, 0) < value:
                seen[name] = value
                e.wait_ge(self.sems[name], value)

        for fn, waits, name, inc in self.q[engine]:
            wait(list(waits))
            ins = fn(e)
            if name:
                ins.then_inc(self.sems[name], inc)


class Ring:

    def __init__(self, items):
        self.items = items
        self.free = [[] for _ in items]
        self.i = -1

    def get(self):
        self.i = (self.i + 1) % len(self.items)
        return self.items[self.i], self.free[self.i], self.i

    def release(self, i, *tokens):
        self.free[i] = list(tokens)


def run_both(a, b, every=1):
    n = 0
    for _ in a:
        n += 1
        if n % every == 0 and b is not None:
            next(b, None)
    if b is not None:
        for _ in b:
            pass


def build(nc, xT, vecs, w_in, w_out, m_w1, m_w2, ctxT, c_d, w_ada, w_in2, gains, biasE, biasM, w_gate, w_fo, w_ao,
          w_o2, m2_w1, m2_w2, ident_d, masks_d, rope_d, dft_d, cd_d, out):
    with ExitStack() as ctx:
        Q = Queues(nc, ctx)
        op, dma = Q.op, Q.dma
        base = 16512
        R1A = base
        HA = R1A + 32768
        WRA = HA + 65536
        WSA = WRA + 8192
        SA = WSA + 32768
        CA = SA + 65536

        def at(name, shape, dt, off):
            return nc.alloc_sbuf_tensor_at(name, shape, dt, offset=off)

        R1 = at("R1", [P, 8, T], F, R1A)
        Hh = at("Hh", [P, 8, T], R, HA)
        Hl = at("Hl", [P, 8, T], R, HA + 32768)
        HT = at("HT", [P, 8, T], F, HA + 32768)
        Wraw = [at(f"Wraw{i}", [P, 1024], F, WRA + 4096 * i) for i in range(2)]
        Whi = [at(f"Whi{i}", [P, 1024], R, WSA + 8192 * i) for i in range(4)]
        Wlo = [at(f"Wlo{i}", [P, 1024], R, WSA + 8192 * i + 4096) for i in range(4)]

        def sa(name, i, dt=F, shape=(P, 1024)):
            return at(name, list(shape), dt, SA + 4096 * i)

        coff = [CA]

        def const(name, shape, dt=F, size=4):
            n = int(np.prod(shape[1:])) * size
            t = at(name, shape, dt, coff[0])
            coff[0] += (n + 31) // 32 * 32
            assert coff[0] <= 229344
            return t

        ident = const("ident", [P, P])
        ones = const("ones", [P, P])
        vec = const("vec", [P, V_END])
        masks = const("masks", [P, 8, P], U8, 1)
        eps = const("eps", [P, 1])
        lb = const("lb", [P, 8])
        oml = const("oml", [P, 8])
        lt = const("lt", [P, 3, 8])
        tot = const("tot", [P, 8])
        mods = const("mods", [P, 48, 2])
        modA = const("modA", [P, 3, 8])
        small = const("small", [P, 96])
        gq = const("gq", [P, 128])
        spare = coff[0]
        assert spare + 3328 <= 229344

        psum = [ctx.enter_context(nc.psum_tensor(f"ps{i}", [P, 1024], F)) for i in range(4)]
        xs_d = nc.dram_tensor("xs_scratch", [8, P, T], F, kind="Internal").ap()
        kc_d = nc.dram_tensor("kc_scratch", [P, 4, 256], F, kind="Internal").ap()
        vc_d = nc.dram_tensor("vc_scratch", [P, 2, 512], F, kind="Internal").ap()
        mf_d = nc.dram_tensor("mf_scratch", [8, P, T], F, kind="Internal").ap()

        class Weights:
            def __init__(self):
                self.plan = []
                self.loaded = 0
                self.taken = 0
                self.raw_free = [[], []]
                self.free = [[], [], [], []]
                self.released = [True] * 4
                self.tok = {}
                self.lo_engine = "vector"

            def pump(self, ahead=4):
                while self.loaded < len(self.plan) and self.loaded < self.taken + ahead and self.released[self.loaded % 4]:
                    n = self.loaded
                    src, a = self.plan[n]
                    r, s = n % 2, n % 4
                    raw, hi, lo = Wraw[r], Whi[s], Wlo[s]
                    d = dma(raw[:].rearrange("p (a b) -> p a b", a=a), src, f"w{r}", self.raw_free[r])
                    th = op("scalar", lambda e, raw=raw, hi=hi: e.activation(hi[:], raw[:], ACT.Copy), d, self.free[s])
                    tl = op(self.lo_engine, lambda e, raw=raw, hi=hi, lo=lo: e.tensor_tensor(
                        lo[:], raw[:], hi[:].bitcast(F), ALU.subtract), th, self.free[s])
                    self.raw_free[r] = [th, tl]
                    self.tok[n] = (th, tl)
                    self.released[s] = False
                    self.loaded += 1

            def get(self, a):
                n = self.taken
                self.taken += 1
                self.pump()
                assert self.loaded > n and self.plan[n][1] == a
                s = n % 4
                v = lambda t: t[:].rearrange("p (a b) -> p a b", a=a)
                return v(Whi[s]), v(Wlo[s]), self.tok[n][0], self.tok[n][1], s

            def release(self, s, tok):
                self.free[s] = [tok]
                self.released[s] = True
                self.pump()

        W = Weights()

        def cols128(w, c0, rows=1024, r0=0):
            return (w[r0:r0 + rows, c0:c0 + 128].rearrange("(k p) c -> p k c", p=P), rows // P)

        def cols256(w, c0, r0):
            return (w[r0:r0 + 512, c0:c0 + 256].rearrange("(k p) c -> p k c", p=P), 4)

        W.plan += [cols128(w_in, 1024)]
        for h in range(8):
            W.plan += [cols128(w_in, 128 * h), cols128(w_in, 3072 + 128 * h)]
            if h % 2 == 0:
                W.plan += [cols256(w_in, 2048 + 128 * h, 0), cols256(w_in, 2048 + 128 * h, 512)]
            if h < 7:
                W.plan += [cols128(w_in, 1152 + 128 * h)]
        W.plan += [cols128(w_out, 128 * m) for m in range(8)]

        def mlp_plan(w1, w2):
            s1 = lambda t: [cols128(w1, 128 * t)]
            s2 = lambda c: [cols256(w2, 256 * j, 512 * c) for j in range(4)]
            order = []
            for t in range(4):
                order += s1(t)
            for c in range(8):
                if c < 7:
                    order += s1(4 * c + 4)
                order += s2(c)
                if c < 7:
                    for t in range(4 * c + 5, 4 * c + 8):
                        order += s1(t)
            return order

        W.plan += mlp_plan(m_w1, m_w2)
        for c0 in (1536, 1792, 1024, 1280, 0, 256):
            W.plan += [cols256(w_in2, c0, 0), cols256(w_in2, c0, 512)]
        for par in range(2):
            for j in range(2):
                for cs in range(2):
                    W.plan.append((dft_d[par, cs].rearrange("(k p) c -> p k c", p=P)[:, :, 256 * j:256 * j + 256], 4))
        for m in range(0, 8, 2):
            W.plan += [cols128(w_gate, 128 * m), cols128(w_gate, 128 * m + 128), cols256(w_fo, 128 * m, 0)]
        for half in range(2):
            for c0 in (512, 1024, 1536):
                W.plan += [cols256(w_in2, c0 + 256 * half, 0), cols256(w_in2, c0 + 256 * half, 512)]
        for m in range(0, 8, 2):
            W.plan += [cols128(w_gate, 1024 + 128 * m), cols128(w_gate, 1152 + 128 * m), cols256(w_ao, 128 * m, 0)]
        W.plan += [cols128(w_o2, 128 * m) for m in range(8)]
        W.plan += mlp_plan(m2_w1, m2_w2)

        def mm(out_, l, r, *waits, start=False, stop=False, sig=False):
            return op("tensor", lambda e: e.matmul(out_, l, r, start=start, stop=stop), *waits, sig=sig)

        def part_of(tok, hf):
            return tok[hf] if isinstance(tok, dict) else tok

        def fm_steps(ps, psw, w, kt, Ah, Al, tokh, tokl, m0=0, nw=128, halves=False):
            wh, wl, th, tl, _ = w
            last = None
            for k in range(kt):
                for hf in range(2):
                    c = slice(512 * hf, 512 * hf + 512)
                    mm(ps[:, c], wh[:, k, m0:m0 + nw], Ah[:, k, c], psw, th, part_of(tokh[k], hf), start=(k == 0))
                for hf in range(2):
                    c = slice(512 * hf, 512 * hf + 512)
                    mm(ps[:, c], wl[:, k, m0:m0 + nw], Ah[:, k, c], tl)
                if k % 2:
                    yield None
            if halves:
                last = []
                for hf in range(2):
                    c = slice(512 * hf, 512 * hf + 512)
                    for k in range(kt):
                        end = k == kt - 1
                        t = mm(ps[:, c], wh[:, k, m0:m0 + nw], Al[:, k, c], tokl[k], stop=end, sig=end)
                    last.append(t)
                return last
            for k in range(kt):
                for hf in range(2):
                    c = slice(512 * hf, 512 * hf + 512)
                    end = k == kt - 1
                    last = mm(ps[:, c], wh[:, k, m0:m0 + nw], Al[:, k, c], tokl[k], stop=end, sig=end and hf == 1)
                if k % 2:
                    yield None
            return last

        def fm_tile(ring, kt, Ah, Al, tokh, tokl, post, w=None, m0=0, release=True, before=None, halves=False):
            if w is None:
                w = W.get(kt)
            ps, psw, i = ring.get()
            last = yield from fm_steps(ps, psw, w, kt, Ah, Al, tokh, tokl, m0, halves=halves)
            if release:
                W.release(w[4], last)
            if before is not None:
                for _ in before:
                    pass
            post(ps, last, ring, i)

        def tm_pair(ring, tiles, Ah, Al, tokh, tokl, post, flushes=True):
            ws = [W.get(4), W.get(4)]
            last = None
            for s in range((tiles + 3) // 4):
                ps, psw, i = ring.get()
                nt = min(4, tiles - 4 * s)
                for t in range(nt):
                    o = ps[:, 256 * t:256 * t + 256]
                    c = slice(128 * (4 * s + t), 128 * (4 * s + t) + 128)
                    for k in range(8):
                        wh, wl, th, tl, _ = ws[k // 4]
                        mm(o, Ah[:, k, c], wh[:, k % 4, :], psw, th, part_of(tokh[k], s), start=(k == 0))
                        mm(o, Ah[:, k, c], wl[:, k % 4, :], tl)
                        end = k == 7
                        last = mm(o, Al[:, k, c], wh[:, k % 4, :], tokl[k], stop=end, sig=end and t == nt - 1)
                        if k % 2:
                            yield None
                if s == (tiles + 3) // 4 - 1:
                    for w in ws:
                        W.release(w[4], last)
                if flushes:
                    flush()
                post(s, ps, last, ring, i)

        def drain(g):
            for _ in g:
                pass

        allps = Ring(psum)
        pending = []

        def flush():
            while pending:
                pending.pop(0)()

        LOG, SIG = "natural_log_exp_and_others", "sigmoid_and_others"
        tables = [None]

        def table(name):
            if tables[0] != name:
                tables[0] = name
                Q.q["scalar"].append((lambda e: e.preload_act_table_set(name), (), None, 0))

        t_vec = dma(vec[:], vecs, "c1")
        t_x = [dma(R1[:, k, :], xT[k], f"x{k}") for k in range(8)]
        t_id = dma(ident[:], ident_d, "c0")
        t_ones = op("vector", lambda e: e.memset(ones[:], 1.0))
        t_eps = op("vector", lambda e: e.memset(eps[:], EPS))

        lbr = vec[:, V_LB:V_LB + 8]
        a = op("vector", lambda e: e.tensor_tensor(lt[:, 0, :], lbr, lbr, ALU.subtract), t_vec)
        table(LOG)
        a = op("scalar", lambda e: e.activation(lt[:, 1, :], lt[:, 0, :], ACT.Exp), a)
        a = op("vector", lambda e: e.reciprocal(lt[:, 2, :], lt[:, 1, :]), a)
        a = op("vector", lambda e: e.tensor_tensor(lt[:, 0, :], lt[:, 1, :], lt[:, 2, :], ALU.mult), a)
        a = op("vector", lambda e: e.tensor_tensor(lb[:], lt[:, 0, :], lt[:, 0, :], ALU.subtract), a)
        t_lb = op("vector", lambda e: e.tensor_scalar(oml[:], lb[:], -1.0, 1.0, ALU.mult, ALU.add), a)

        class Stats:

            def __init__(self, acc, sq, waits, n=T, acc2=None, gain=None, adders=("vector", "gpsimd")):
                self.adders = adders
                self.acc, self.sq = [acc, acc2], sq
                self.gains = [None] if acc2 is None else [None, gain]
                self.sqfree = [list(waits) for _ in sq]
                self.i, self.j, self.n = 0, 0, n
                self.tok = [list(waits), list(waits)]
                self.last = {}

            def add(self, x, tok):
                n = self.n
                end = self.i == 7
                parts = [slice(0, 512), slice(512, 1024)] if end and n == T else [slice(0, n)]
                toks = tok if isinstance(tok, list) and len(tok) == len(parts) else [tok] * len(parts)
                bufs = []
                for a_, gain in enumerate(self.gains):
                    if self.i == 0:
                        bufs.append((a_, self.acc[a_], self.tok[a_], None))
                    else:
                        bufs.append((a_, self.sq[self.j % len(self.sq)], self.sqfree[self.j % len(self.sq)],
                                     self.j % len(self.sq)))
                        self.j += 1
                for p_, c in enumerate(parts):
                    for a_, o, w, s in bufs:
                        sc = 1.0 if a_ == 0 else self.gains[1](self.i)
                        t = op("scalar", lambda e, o=o, c=c, sc=sc: e.activation(o[:, c], x[:, c], ACT.Square, scale=sc),
                               toks[p_], w)
                        if end:
                            self.last.setdefault(a_, []).append((o, t))
                            self.sqfree[s] = [t]
                        elif self.i == 0:
                            self.tok[a_] = [t]
                        else:
                            b = op(self.adders[a_], lambda e, o=o, a_=a_: e.tensor_tensor(
                                self.acc[a_][:, :n], self.acc[a_][:, :n], o[:, :n], ALU.add), t, self.tok[a_])
                            self.tok[a_] = [b]
                            self.sqfree[s] = [b]
                self.i += 1

            def last_tokens(self):
                return [t for v in self.last.values() for _, t in v]

            def sums(self, ps, psw, a_):
                parts = [slice(c0, c0 + min(512, self.n)) for c0 in range(0, self.n, 512)]
                for c in parts:
                    mm(ps[:, c], ones[:], self.acc[a_][:, c], psw, self.tok[a_], t_ones, start=True)
                return [(c, mm(ps[:, c], ones[:], self.last[a_][p_][0][:, c], self.last[a_][p_][1], stop=True, sig=True))
                        for p_, c in enumerate(parts)]

            def second(self, ring, rs, rt, rs2, waits):
                ps, psw, i = ring.get()
                toks = []
                for p_, (c, a) in enumerate(self.sums(ps, psw, 1)):
                    b = op("scalar", lambda e, c=c: e.activation(rs2[:, c], rs[:, c], ACT.Square), rt[p_], waits)
                    b = op("vector", lambda e, c=c: e.tensor_tensor(rs2[:, c], rs2[:, c], ps[:, c], ALU.mult), a, b)
                    table(LOG)
                    d = op("scalar", lambda e, c=c: e.activation(rs2[:, c], rs2[:, c], ACT.Ln, bias=eps[:, 0:1],
                                                                 scale=1.0 / 1024), b)
                    d = op("scalar", lambda e, c=c: e.activation(rs2[:, c], rs2[:, c], ACT.Exp, scale=-0.5), d)
                    d = op("vector", lambda e, c=c: e.tensor_tensor(rs2[:, c], rs2[:, c], rs[:, c], ALU.mult), d)
                    toks.append(d)
                ring.release(i, b)
                return toks

            def finish(self, ring, rstd, waits, inv=1.0 / 1024):
                ps, psw, i = ring.get()
                toks = []
                for c, a in self.sums(ps, psw, 0):
                    table(LOG)
                    b = op("scalar", lambda e, c=c: e.activation(rstd[:, c], ps[:, c], ACT.Ln, bias=eps[:, 0:1],
                                                                 scale=inv), a, t_eps, waits)
                    d = op("scalar", lambda e, c=c: e.activation(rstd[:, c], rstd[:, c], ACT.Exp, scale=-0.5), b)
                    toks.append(d)
                ring.release(i, toks[-1])
                return toks

        def split(src, hi, lo, tok, waits, lo_engine="vector"):
            th = op("scalar", lambda e: e.activation(hi, src, ACT.Copy), tok, waits)
            tl = op(lo_engine, lambda e: e.tensor_tensor(lo, src, hi.bitcast(F), ALU.subtract), th, waits)
            return th, tl

        def apply_norm(*args, **kw):
            tokh, tokl = [], []
            drain(norm_steps(tokh, tokl, *args, **kw))
            return tokh, tokl

        def norm_steps(tokh, tokl, xk, tok, gain, rstd, rt, Tk, Hh_, Hl_, waits, shift=None, n=T, hw=None, on_vector=False):
            ta = []
            for k in range(8):
                parts = [slice(0, 512), slice(512, n)] if k == 0 and len(rt) == 2 else [slice(0, n)]
                ta.append([op("vector", lambda e, k=k, c=c: e.scalar_tensor_tensor(
                    Tk[:, k, c], xk(k)[:, c], gain(k), rstd[:, c], ALU.mult, ALU.mult), tok[k],
                    rt[p_] if len(parts) == 2 else rt, waits) for p_, c in enumerate(parts)])
            yield None
            hws = hw or (lambda: None)
            for k in range(8):
                parts = [slice(0, 512), slice(512, n)] if k == 0 and len(rt) == 2 else [slice(0, n)]
                th = {}
                for p_, c in enumerate(parts):
                    t, hi, a = Tk[:, k, c], Hh_[:, k, c], ta[k][p_] if len(parts) == 2 else ta[k]
                    if shift is not None:
                        th[p_] = op("scalar", lambda e, k=k, t=t, hi=hi: e.activation(hi, t, ACT.Identity, bias=shift(k)),
                                    a, hws())
                    else:
                        th[p_] = op("scalar", lambda e, t=t, hi=hi: e.activation(hi, t, ACT.Copy), a, hws())
                t, hi, lo = Tk[:, k, :n], Hh_[:, k, :n], Hl_[:, k, :n]
                if shift is not None and k % 2 == 0 and not on_vector:
                    a = op("scalar", lambda e, k=k, t=t: e.activation(t, t, ACT.Identity, bias=shift(k)), ta[k], th)
                    tl = op("gpsimd", lambda e, t=t, hi=hi, lo=lo: e.tensor_tensor(lo, t, hi.bitcast(F), ALU.subtract),
                            a, th)
                elif shift is not None:
                    tl = op("vector", lambda e, k=k, t=t, hi=hi, lo=lo: e.scalar_tensor_tensor(
                        lo, t, shift(k), hi.bitcast(F), ALU.add, ALU.subtract), th)
                else:
                    tl = op("vector" if k % 2 else "gpsimd", lambda e, t=t, hi=hi, lo=lo: e.tensor_tensor(
                        lo, t, hi.bitcast(F), ALU.subtract), th)
                tokh.append(th if len(parts) == 2 else th[0])
                tokl.append(tl)

        col = lambda c: (lambda k: vec[:, c + k:c + k + 1])

        V = sa("V", 0, F, (P, 8, 256))
        Qb, Kb = [sa("q0", 2), sa("q1", 4)], [sa("k0", 5), sa("k1", 7)]
        Pt, sg, Tb, spare_t = sa("Pt", 3), sa("sg", 6), sa("Tb", 8), sa("spare", 9)
        acc = sa("acc", 10)
        kST = sa("kST", 11)
        St = sa("St", 12)
        t1, t2, t3 = sa("t1", 13), sa("t2", 14), sa("t3", 15)

        t_mraw = dma(spare_t[:].rearrange("p (a b) -> p a b", a=8), masks_d, "c2")
        t_mask = op("gpsimd", lambda e: e.tensor_copy(masks[:], spare_t[:].rearrange("p (a b) -> p a b", a=8)), t_mraw)
        st = Stats(t1, [t2, t3], [])
        for k in range(8):
            st.add(R1[:, k, :], t_x[k])
        W.pump(2)
        rt = st.finish(allps, t2, [])
        tokh, tokl = apply_norm(lambda k: R1[:, k, :], t_x, col(V_MIX), t2, rt, HT, Hh, Hl, [t_vec])
        h_done = list(tokl)
        t_memacc = op("gpsimd", lambda e: e.memset(acc[:], 0.0))

        A = Ring(psum[0:2])
        B = Ring(psum[2:4])
        A.free = [list(allps.free[0]), list(allps.free[1])]
        B.free = [list(allps.free[2]), list(allps.free[3])]
        c3 = lambda t: t[:].rearrange("p (c m) -> p c m", m=128)
        free = {n: [] for n in ("q0", "q1", "P", "T", "k0", "k1", "sg", "acc", "kST", "St", "tot", "V")}
        free["acc"] = [t_memacc]
        free["t1"] = [rt]
        free["t2"] = list(tokh)
        free["t3"] = list(tokh)
        last_t = {}
        tv = {}
        oT = []

        def v_post(s, ps, last, ring, i):
            a = op("scalar", lambda e: e.activation(V[:, 4 * s:4 * s + 4, :],
                                                    ps[:].rearrange("p (c m) -> p c m", m=256), ACT.Copy),
                   last, free["V"])
            ring.release(i, a)
            tv[s] = a

        def head_f(h, before=None):
            def post(ps, last, ring, i):
                k0 = Kb[0]
                table(SIG)
                a = op("scalar", lambda e: e.activation(Pt[:], ps[:], ACT.Sigmoid), last, free["P"])
                b = op("scalar", lambda e: e.activation(k0[:], ps[:], ACT.Sigmoid, scale=-1.0), last, free["k0"])
                ring.release(i, b)
                last_t["P"] = op("vector", lambda e: e.tensor_scalar(Pt[:], Pt[:], oml[:, h:h + 1], lb[:, h:h + 1],
                                                                     ALU.mult, ALU.add), a, t_lb)
                last_t["k"] = op("vector", lambda e: e.tensor_scalar(k0[:], k0[:], oml[:, h:h + 1], None, ALU.mult),
                                 b, t_lb)
            return fm_tile(A, 8, Hh, Hl, tokh, tokl, post, before=before)

        def head_q(h):
            def post(ps, last, ring, i):
                qt, w = Qb[h % 2], free[f"q{h % 2}"]
                table(SIG)
                a = op("scalar", lambda e: e.activation(qt[:], ps[:], ACT.Sigmoid), last, w)
                b = op("vector", lambda e: e.scalar_tensor_tensor(qt[:], qt[:], float(128 ** -0.5), ps[:], ALU.mult,
                                                                  ALU.mult), a)
                ring.release(i, b)
                last_t["q"] = b
            return fm_tile(A, 8, Hh, Hl, tokh, tokl, post)

        def head_g(h):
            def post(ps, last, ring, i):
                table(SIG)
                a = op("scalar", lambda e: e.activation(sg[:], ps[:], ACT.Sigmoid), last, free["sg"])
                b = op("vector", lambda e: e.tensor_tensor(sg[:], sg[:], ps[:], ALU.mult), a)
                ring.release(i, b)
                last_t["sg"] = b
                last_t["proj"] = last
            return fm_tile(A, 8, Hh, Hl, tokh, tokl, post)

        def scan_levels(h):
            iq, ik = h % 2, 0
            a3 = c3(acc)
            tk, tp = [last_t["k"]], last_t["P"]
            tq = [last_t["q"]]
            yield None

            def scores(q, k, w):
                ps, psw, i = B.get()
                for c in range(8):
                    last = mm(c3(ps)[:, c, :], c3(k)[:, c, :], c3(q)[:, c, :], psw, w, start=True, stop=True,
                              sig=c == 7)
                return ps, i, last

            def masked(ps, i, tok, lev, prev):
                toks = []
                for hf in range(2):
                    c = slice(4 * hf, 4 * hf + 4)
                    toks.append(op("vector", lambda e, c=c: e.copy_predicated(
                        a3[:, c, :], masks[:, lev, :][:, None, :].broadcast_to([P, 4, P]), c3(ps)[:, c, :]),
                        tok, t_mask, prev[hf]))
                B.release(i, toks[1])
                return toks

            Q0, Q1, K0 = Qb[iq], Qb[1 - iq], Kb[0]
            ps, i, last = scores(Q0, K0, [tq, tk])
            readq = {iq: last, 1 - iq: None}
            readk = {0: last, 1: None}
            tq = [op("vector", lambda e: e.tensor_tensor(Q1[:], Q0[:], Pt[:], ALU.mult), tq, tp,
                     free[f"q{1 - iq}"])]
            iq = 1 - iq
            prev = masked(ps, i, last, 0, [free["acc"], free["acc"]])
            yield None
            Tm, tT, off = Pt[:], [tp], 0
            m, lev = 1, 1
            while m < 128:
                v = lambda t, m=m: t[:].rearrange("p (b two m) -> p b two m", two=2, m=m)
                Qc, Qn, Kc, Kn = Qb[iq], Qb[1 - iq], Kb[ik], Kb[1 - ik]
                nb = T // (2 * m)
                sh = [P, nb, m]
                if m < 32:
                    ps, i, last = scores(Qc, Kc, [tq, tk])
                elif m == 32:
                    ps, psw, i = B.get()
                    for b0 in (0, 64):
                        for c in range(8):
                            last = mm(ps[b0:b0 + 32, 32 * c:32 * c + 32], c3(Kc)[:, c, b0:b0 + 32],
                                      c3(Qc)[:, c, b0 + 32:b0 + 64], psw, tq, tk, start=True, stop=True,
                                      sig=(b0 == 64 and c == 7))
                else:
                    ps, psw, i = B.get()
                    for c in range(8):
                        last = mm(ps[0:64, 64 * c:64 * c + 64], c3(Kc)[:, c, 0:64], c3(Qc)[:, c, 64:128], psw, tq, tk,
                                  start=True, stop=True, sig=c == 7)
                T2 = Tm.rearrange("p (b two) -> p b two", two=2)
                wq = [readq[1 - iq], free[f"q{1 - iq}"] if m == 1 else None]
                wk = [readk[1 - ik], free["k1"] if m == 1 else None]
                q1 = op("vector", lambda e, v=v, sh=sh, Qc=Qc, Qn=Qn, T2=T2: e.tensor_tensor(
                    v(Qn)[:, :, 1, :], v(Qc)[:, :, 1, :], T2[:, :, 0:1].broadcast_to(sh), ALU.mult), tq, tT, wq)
                q2 = op("scalar", lambda e, v=v, Qc=Qc, Qn=Qn: e.activation(
                    v(Qn)[:, :, 0, :], v(Qc)[:, :, 0, :], ACT.Copy), tq, wq)
                k1 = op("gpsimd", lambda e, v=v, sh=sh, Kc=Kc, Kn=Kn, T2=T2: e.tensor_tensor(
                    v(Kn)[:, :, 0, :], v(Kc)[:, :, 0, :], T2[:, :, 1:2].broadcast_to(sh), ALU.mult), tk, tT, wk)
                k2 = op("scalar", lambda e, v=v, Kc=Kc, Kn=Kn: e.activation(
                    v(Kn)[:, :, 1, :], v(Kc)[:, :, 1, :], ACT.Copy), tk, wk)
                if m < 64:
                    Tn, tw = Tb[:, off:off + nb], free["T"]
                    off += nb
                else:
                    Tn, tw = tot[:], free["tot"]
                tT_ = [op("gpsimd", lambda e, Tn=Tn, T2=T2: e.tensor_tensor(Tn, T2[:, :, 0], T2[:, :, 1], ALU.mult),
                          tT, tw)]
                if m < 32:
                    prev = masked(ps, i, last, lev, prev)
                elif m == 32:
                    prev_ = []
                    for b0 in (0, 64):
                        prev_.append(op("scalar", lambda e, b0=b0, ps=ps: e.activation(
                            a3[b0:b0 + 32, :, b0 + 32:b0 + 64],
                            ps[b0:b0 + 32, 0:256].rearrange("p (c t) -> p c t", c=8), ACT.Copy), last, prev))
                    B.release(i, prev_)
                    prev = prev + prev_
                else:
                    t = op("scalar", lambda e, ps=ps: e.activation(
                        a3[0:64, :, 64:128], ps[0:64, 0:512].rearrange("p (c t) -> p c t", c=8), ACT.Copy), last,
                        prev)
                    B.release(i, t)
                    prev = prev + [t]
                readq[iq], readk[ik] = last, last
                if m == 1:
                    free["P"] = [q1, k1, tT_]
                tq, tk, tT = [q1, q2], [k1, k2], tT_
                Tm = Tn
                iq, ik = 1 - iq, 1 - ik
                yield None
                m *= 2
                lev += 1
            free["T"] = [q1, k1, tT_]
            last_t["acc"] = prev
            free["k0"] = [last, tk]
            free[f"q{1 - iq}"] = [last, tq]
            last_t["kS"], last_t["qP"], last_t["tot"] = (Kb[ik], tk), (Qb[iq], tq, iq), tT_

        def scan_tail(h):
            kS, tks = last_t["kS"]
            qP, tqp, qi = last_t["qP"]
            acct = last_t["acc"]
            tsg = last_t["sg"]
            vo = 128 * (h % 2)
            a3 = c3(acc)
            ps, psw, i = B.get()
            for c in range(7):
                last = op("tensor", lambda e, c=c, ps=ps: e.transpose(c3(ps)[:, c, :], c3(kS)[:, c, :], ident[:]),
                          psw, tks, t_id, sig=c == 6)
            free["k1"] = [last]
            t = op("scalar", lambda e, ps=ps: e.activation(kST[:, 0:896], ps[:, 0:896], ACT.Copy), last, free["kST"])
            B.release(i, t)
            yield None
            yield None
            ps, psw, i = B.get()
            for c in range(7):
                last = mm(c3(ps)[:, c, :], c3(kST)[:, c, :], V[:, c, vo:vo + 128], psw, t, tv[0], tv[1], start=True,
                          stop=True, sig=c == 6)
            free["kST"] = [last]
            s3 = c3(St)
            t = op("vector", lambda e, ps=ps: e.tensor_copy(s3[:, 1, :], c3(ps)[:, 0, :]), last, free["St"])
            for c in range(1, 7):
                t = op("vector", lambda e, c=c, ps=ps: e.scalar_tensor_tensor(
                    s3[:, c + 1, :], s3[:, c, :], tot[:, c:c + 1], c3(ps)[:, c, :], ALU.mult, ALU.add), t,
                    last_t["tot"])
            B.release(i, t)
            free["tot"] = [t]
            yield None
            yield None
            ps, psw, i = B.get()
            for c in range(8):
                mm(c3(ps)[:, c, :], V[:, c, vo:vo + 128], a3[:, c, :], psw, acct, tv[0], tv[1], start=True,
                   stop=(c == 0))
                if c:
                    last = mm(c3(ps)[:, c, :], s3[:, c, :], c3(qP)[:, c, :], tqp, t, stop=True, sig=c == 7)
            free[f"q{qi}"] = [last]
            free["acc"] = [last]
            free["St"] = [last]
            free["V"] = [last]
            to = op("scalar", lambda e, ps=ps: e.activation(R1[:, h, :], ps[:], ACT.Copy), last, h_done)
            tq2 = op("scalar", lambda e, ps=ps: e.activation(t1[:], ps[:], ACT.Square), last, free["t1"])
            B.release(i, to, tq2)
            yield None
            yield None
            ps, psw, i = B.get()
            table(LOG)
            halves = [slice(0, 512), slice(512, 1024)]
            last = [mm(ps[:, c], ones[:], t1[:, c], psw, tq2, start=True, stop=True, sig=True) for c in halves]
            free["t1"] = [last]
            ta, tb = [], []
            for l, c in zip(last, halves):
                t = op("scalar", lambda e, ps=ps, c=c: e.activation(t2[:, c], ps[:, c], ACT.Ln, bias=eps[:, 0:1],
                                                                    scale=1.0 / 128), l, free["t2"])
                ta.append(t)
                t = op("scalar", lambda e, c=c: e.activation(t2[:, c], t2[:, c], ACT.Exp, scale=-0.5), t)
                t = op("vector", lambda e, c=c: e.tensor_tensor(t2[:, c], t2[:, c], sg[:, c], ALU.mult), t, tsg)
                t = op("vector", lambda e, c=c: e.scalar_tensor_tensor(R1[:, h, c], R1[:, h, c],
                                                                       vec[:, V_ON + h:V_ON + h + 1], t2[:, c],
                                                                       ALU.mult, ALU.mult), t, to)
                tb.append(t)
            B.release(i, *ta)
            t = tb
            free["sg"] = [t]
            free["t2"] = [t]
            oT.append(t)
            yield None

        def chain(*gs):
            for g in gs:
                yield from g

        oh, ol, part = [], [], []

        def split_out(k):
            th, tl = split(R1[:, k, :], Hh[:, k, :], Hl[:, k, :], oT[k], [last_t["proj"]],
                           "vector" if k % 2 == 0 else "gpsimd")
            oh.append(th)
            ol.append(tl)

        def wout_products(w, ps, psw, k):
            for a_, b_, tok in ((w[0], Hh, (psw, w[2], oh[k])), (w[1], Hh, (w[3],)), (w[0], Hl, (ol[k],))):
                for hf in range(2):
                    c = slice(512 * hf, 512 * hf + 512)
                    last = mm(ps[:, c], a_[:, k, :], b_[:, k, c], *tok, start=(k == 0 and a_ is w[0] and b_ is Hh),
                              stop=(k == 7 and b_ is Hl), sig=(k == 7 and b_ is Hl and hf == 1))
            return last

        def wout_start():
            split_out(0)
            split_out(1)
            for _ in range(2):
                part.append((W.get(8), *A.get()))
            for k in range(7):
                if k < 5:
                    split_out(k + 2)
                for w, ps, psw, _ in part:
                    wout_products(w, ps, psw, k)
                    yield None

        drain(head_f(0))
        tail = None
        for h in range(8):
            run_both(head_q(h), tail, 1)
            levels = scan_levels(h)
            more = [head_g(h)]
            if h % 2 == 0:
                more.append(tm_pair(A, 8, Hh, Hl, tokh, tokl, v_post))
            if h < 7:
                more.append(head_f(h + 1, levels))
            tail = scan_tail(h)
            if h < 7:
                run_both(chain(*more), levels, 2 if h % 2 else 4)
        rest = chain(levels, tail)
        for _ in more[0]:
            next(rest, None)
        run_both(wout_start(), rest, 1)

        split_out(7)
        tokh, tokl = oh, ol
        t_x = [dma(R1[:, k, :], xT[k], f"x{k}", tokh[k], tokl[k]) for k in range(8)]

        def add_tile(m, st, scale=None, tok=None, final=True):
            def post(ps, last, ring, i):
                t = []
                lasts = last if isinstance(last, list) else [last]
                w = T // len(lasts)
                for p_, l in enumerate(lasts):
                    c = slice(w * p_, w * p_ + w)
                    if scale is None:
                        t.append(op("vector", lambda e, c=c: e.tensor_tensor(R1[:, m, c], ps[:, c], R1[:, m, c], ALU.add),
                                    l, tok[m]))
                    else:
                        t.append(op("vector", lambda e, c=c: e.scalar_tensor_tensor(
                            R1[:, m, c], ps[:, c], scale(m), R1[:, m, c], ALU.mult, ALU.add), l, tok[m]))
                ring.release(i, *t)
                tok[m] = t
                if final and st is not None:
                    st.add(R1[:, m, :], t)
            return post

        tx = list(t_x)
        st = Stats(t1, [kST, t3], [free["t1"], free["kST"], free["t3"], free["t2"]])
        for m, (w, ps, psw, i) in enumerate(part):
            last = wout_products(w, ps, psw, 7)
            W.release(w[4], last)
            add_tile(m, st, tok=tx)(ps, last, A, i)
        allps.free = [A.free[0], A.free[1], B.free[0], B.free[1]]
        allps.i = 1
        for m in range(2, 8):
            drain(fm_tile(allps, 8, Hh, Hl, tokh, tokl, add_tile(m, st, tok=tx), halves=m == 7))
        h_read = ("tensor", Q.n["tensor"])

        def mlp(tx, tokh, tokl, waits, st_of, scale=None, done=None):
            ah = at("ah" + ("2" if scale else ""), [P, 5, T], R, SA)
            al = at("al" + ("2" if scale else ""), [P, 5, T], R, SA + 5 * 4096)
            nm = "m2" if scale else "m1"
            tr = Ring([sa(nm + f"r{i}", 10 + i) for i in range(3)])
            done["tr"] = tr
            tr.free = [list(waits) for _ in tr.free]

            def hook():
                if done.get("hook"):
                    next(done["hook"], None)
            afree = [list(waits) for _ in range(5)]
            at_ = {}

            def s1(t):
                sl = t % 5

                def post(ps, last, ring, i):
                    rl, w1, i1 = tr.get()
                    a = op("scalar", lambda e: e.activation(rl[:], ps[:], ACT.Relu), last, w1)
                    ring.release(i, a)
                    b = op("vector", lambda e: e.tensor_tensor(rl[:], rl[:], rl[:], ALU.mult), a)
                    th, tl = split(rl[:], ah[:, sl, :], al[:, sl, :], b, afree[sl])
                    tr.release(i1, th, tl)
                    at_[t] = (th, tl)
                    hook()
                drain(fm_tile(allps, 8, Hh, Hl, tokh, tokl, post))

            def s2(c):
                for j in range(4):
                    w = W.get(4)
                    for mm_ in range(2):
                        m = 2 * j + mm_
                        ps, psw, i = allps.get()
                        halves = c == 7 and m == 7 and scale is None
                        lasts, last = [], None
                        late = c == 7 and m == 0
                        for part, only, ks in (((0, None, (0, 1, 2)), (1, None, (0, 1, 2)), (0, None, (3,)),
                                                (1, None, (3,))) if late else
                                               ((0, None, range(4)), (1, 0, range(4)), (1, 1, range(4))) if halves else
                                               ((0, None, range(4)), (1, None, range(4)))):
                            for k in ks:
                                sl = (4 * c + k) % 5
                                th, tl = at_[4 * c + k]
                                for hf in (0, 1) if only is None else (only,):
                                    cs = slice(512 * hf, 512 * hf + 512)
                                    ws = slice(128 * mm_, 128 * mm_ + 128)
                                    if part == 0:
                                        mm(ps[:, cs], w[0][:, k, ws], ah[:, sl, cs], psw, w[2], th, start=(k == 0))
                                        mm(ps[:, cs], w[1][:, k, ws], ah[:, sl, cs], w[3])
                                    else:
                                        last = mm(ps[:, cs], w[0][:, k, ws], al[:, sl, cs], tl, stop=(k == 3),
                                                  sig=(k == 3 and (hf == 1 or halves)))
                            lasts.append(last)
                        if mm_ == 1:
                            W.release(w[4], last)
                        if m == 7:
                            for k in range(4):
                                afree[(4 * c + k) % 5] = [last]
                        if c == 7 and m == 0:
                            if done.get("hook"):
                                drain(done["hook"])
                            done["relu"] = [tr.free]
                            done["st"] = st_of()
                        add_tile(m, done.get("st"), scale, tx, final=(c == 7))(ps, lasts[1:] if halves else last, allps, i)
                        if c < 7:
                            hook()
                        if c == 7 and done.get("post"):
                            done["post"](m)

            for t in range(4):
                s1(t)
            for c in range(8):
                if c < 7:
                    s1(4 * c + 4)
                s2(c)
                if c < 7:
                    for t in range(4 * c + 5, 4 * c + 8):
                        s1(t)

        rt = st.finish(allps, t2, [st.sqfree, free["t2"]])
        tokh, tokl = apply_norm(lambda k: R1[:, k, :], tx, col(V_MLP), t2, rt, HT, Hh, Hl, [h_read])
        tn = [tokl, tokh, st.sqfree]
        done = {}
        n1, n2, n3 = sa("n1", 14), sa("n2", 15), sa("n3", 13)
        mod_t = []

        def modulations():
            raws = Ring([n3, n1])
            raws.free = [[tn, h_read]] * 2
            t = [tn, h_read]
            for w, tiles in ((0, 48), (1, 16)):
                d = dma(n2[:], c_d[w], "cb", t)
                raw, rw, ri = raws.get()
                table(SIG)
                a = op("scalar", lambda e, raw=raw: e.activation(raw[:], n2[:], ACT.Sigmoid), d, rw)
                tc = op("vector", lambda e, raw=raw: e.tensor_tensor(n2[:], n2[:], raw[:], ALU.mult), a)
                raws.release(ri, tc)
                yield None
                for j in range(tiles):
                    raw, rw, ri = raws.get()
                    d = dma(raw[:], w_ada[j], f"a{ri}", rw)
                    t = op("vector", lambda e, raw=raw, j=j, w=w: e.tensor_tensor_reduce(
                        raw[:], raw[:], n2[:], 1.0, vec[:, V_BADA + j:V_BADA + j + 1], ALU.mult, ALU.add,
                        mods[:, j, w:w + 1]), d, tc)
                    raws.release(ri, t)
                    yield None
                mod_t.append(t)
            done["ada"] = [t, raws.free]

        cx = at("cx", [P, 8, 256], F, HA)
        hch, hcl = at("hch", [P, 8, 256], R, HA + 8192), at("hcl", [P, 8, 256], R, HA + 16384)
        hcT = at("hcT", [P, 8, 256], F, HA + 16384)
        cacc, csq, csq2, crs = (at(n, [P, 256], F, HA + 24576 + 1024 * i)
                                for i, n in enumerate(("cacc", "csq", "csq2", "crs")))
        gnq = at("gnq", [P, 128], F, HA + 28672)
        gA = lambda j: (lambda k: modA[:, j, k:k + 1])
        mc = lambda m0, w0=0: (lambda k: mods[:, m0 + k, w0:w0 + 1])
        pe_now = lambda: ("tensor", Q.n["tensor"])
        cxn = {}

        def first_stats():
            free_ = pe_now()
            cxn["h_read"] = free_
            tcx = dma(cx[:], ctxT.rearrange("k p t -> p k t"), "c3", free_, tn)
            cxn["g"] = dma(gnq[:], gains, "c4", free_, tn)
            for j, (g0, m0, w0) in enumerate(((V_N1, 8, 0), (V_N1, 8, 1), (V_N2, 32, 0))):
                cxn["A"] = op("vector", lambda e, j=j, g0=g0, m0=m0, w0=w0: e.scalar_tensor_tensor(
                    modA[:, j, :], mods[:, m0:m0 + 8, w0], 1.0, vec[:, g0:g0 + 8], ALU.add, ALU.mult), mod_t)
            cxn["A"] = op("vector", lambda e: e.tensor_tensor(modA[:, 0, :], modA[:, 0, :],
                                                              vec[:, V_FINAL:V_FINAL + 8], ALU.mult), cxn["A"])
            cxn["st"], cxn["x"] = Stats(cacc, [csq, csq2], [free_, tn], n=256,
                                        adders=("gpsimd",)), tcx
            return Stats(n1, [n2, done["tr"].items[1]], [tn, done["ada"], done["relu"]], acc2=n3, gain=col(V_FINAL))

        def ctx_norm(m):
            if m <= 3:
                for k in (2 * m, 2 * m + 1):
                    cxn["st"].add(cx[:, k, :], cxn["x"])
            if m == 5:
                w = [cxn["h_read"], tn]
                rtc = cxn["st"].finish(allps, crs, w)
                cxn["h"] = ([], [])
                drain(norm_steps(*cxn["h"], lambda k: cx[:, k, :], [cxn["x"]] * 8, gA(1), crs, rtc, hcT, hch, hcl,
                                 [w, cxn["A"]], shift=mc(0, 1), n=256))
                cxn["free"] = [*cxn["h"], rtc, cxn["st"].tok, cxn["st"].sqfree]

        done["hook"] = modulations()
        done["post"] = ctx_norm
        mlp(tx, tokh, tokl, tn, first_stats, done=done)
        h_read = ("tensor", Q.n["tensor"])
        t_A = cxn["A"]

        st = done["st"]
        rs, rs2 = sa("rs", 12), sa("rs2", 10)
        tch, tcl, ctx_read = cxn["h"][0], cxn["h"][1], cxn["free"]
        qT = at("qT", [P, 4, T], F, R1A)
        kT = at("kT", [P, 2, T], F, SA + 12 * 4096)
        Vx = at("Vx", [P, 8, 256], F, R1A + 16384)
        kcT = at("kcT", [P, 4, 256], F, R1A + 24576)
        vc = at("vc", [P, 2, 512], F, R1A + 28672)
        rope = at("rope", [P, 2, 8, 64], F, SA)
        a1, a2, a3_ = (sa(n, 1 + i) for i, n in enumerate(("a1", "a2", "a3")))
        kcS, vcS = at("kcS", [P, 4, 256], F, SA), at("vcS", [P, 2, 512], F, SA + 3 * 4096)
        t_gq = op("vector", lambda e: e.tensor_scalar(gq[:, 0:64], gnq[:, 0:64], 0.125, None, ALU.mult), cxn["g"])
        t_gk = op("vector", lambda e: e.tensor_copy(gq[:, 64:128], gnq[:, 64:128]), cxn["g"])
        fre = {n: [h_read] for n in ("a1", "a2", "a3", "a4", "a5")}
        t_rope = None
        att = []

        work = {"a1": a1, "a2": a2, "a4": sa("a4", 4), "a5": sa("a5", 5)}

        def heads_post(nt, which, dst, tile0, roped, dfree, bufs=("a1", "a2"), rests=None):
            n = nt * 256
            n1_, n2_ = bufs
            a1, a2 = work[n1_], work[n2_]

            def post(s, ps, last, ring, i):
                v3 = lambda t: t[:, 0:n].rearrange("p (x c) -> p x c", c=64)
                b3 = [P, n // 64, 64]
                ss = small[:, 0:n // 64]
                a = op("scalar", lambda e: e.activation(a1[:, 0:n], ps[:, 0:n], ACT.Copy), last, fre[n1_])
                b = op("scalar", lambda e: e.activation(a2[:, 0:n], ps[:, 0:n], ACT.Square), last, fre[n2_])
                ring.release(i, b)
                def rest():
                    c = op("vector", lambda e: e.tensor_reduce(ss, v3(a2), AX, ALU.add), b, fre.get("ss"))
                    table(LOG)
                    c = op("scalar", lambda e: e.activation(ss, ss, ACT.Ln, bias=eps[:, 0:1], scale=1.0 / 64), c)
                    c = op("scalar", lambda e: e.activation(ss, ss, ACT.Exp, scale=-0.5), c)
                    c = op("vector", lambda e: e.tensor_tensor(v3(a1), v3(a1), ss[:, :, None].broadcast_to(b3),
                                                               ALU.mult), a, c)
                    fre["ss"] = [c]
                    gcol = gq[:, 64 * which:64 * which + 64][:, None, :].broadcast_to(b3)
                    c = op("vector", lambda e: e.tensor_tensor(v3(a1), v3(a1), gcol, ALU.mult), c, t_gq, t_gk)
                    src = a1
                    if roped:
                        tl0 = 4 * s
                        v4 = lambda t: t[:, 0:n].rearrange("p (t h c) -> p t h c", t=4, c=64)
                        tab = lambda j: rope[:, j, tl0:tl0 + 4, :][:, :, None, :].broadcast_to([P, 4, 4, 64])
                        d = op("vector", lambda e: e.tensor_tensor(v4(a2), v4(a1), tab(0), ALU.mult), c, t_rope)
                        for ax in range(2):
                            for hf in range(2):
                                o = slice(32 * ax + 16 * hf, 32 * ax + 16 * hf + 16)
                                w_ = slice(32 * ax + 16 - 16 * hf, 32 * ax + 32 - 16 * hf)
                                g = op("vector", lambda e, o=o, w_=w_: e.tensor_tensor(
                                    v4(a3_)[:, :, :, o], v4(a1)[:, :, :, w_], tab(1)[:, :, :, o], ALU.mult), c,
                                    t_rope, fre["a3"])
                        c = op("vector", lambda e: e.tensor_tensor(a2[:, 0:n], a2[:, 0:n], a3_[:, 0:n], ALU.add),
                               g, d)
                        fre[n1_] = [g, d]
                        fre["a3"] = [c]
                        src = a2
                    def later():
                        ps2, pw, i2 = ring.get()
                        for cb in range(2):
                            for t in range(nt):
                                l2 = op("tensor", lambda e, cb=cb, t=t: e.transpose(
                                    ps2[:, 128 * (cb * nt + t):128 * (cb * nt + t) + 128],
                                    src[:, 256 * t + 128 * cb:256 * t + 128 * cb + 128], ident[:]), pw, c,
                                    sig=(cb == 1 and t == nt - 1))
                        if roped:
                            fre[n2_] = [l2]
                        else:
                            fre[n1_] = [l2]
                            fre[n2_] = [c]
                        tc = slice(512 * s, 512 * s + 128 * nt)
                        p3 = ps2[:, 0:256 * nt].rearrange("p (cb t) -> p cb t", cb=2)
                        if which == 0:
                            td = [op("scalar", lambda e: e.activation(dst[0:64, 0:4:2, tc], p3[0:64], ACT.Copy), l2,
                                     dfree),
                                  op("vector", lambda e: e.tensor_copy(dst[64:128, 1:4:2, tc], p3[64:128]), l2,
                                     dfree)]
                        else:
                            td = [op("scalar", lambda e: e.activation(dst[:, tile0:tile0 + 2, tc], p3, ACT.Copy), l2,
                                     dfree)]
                        ring.release(i2, *td)
                        att.extend(td)
                    pending.append(later)
                if rests is None:
                    rest()
                else:
                    rests.append(rest)
            return post

        def ctx_v(j):
            def vpost(s, ps, last, ring, i):
                a = op("scalar", lambda e: e.activation(vcS[:, :, 256 * j:256 * j + 256],
                                                        ps[:, 0:512].rearrange("p (t c) -> p t c", t=2), ACT.Copy),
                       last, h_read)
                ring.release(i, a)
                att.append(a)
            drain(tm_pair(allps, 2, hch, hcl, tch, tcl, vpost))

        W.lo_engine = "gpsimd"
        ctx_v(0)
        rt = st.finish(allps, rs, done["relu"])
        ctx_v(1)
        rt2 = st.second(allps, rs, rt, rs2, done["relu"])
        tokh, tokl = [], []
        ctx_pe = []
        steps = norm_steps(tokh, tokl, lambda k: R1[:, k, :], tx, gA(0), rs2, rt2, HT, Hh, Hl, [h_read, t_A],
                           shift=mc(0), hw=lambda: [ctx_pe, ctx_read, t_gq, t_gk], on_vector=True)
        next(steps)
        t_vc = dma(vc_d, vcS[:], "vc", list(att))
        att, rests = [], []
        for j in range(2):
            drain(tm_pair(allps, 2, hch, hcl, tch, tcl, heads_post(2, 1, kcS, 2 * j, False, h_read,
                                                                   (("a1", "a2"), ("a4", "a5"))[j], rests),
                          flushes=False))
        ctx_pe.append(pe_now())
        drain(steps)
        for rest in rests:
            rest()
        for k in range(8):
            tx[k] = op("vector", lambda e, k=k: e.scalar_tensor_tensor(
                R1[:, k, :], R1[:, k, :], vec[:, V_FINAL + k:V_FINAL + k + 1], rs[:], ALU.mult, ALU.mult),
                rt, tx[k])
        t_sp = [dma(xs_d[k], R1[:, k, :], f"sp{k}", tx[k]) for k in range(8)]
        x_free = [tokh, tokl]
        ctx_st = []
        kc_att = att
        pending.append(lambda: ctx_st.append(dma(kc_d, kcS[:], "kc", list(kc_att))))
        ada_done = mod_t

        U = [[at(f"U{a}{b}", [P, 4, 512], R, R1A + 8192 * (2 * a + b)) for b in range(2)] for a in range(2)]
        Yh, Yl = at("Yh", [P, 4, T], R, SA), at("Yl", [P, 4, T], R, SA + 16384)
        Z = [[[sa(f"Z{z}{a}{b}", (8, 12)[z] + 2 * a + b, R) for b in range(2)] for a in range(2)]
             for z in range(2)]
        f1, f2, f3 = sa("f1", 12), sa("f2", 13), sa("f3", 14)
        CD = [[at(f"CD{a}{b}", [P, 128], R, spare + 512 * (2 * a + b))[:] for b in range(2)] for a in range(2)]
        cdr = at("cdr", [P, 2, 128], F, SA + 8 * 4096)
        n_done = [tokl, tokh, rt2, st.sqfree]
        d = dma(cdr[:], cd_d, "c3", n_done, ada_done)
        cdt = []
        for a in range(2):
            cdt += split(cdr[:, a, :], CD[a][0], CD[a][1], d, n_done)
        tU = []
        tUd = {}
        ufree = {"f1": n_done, "f2": n_done, "f3": n_done}
        sp_done = [t_sp, x_free]

        def u_post(c0):
            held = {}

            def post(s, ps, last, ring, i):
                if s == 0:
                    held[0] = (ps, last, ring, i)
                    return
                ps0, l0, _, i0 = held[0]
                a = op("scalar", lambda e: e.activation(f1[:], ps0[:], ACT.Copy), l0, ufree["f1"])
                ring.release(i0, a)
                b = op("vector", lambda e: e.tensor_tensor(f2[:], f1[:], ps[:], ALU.add), a, last, ufree["f2"])
                c = op("vector", lambda e: e.tensor_tensor(f3[:], f1[:], ps[:], ALU.subtract), a, last,
                       ufree["f3"])
                ring.release(i, c)
                ufree["f1"] = [c, b]
                for par, (f, t, nm) in enumerate(((f2, b, "f2"), (f3, c, "f3"))):
                    f4 = f[:].rearrange("p (t c) -> p t c", c=256)
                    th, tl = split(f4, U[par][0][:, :, c0:c0 + 256], U[par][1][:, :, c0:c0 + 256], t, sp_done)
                    ufree[nm] = [th, tl]
                    tUd[par, c0] = [th, tl]
                    tU.extend([th, tl])
            return post

        for c0 in (0, 256):
            drain(tm_pair(allps, 8, Hh, Hl, tokh, tokl, u_post(c0), flushes=c0 > 0))

        W.lo_engine = "vector"
        zs = Ring([0, 1])
        tY = []
        y_wait = [ada_done, cdt, t_vc, ctx_st, t_gq, t_gk, fre]
        zs.free[1] = [ufree]
        zs.free[0] = [n_done]

        def dft_step(par, j):
            tz = []
            zi, zw, _ = zs.get()
            wp = [(W.get(4), *allps.get()) for _ in range(2)]
            for g0 in (0, 2):
                for cs in range(2):
                    w, ps, psw, i = wp[cs]
                    for g in (g0, g0 + 1):
                        o = ps[:, 256 * g:256 * g + 256]
                        gs = slice(128 * g, 128 * g + 128)
                        for k in range(4):
                            mm(o, U[par][0][:, k, gs], w[0][:, k, :], psw, w[2], tUd[par, 128 * g0], start=(k == 0))
                            mm(o, U[par][0][:, k, gs], w[1][:, k, :], w[3])
                            last = mm(o, U[par][1][:, k, gs], w[0][:, k, :], stop=(k == 3),
                                      sig=(k == 3 and g == 3))
                    if g0 == 2:
                        W.release(w[4], last)
                        th, tl = split(ps[:], Z[zi][cs][0][:], Z[zi][cs][1][:], last, [zw, y_wait])
                        allps.release(i, th, tl)
                        tz.append((th, tl))
            return zi, tz

        def chan_step(par, j, ztz):
            zi, tz = ztz
            Zz = Z[zi]
            ps, psw, i = allps.get()
            for g in range(4):
                o = ps[:, 256 * g:256 * g + 256]
                gs = slice(256 * g, 256 * g + 256)
                for cs in range(2):
                    mm(o, CD[cs][0], Zz[cs][0][:, gs], psw, tz[cs][0], cdt, start=(cs == 0))
                    mm(o, CD[cs][1], Zz[cs][0][:, gs])
                    last = mm(o, CD[cs][0], Zz[cs][1][:, gs], tz[cs][1], stop=(cs == 1), sig=(cs == 1 and g == 3))
            zs.release(zi, last)
            v = lambda t: t[:].rearrange("p g (n two) -> p g n two", two=2)[:, :, 256 * j:256 * j + 256, par]
            th, tl = split(ps[:].rearrange("p (g n) -> p g n", g=4), v(Yh), v(Yl), last, [y_wait])
            allps.release(i, th, tl)
            tY.extend([th, tl])

        for par in range(2):
            for j in range(2):
                tz = dft_step(par, j)
                flush()
                pending.append(lambda par=par, j=j, tz=tz: chan_step(par, j, tz))
        flush()
        u_done = pe_now()

        mfr = Ring([sa("mf0", 12), sa("mf1", 13)])
        sgr = Ring([sa("sgr0", 14), sa("sgr1", 15)])
        for r in (mfr, sgr):
            r.free = [[u_done, tU, cdt] for _ in r.free]
        mf_st = {}

        def gate(sigs):
            def post(ps, last, ring, i):
                g, w, gi = sgr.get()
                table(SIG)
                a = op("scalar", lambda e: e.activation(g[:], ps[:], ACT.Sigmoid), last, w)
                ring.release(i, a)
                sigs.append((g, a, gi))
            return post

        for m in range(0, 8, 2):
            sigs = []
            for x in range(2):
                drain(fm_tile(allps, 8, Hh, Hl, tokh, tokl, gate(sigs)))
            w = W.get(4)
            for x in range(2):
                def post(ps, last, ring, i, x=x):
                    g, a, gi = sigs[x]
                    o, ow, oi = mfr.get()
                    b = op("vector", lambda e: e.tensor_tensor(o[:], g[:], ps[:], ALU.mult), a, last, ow)
                    ring.release(i, b)
                    sgr.release(gi, b)
                    mf_st[m + x] = dma(mf_d[m + x], o[:], f"mf{(m + x) % 2}", b)
                    mfr.release(oi, mf_st[m + x])
                drain(fm_tile(allps, 4, Yh, Yl, [tY] * 4, [tY] * 4, post, w=w, m0=128 * x, release=(x == 1)))
        y_read = pe_now()
        ctx_att = [dma(kcT[:], kc_d, "c5", u_done, ctx_st), dma(vc[:], vc_d, "c6", u_done, t_vc)]
        t_rope = dma(rope[:], rope_d.rearrange("p two t c -> p two t c"), "c7", y_read)
        fre = {n: [y_read] for n in ("a1", "a2", "a3")}
        mf_done = [mf_st[6], mf_st[7]]

        ya = at("ya", [P, 4, T], F, SA + 8 * 4096)
        aA = SA + 4 * 4096
        be = [at(f"be{i}", [P, 14, 64], F, aA + 3584 * i) for i in range(2)]
        bm = [at(f"bm{i}", [P, 9, 64], F, aA + 7168 + 2304 * i) for i in range(2)]
        pr = Ring([at("pr0", [P, 832], F, spare), at("pr1", [P, 832], F, aA + 11776),
                   at("pr2", [P, 832], F, SA + 3 * 4096)])
        ptr = Ring([at(f"pt{i}", [P, 896], F, SA + 14 * 4096 + 3584 * i) for i in range(2)])
        pr.free = [[u_done, y_read]] * 3
        ptr.free = [[u_done, y_read, mfr.free, sgr.free]] * 2
        t_qz = [op("gpsimd", lambda e: e.memset(qT[64:128, 0:4:2, :], 0.0), u_done),
                op("gpsimd", lambda e: e.memset(qT[0:64, 1:4:2, :], 0.0), u_done)]

        bias_free = [[y_read], [y_read]]
        bias_t = {}

        def load_bias(h):
            i = h % 2
            bias_t[h] = [dma(be[i][:], biasE[h], f"be{i}", bias_free[i]),
                         dma(bm[i][:], biasM[h], f"bm{i}", bias_free[i])]

        tya = []
        attf = {"qT": [t_gq, t_gk, u_done, y_read, mfr.free, sgr.free], "O": []}
        for half in range(2):
            att, att_v = [], []
            drain(tm_pair(allps, 8, Hh, Hl, tokh, tokl, heads_post(4, 0, qT, 0, True, attf["qT"])))
            drain(tm_pair(allps, 8, Hh, Hl, tokh, tokl, heads_post(4, 1, kT, 0, True, attf["qT"])))

            def vpost(s, ps, last, ring, i):
                a = op("scalar", lambda e: e.activation(Vx[:, 4 * s:4 * s + 4, :],
                                                        ps[:].rearrange("p (t c) -> p t c", c=256), ACT.Copy),
                       last, attf["qT"])
                ring.release(i, a)
                att_v.append(a)
            if half == 0:
                load_bias(0)
                load_bias(1)
            drain(tm_pair(allps, 8, Hh, Hl, tokh, tokl, vpost))
            flush()
            att_t = [list(att), ctx_att, t_qz]
            ptv = list(att_v)
            pr.free[2] = [pr.free[2], fre["a3"]]
            SR = Ring(psum[0:2])
            SR.free = [list(allps.free[0]), list(allps.free[1])]
            ptfree = list(allps.free[2])
            OR = Ring([psum[3][:, 0:512], psum[3][:, 512:1024]])
            OR.free = [list(allps.free[3]) for _ in range(2)]
            its = [(hh, j) for hh in range(4) for j in (0, 1, 6, 7, 2, 3, 4, 5)]
            state = {}

            def qk(n):
                hh, j = its[n]
                h = 4 * half + hh
                cb = hh // 2
                mid_ = 2 <= j <= 5
                rs_ = 2 * j - 4 if mid_ else (0 if j < 2 else 8)
                ps, psw, i = SR.get()
                pt, pw, pi = pr.get()
                z = 32 + 8 * (n % 4)
                L = 576 if mid_ else 512
                s = state[n] = dict(pt=pt, pi=pi, L=L, rs=rs_, z=z)

                def scores():
                    q = qT[:, hh, 128 * j:128 * j + 128]
                    k0, na = 64 * rs_, 320 if mid_ else 256
                    mm(ps[:, 512 - na:512], q, kT[:, cb, k0:k0 + na], psw, att_t, start=True, stop=True)
                    mm(ps[:, 512:768], q, kT[:, cb, k0 + na:k0 + na + 256], start=True, stop=True)
                    last = mm(ps[:, 768:1024], q, kcT[:, 2 * half + cb, :], start=True, stop=True, sig=True)
                    s["qk"] = last

                def softmax():
                    last = s["qk"]
                    b = h % 2
                    if mid_:
                        bias = bm[b][:].rearrange("p a b -> p (a b)")
                    else:
                        i0 = rs_ - 2 * j + 6
                        bias = be[b][:, i0:i0 + 8, :].rearrange("p a b -> p (a b)")
                    col_ = lambda c: small[:, z + c:z + c + 1]
                    o4 = state.get(("s", n - 4))
                    a = op("vector", lambda e: e.tensor_reduce(col_(0), ps[:, 768:1024], AX, ALU.max), last, o4)
                    a = op("vector", lambda e: e.tensor_tensor_reduce(pt[:, 0:L], ps[:, 768 - L:768], bias, 1.0, col_(0),
                                                                      ALU.add, ALU.max, col_(1)), a, pw, bias_t[h])
                    if j == 5:
                        bias_free[b] = [a]
                        if h + 2 < 8:
                            load_bias(h + 2)
                    a = op("vector", lambda e: e.tensor_scalar(col_(2), col_(1), -1.0, None, ALU.mult), a)
                    table(LOG)
                    x2 = op("scalar", lambda e: e.activation(pt[:, L:L + 256], ps[:, 768:1024], ACT.Exp, bias=col_(2),
                                                             accum_out=col_(4)), a, pw)
                    SR.release(i, x2)
                    x1 = op("scalar", lambda e: e.activation(pt[:, 0:L], pt[:, 0:L], ACT.Exp, bias=col_(2),
                                                             accum_out=col_(3)), a)
                    s["x"] = [x1, x2]

                return scores, softmax

            def fin(n):
                s = state[n]
                pt, L, z = s["pt"], s["L"], s["z"]
                col_ = lambda c: small[:, z + c:z + c + 1]
                a = op("vector", lambda e: e.tensor_tensor(col_(5), col_(3), col_(4), ALU.add), s["x"])
                a = op("vector", lambda e: e.reciprocal(col_(6), col_(5)), a)
                a = op("vector", lambda e: e.tensor_scalar(pt[:, 0:L + 256], pt[:, 0:L + 256], col_(6), None,
                                                           ALU.mult), a)
                state[("s", n)] = a
                s["a"] = a

            def tr(n):
                s = state[n]
                hh, j = its[n]
                ps = psum[2]
                col_ = lambda c: small[:, s["z"] + c:s["z"] + c + 1]
                pt, L = s["pt"], s["L"]
                half9 = L == 576
                a = s["a"]
                for b in range(4):
                    last = op("tensor", lambda e, b=b: e.transpose(ps[:, 128 * b:128 * b + 128],
                                                                   pt[:, 128 * b:128 * b + 128], ident[:]),
                              ptstate["free"], a, sig=(b == 3))
                first = last
                for b in range(2):
                    last = op("tensor", lambda e, b=b: e.transpose(ps[:, 512 + 128 * b:640 + 128 * b],
                                                                   pt[:, L + 128 * b:L + 128 * b + 128], ident[:]),
                              sig=(b == 1 and not half9))
                if half9:
                    last = op("tensor", lambda e: e.transpose(ps[0:64, 768:896], pt[:, 512:576], ident[:]))
                pr.release(s["pi"], last)
                s["tr"] = first, last

            def evac(n):
                s = state[n]
                ps = psum[2]
                half9 = s["L"] == 576
                first, last = s["tr"]
                o, ow, oi = ptr.get()
                c1 = op("vector", lambda e: e.tensor_copy(o[:, 0:512], ps[:, 0:512]), first, ow)
                c2 = op("scalar", lambda e: e.activation(o[:, 512:768], ps[:, 512:768], ACT.Copy), last, ow)
                if half9:
                    c2 = op("scalar", lambda e: e.activation(o[0:64, 768:896], ps[0:64, 768:896], ACT.Copy), last)
                ptstate["free"] = [c1, c2]
                s["o"], s["oi"], s["c"] = o, oi, [c1, c2]

            def pv(n):
                s = state.pop(n)
                hh, j = its[n]
                h = 4 * half + hh
                pb = 64 * (hh % 2)
                ob, ow, oi = OR.get()
                O = ob[pb:pb + 64, 0:128]
                t0 = s["rs"] // 2
                o = s["o"]
                half9 = s["L"] == 576
                for b in range(4):
                    mm(O, Vx[:, t0 + b, 64 * hh:64 * hh + 64], o[:, 128 * b:128 * b + 128], ow, s["c"],
                       ptv, start=(b == 0))
                for b in range(2):
                    last = mm(O, vc[:, b, 64 * h:64 * h + 64], o[:, 512 + 128 * b:640 + 128 * b],
                              stop=(b == 1 and not half9), sig=(b == 1 and not half9))
                if half9:
                    last = mm(O, Vx[0:64, t0 + 4, 64 * hh:64 * hh + 64], o[0:64, 768:896], stop=True, sig=True)
                ptr.release(s["oi"], last)
                dst = ya[pb:pb + 64, 2 * half + hh // 2, 128 * j:128 * j + 128]
                ty = op("scalar", lambda e: e.activation(dst, O, ACT.Copy), last)
                OR.release(oi, ty)
                tya.append(ty)

            ptstate = {"free": ptfree}
            N = len(its)
            for n in range(N + 3):
                if n < N:
                    scores, softmax = qk(n)
                    scores()
                if 0 <= n - 2 < N:
                    tr(n - 2)
                if n < N:
                    softmax()
                if 0 <= n - 1 < N:
                    fin(n - 1)
                if 0 <= n - 2 < N:
                    evac(n - 2)
                if n >= 3:
                    pv(n - 3)
            fre["a3"] = [fre["a3"], pe_now()]
            attf["qT"] = [pe_now()]
            allps.free = [SR.free[0], SR.free[1], ptstate["free"], [OR.free]]

        a_read = pe_now()
        t_mf = [dma(R1[:, m, :], mf_d[m], f"x{m}", a_read, mf_done, att_t) for m in range(8)]
        yah, yal = at("yah", [P, 4, T], R, SA), at("yal", [P, 4, T], R, SA + 16384)
        sgr2 = Ring([sa("sg20", 12), sa("sg21", 13)])
        mr2 = Ring([sa("mr20", 14), sa("mr21", 15)])
        for r in (sgr2, mr2):
            r.free = [[a_read, ptr.free]] * 2
        tyh, tyl = [], []
        for k in range(4):
            th, tl = split(ya[:, k, :], yah[:, k, :], yal[:, k, :], tya, [a_read, bias_free, fre["ss"], pr.free])
            tyh.append(th)
            tyl.append(tl)
        sgr = sgr2
        tm_ = [None] * 8
        for m in range(0, 8, 2):
            sigs = []
            for x in range(2):
                def gpost(ps, last, ring, i):
                    g, w, gi = sgr2.get()
                    table(SIG)
                    a = op("scalar", lambda e: e.activation(g[:], ps[:], ACT.Sigmoid), last, w)
                    ring.release(i, a)
                    sigs.append((g, a, gi))
                drain(fm_tile(allps, 8, Hh, Hl, tokh, tokl, gpost))
            w = W.get(4)
            for x in range(2):
                def post(ps, last, ring, i, mx=m + x, x=x):
                    g, a, gi = sigs[x]
                    o, ow, oi = mr2.get()
                    b = op("vector", lambda e: e.tensor_tensor(o[:], g[:], ps[:], ALU.mult), a, last, ow)
                    ring.release(i, b)
                    sgr2.release(gi, b)
                    b = op("vector", lambda e: e.tensor_tensor(R1[:, mx, :], R1[:, mx, :], o[:], ALU.add), b,
                           t_mf[mx])
                    mr2.release(oi, b)
                    tm_[mx] = b
                drain(fm_tile(allps, 4, yah, yal, tyh, tyl, post, w=w, m0=128 * x, release=(x == 1)))
        h_read = pe_now()
        tokh, tokl = [], []
        for k in range(8):
            th, tl = split(R1[:, k, :], Hh[:, k, :], Hl[:, k, :], tm_[k], [h_read],
                           "gpsimd" if k % 2 else "vector")
            tokh.append(th)
            tokl.append(tl)
        tx = [dma(R1[:, k, :], xs_d[k], f"x{k}", tokh[k], tokl[k], t_sp[k]) for k in range(8)]
        b1, b2, b3_, b4 = sa("b1", 12), sa("b2", 13), sa("b3", 14), sa("b4", 15)
        bw = [sgr2.free, mr2.free]
        table(LOG)
        st = Stats(b1, [b2, b3_], bw)
        for m in range(8):
            drain(fm_tile(allps, 8, Hh, Hl, tokh, tokl, add_tile(m, st, mc(16), tok=tx), halves=m == 7))
        h_read = pe_now()
        rt = st.finish(allps, b4, bw)
        tokh, tokl = apply_norm(lambda k: R1[:, k, :], tx, gA(2), b4, rt, HT, Hh, Hl, [h_read, t_A],
                                shift=mc(24))
        tn = [tokl, tokh, rt, st.tok, st.sqfree, h_read, st.last_tokens()]
        done = {"post": lambda m: outs.append(dma(out[m], R1[:, m, :], f"x{m}", tx[m]))}
        outs = []
        mlp(tx, tokh, tokl, tn, lambda: None, scale=mc(40), done=done)
        fin = [(f"x{k}", Q.n[f"x{k}"]) for k in range(8)]
        Q.q["sync"].append((lambda e: None, (fin,), None, 0))

        block = ctx.enter_context(nc.Block())
        for name in ENGINES:
            on = {"tensor": block.tensor, "vector": block.vector, "scalar": block.scalar, "gpsimd": block.gpsimd,
                  "sync": block.sync}[name]
            on(lambda e, name=name: Q.emit(name, e))


def layout(inputs):
    c = np.ascontiguousarray
    f = np.float32
    i = inputs

    def fm(a):
        return c(np.asarray(a).T.reshape(8, 128, -1))

    def pk(a):
        return np.asarray(a).reshape(-1, 128).T

    vecs = c(np.concatenate([pk(i[n]) for n in (
        "norm_mix", "norm_mlp", "norm_final", "hgrn_lower_bound", "hgrn_out_norm", "norm1_g_2", "norm2_g_2",
        "b_ada_2")], axis=1))
    gains = c(np.broadcast_to(np.concatenate([i["q_norm_g_2"][0], i["k_norm_g_2"][0]]), (128, 128)))

    rpb = np.asarray(i["rpb_2"])[0]
    cq, ck = np.arange(64)[:, None], np.arange(64)[None, :]
    start = np.clip(cq - 8, 0, 48)
    inside = (ck >= start) & (ck < start + 16)
    idx = np.clip(ck - cq + 15, 0, 30)
    toe = np.where(inside[None, None], rpb[:, :, idx], f(NEG)).transpose(0, 2, 1, 3)
    edge = np.full((8, 128, 14, 64), NEG, f)
    edge[:, :64] = toe[:, :, 1:15]
    edge[:, 64:] = toe[:, :, 0:14]
    mid = np.full((8, 128, 9, 64), NEG, f)
    mid[:, :64, 0:8] = toe[:, :, 3:11]
    mid[:, 64:, 1:9] = toe[:, :, 3:11]

    s, t = np.arange(128)[:, None], np.arange(128)[None, :]
    masks = [s == t]
    for lev in range(7):
        m = 1 << lev
        masks.append((s // (2 * m) == t // (2 * m)) & (s // m % 2 == 0) & (t // m % 2 == 1))
    masks = c(np.stack(masks, 1).astype(f))

    tok = np.arange(1024)
    inv = f(10000.0) ** (-np.arange(0, 32, 2, dtype=f) / f(32))
    ang = np.stack([(tok // 64).astype(f)[:, None] * inv, (tok % 64).astype(f)[:, None] * inv], 1)
    cos, sin = np.cos(ang).astype(f), np.sin(ang).astype(f)
    rope = np.stack([np.stack([cos, cos], 2), np.stack([-sin, sin], 2)], 0)
    rope = c(rope.reshape(2, 8, 128, 64).transpose(2, 0, 1, 3))

    n = np.arange(512)
    dft = np.empty((2, 2, 512, 512))
    for par in range(2):
        a = 2 * np.pi * (n[:, None] * (2 * n[None, :] + par) % 1024) / 1024
        dft[par] = np.cos(a), np.sin(a)
    d = np.arange(128)
    a = 2 * np.pi * (d[:, None] * d[None, :] % 128) / 128
    g = 1.0 / np.sqrt(1024 * 128)
    cd = np.stack([np.cos(a) * g, -np.sin(a) * g], 1)

    return {
        "xT": fm(i["x"][0]), "vecs": vecs, "w_in": c(i["hgrn_w_in"][0]), "w_out": c(i["hgrn_w_out"][0]),
        "m_w1": c(i["mlp_w1"][0]), "m_w2": c(i["mlp_w2"][0]), "ctxT": fm(i["ctx_2"][0]), 
        "c_d": c(np.broadcast_to(np.stack([i["c_2"].reshape(1, 1024), i["c_ctx_2"].reshape(1, 1024)]), (2, 128, 1024))),
        "w_ada": c(np.asarray(i["w_ada_2"][0]).T.reshape(48, 128, 1024)),
        "w_in2": c(i["w_in_2"][0]), "gains": gains, "biasE": c(edge), "biasM": c(mid),
        "w_gate": c(i["w_branch_gate_2"][0]), "w_fo": c(i["w_fourier_out_2"][0]), "w_ao": c(i["w_attn_out_2"][0]),
        "w_o2": c(i["w_out_2"][0]), "m2_w1": c(i["w_mlp1_2"][0]), "m2_w2": c(i["w_mlp2_2"][0]),
        "ident_d": np.eye(128, dtype=f), "masks_d": masks, "rope_d": rope, "dft_d": dft.astype(f),
        "cd_d": c(cd.astype(f)),
    }


def kernel(**inputs):
    from concourse import bacc
    from concourse.bass_utils import run_bass_kernel_spmd

    arrays = layout({k: np.asarray(v) for k, v in inputs.items()})
    nc = bacc.Bacc("TRN2", target_bir_lowering=False, num_devices=1)
    args = [nc.dram_tensor("in_" + n, a.shape, mybir.dt.from_np(a.dtype), kind="ExternalInput").ap()
            for n, a in arrays.items()]
    args.append(nc.dram_tensor("out_0", (8, 128, 1024), F, kind="ExternalOutput").ap())
    build(nc, *args)
    r = run_bass_kernel_spmd(nc, [{"in_" + n: a for n, a in arrays.items()}], core_ids=[0])
    got = np.asarray(r.results[0]["out_0"])
    return np.ascontiguousarray(got.reshape(1024, 1024).T).reshape(1, 1024, 1024)
```
